# Optimizing a Trainium2 kernel written in Bass

```python
import jax, jax.numpy as jnp
from jax import lax
import numpy as np

D_MODEL = 1024
BATCH = 1
SEQ = 512
DEPTH = 1
DEC_BATCH = 8
DEC_SEQ = 4
PAST_LEN = 4096
PAGE_SIZE = 128

D_RNN = D_MODEL
N_LRU_BLOCKS = 16
LRU_BLOCK = D_RNN // N_LRU_BLOCKS
LRU_CONV_W = 4
LRU_C = 8.0
D_CONV = D_MODEL
CONF_CONV_W = 31
N_EXPERTS = 16
N_GROUPS = 4
EXPERTS_PER_GROUP = N_EXPERTS // N_GROUPS
TOP_K = 2
D_EXPERT = D_MODEL // 2
N_IN = 2 * D_RNN + 2 * D_CONV + 2 * D_MODEL
SPLITS = [D_RNN, 2 * D_RNN, 2 * D_RNN + D_CONV, 2 * D_RNN + 2 * D_CONV, 2 * D_RNN + 2 * D_CONV + D_MODEL]
RMS_EPS = 1e-6
LN_EPS = 1e-5

kernel_name = 'hawk_conformer_moe_adaln_step'

def rmsnorm(x, g):
    xf = x.astype(jnp.float32)
    y = xf * lax.rsqrt(jnp.mean(xf * xf, axis=-1, keepdims=True) + RMS_EPS)
    return (y * g.astype(jnp.float32)).astype(x.dtype)

def layernorm(x, g, b):
    xf = x.astype(jnp.float32)
    mu = jnp.mean(xf, axis=-1, keepdims=True)
    xc = xf - mu
    var = jnp.mean(xc * xc, axis=-1, keepdims=True)
    y = xc * lax.rsqrt(var + LN_EPS) * g.astype(jnp.float32) + b.astype(jnp.float32)
    return y.astype(x.dtype)

def causal_dwconv(u, buf, w, b):
    width = w.shape[0]
    full = jnp.concatenate([buf.astype(u.dtype), u], axis=1)
    y = lax.conv_general_dilated(full, w[:, None, :].astype(u.dtype), window_strides=(1,),
                                 padding='VALID', dimension_numbers=('NWC', 'WIO', 'NWC'),
                                 feature_group_count=u.shape[-1])
    return y + b.astype(u.dtype), full[:, -(width - 1):]

def rg_lru(x, h0, start, wa, ba, wx, bx, lam):
    bsz, t_len, ch = x.shape
    f32 = jnp.float32
    xf = x.astype(f32)
    xb = xf.reshape(bsz, t_len, N_LRU_BLOCKS, LRU_BLOCK)
    r = jax.nn.sigmoid(jnp.einsum('bthi,hij->bthj', xb, wa.astype(f32)).reshape(bsz, t_len, ch) + ba.astype(f32))
    i = jax.nn.sigmoid(jnp.einsum('bthi,hij->bthj', xb, wx.astype(f32)).reshape(bsz, t_len, ch) + bx.astype(f32))
    log_a = -LRU_C * r * jax.nn.softplus(-lam.astype(f32))
    a = jnp.exp(log_a)
    mult = jnp.sqrt(-jnp.expm1(2.0 * log_a))
    reset = ((start + jnp.arange(t_len)) == 0)[None, :, None]
    a = jnp.where(reset, 0.0, a)
    mult = jnp.where(reset, 1.0, mult)
    bterm = mult * i * xf
    bterm = bterm.at[:, 0].add(a[:, 0] * h0.astype(f32))

    def comb(left, right):
        a1, b1 = left
        a2, b2 = right
        return a1 * a2, a2 * b1 + b2

    _, h = lax.associative_scan(comb, (a, bterm), axis=1)
    return h.astype(x.dtype), h[:, -1]

def moe(h, w_router, b_router, w_gate, w_up, w_down):
    bsz, t_len, d = h.shape
    hf = h.reshape(bsz * t_len, d)
    logits = hf.astype(jnp.float32) @ w_router.astype(jnp.float32) + b_router.astype(jnp.float32)
    probs = jax.nn.softmax(logits, axis=-1)
    grp_top, _ = lax.top_k(probs.reshape(-1, N_GROUPS, EXPERTS_PER_GROUP), TOP_K)
    grp = jnp.argmax(grp_top.sum(-1), axis=-1)
    in_grp = (jnp.arange(N_EXPERTS) // EXPERTS_PER_GROUP)[None, :] == grp[:, None]
    vals, idx = lax.top_k(jnp.where(in_grp, probs, -1.0), TOP_K)
    wts = vals / jnp.sum(vals, axis=-1, keepdims=True)
    combine = jnp.sum(jax.nn.one_hot(idx, N_EXPERTS, dtype=jnp.float32) * wts[..., None], axis=1)
    out = jnp.zeros(hf.shape, jnp.float32)
    for e in range(N_EXPERTS):
        ye = (jax.nn.silu(hf @ w_gate[e]) * (hf @ w_up[e])) @ w_down[e]
        out = out + combine[:, e:e + 1] * ye.astype(jnp.float32)
    return out.astype(h.dtype).reshape(bsz, t_len, d)

def layer(x, c, start, h0, lru_buf, conf_buf, w_ada, b_ada, g_mix, g_ffn, w_in, b_in,
          lru_conv_w, lru_conv_b, lru_wa, lru_ba, lru_wx, lru_bx, lru_lambda, w_lru_o,
          conf_conv_w, conf_conv_b, conf_ln_g, conf_ln_b, w_conf_o, w_out,
          w_router, b_router, w_gate, w_up, w_down):
    mod = jax.nn.silu(c) @ w_ada + b_ada
    sh1, sc1, gt1, sh2, sc2, gt2 = jnp.split(mod[:, None, :], 6, axis=-1)
    hm = rmsnorm(x, g_mix) * (1.0 + sc1) + sh1
    proj = hm @ w_in + b_in
    u_lru, gate_lru, conf_a, conf_b, bg_lru, bg_conf = jnp.split(proj, SPLITS, axis=-1)
    xc, new_lru_buf = causal_dwconv(u_lru, lru_buf, lru_conv_w, lru_conv_b)
    hseq, h_last = rg_lru(xc, h0, start, lru_wa, lru_ba, lru_wx, lru_bx, lru_lambda)
    out_a = (hseq * jax.nn.gelu(gate_lru)) @ w_lru_o
    glu = conf_a * jax.nn.sigmoid(conf_b)
    dc, new_conf_buf = causal_dwconv(glu, conf_buf, conf_conv_w, conf_conv_b)
    out_b = jax.nn.silu(layernorm(dc, conf_ln_g, conf_ln_b)) @ w_conf_o
    merged = jax.nn.sigmoid(bg_lru) * out_a + jax.nn.sigmoid(bg_conf) * out_b
    x = x + gt1 * (merged @ w_out)
    hf = rmsnorm(x, g_ffn) * (1.0 + sc2) + sh2
    x = x + gt2 * moe(hf, w_router, b_router, w_gate, w_up, w_down)
    return x, h_last, new_lru_buf, new_conf_buf

def setup_inputs(seed: int = 0) -> dict:
    key = jax.random.key(seed)
    ks = jax.random.split(key, 40)
    f32 = jnp.float32
    nrm = lambda k, s, sc: jax.random.normal(k, s, f32) * sc
    a0 = jax.random.uniform(ks[20], (DEPTH, D_RNN), f32, 0.9, 0.999)
    s = a0 ** (1.0 / LRU_C)
    lam = jnp.log(s) - jnp.log1p(-s)
    return {
        'x_prompt': nrm(ks[0], (BATCH, SEQ, D_MODEL), 1.0),
        'x_sample': nrm(ks[1], (DEC_BATCH, DEC_SEQ, D_MODEL), 1.0),
        'state_lru_h': nrm(ks[2], (DEPTH, DEC_BATCH, D_RNN), 0.5),
        'state_lru_conv': nrm(ks[3], (DEPTH, DEC_BATCH, LRU_CONV_W - 1, D_RNN), 1.0),
        'state_conf_conv': nrm(ks[4], (DEPTH, DEC_BATCH, CONF_CONV_W - 1, D_CONV), 1.0),
        'c_prompt': nrm(ks[5], (BATCH, D_MODEL), 1.0),
        'c_sample': nrm(ks[6], (DEC_BATCH, D_MODEL), 1.0),
        'w_ada': nrm(ks[7], (DEPTH, D_MODEL, 6 * D_MODEL), 0.5 * D_MODEL ** -0.5),
        'b_ada': nrm(ks[8], (DEPTH, 6 * D_MODEL), 0.02),
        'g_mix': 1.0 + nrm(ks[9], (DEPTH, D_MODEL), 0.05),
        'g_ffn': 1.0 + nrm(ks[10], (DEPTH, D_MODEL), 0.05),
        'w_in': nrm(ks[11], (DEPTH, D_MODEL, N_IN), D_MODEL ** -0.5),
        'b_in': nrm(ks[12], (DEPTH, N_IN), 0.02),
        'lru_conv_w': nrm(ks[13], (DEPTH, LRU_CONV_W, D_RNN), LRU_CONV_W ** -0.5),
        'lru_conv_b': nrm(ks[14], (DEPTH, D_RNN), 0.02),
        'lru_wa': nrm(ks[15], (DEPTH, N_LRU_BLOCKS, LRU_BLOCK, LRU_BLOCK), LRU_BLOCK ** -0.5),
        'lru_ba': nrm(ks[16], (DEPTH, D_RNN), 0.02),
        'lru_wx': nrm(ks[17], (DEPTH, N_LRU_BLOCKS, LRU_BLOCK, LRU_BLOCK), LRU_BLOCK ** -0.5),
        'lru_bx': nrm(ks[18], (DEPTH, D_RNN), 0.02),
        'lru_lambda': lam,
        'w_lru_o': nrm(ks[19], (DEPTH, D_RNN, D_MODEL), D_RNN ** -0.5),
        'conf_conv_w': nrm(ks[21], (DEPTH, CONF_CONV_W, D_CONV), CONF_CONV_W ** -0.5),
        'conf_conv_b': nrm(ks[22], (DEPTH, D_CONV), 0.02),
        'conf_ln_g': 1.0 + nrm(ks[23], (DEPTH, D_CONV), 0.05),
        'conf_ln_b': nrm(ks[24], (DEPTH, D_CONV), 0.02),
        'w_conf_o': nrm(ks[25], (DEPTH, D_CONV, D_MODEL), D_CONV ** -0.5),
        'w_out': nrm(ks[26], (DEPTH, D_MODEL, D_MODEL), D_MODEL ** -0.5),
        'w_router': nrm(ks[27], (D_MODEL, N_EXPERTS), D_MODEL ** -0.5),
        'b_router': nrm(ks[28], (N_EXPERTS,), 0.01),
        'w_gate': nrm(ks[29], (DEPTH, N_EXPERTS, D_MODEL, D_EXPERT), D_MODEL ** -0.5),
        'w_up': nrm(ks[30], (DEPTH, N_EXPERTS, D_MODEL, D_EXPERT), D_MODEL ** -0.5),
        'w_down': nrm(ks[31], (DEPTH, N_EXPERTS, D_EXPERT, D_MODEL), D_EXPERT ** -0.5),
        'g_final': 1.0 + nrm(ks[32], (D_MODEL,), 0.05),
    }

def reference(x_prompt, x_sample, state_lru_h, state_lru_conv, state_conf_conv, c_prompt, c_sample,
              w_ada, b_ada, g_mix, g_ffn, w_in, b_in, lru_conv_w, lru_conv_b, lru_wa, lru_ba,
              lru_wx, lru_bx, lru_lambda, w_lru_o, conf_conv_w, conf_conv_b, conf_ln_g, conf_ln_b,
              w_conf_o, w_out, w_router, b_router, w_gate, w_up, w_down, g_final):
    xp, xs = x_prompt, x_sample
    hp_list, lcp_list, ccp_list = [], [], []
    hs_list, lcs_list, ccs_list = [], [], []
    for l in range(DEPTH):
        lw = (w_ada[l], b_ada[l], g_mix[l], g_ffn[l], w_in[l], b_in[l], lru_conv_w[l], lru_conv_b[l],
              lru_wa[l], lru_ba[l], lru_wx[l], lru_bx[l], lru_lambda[l], w_lru_o[l],
              conf_conv_w[l], conf_conv_b[l], conf_ln_g[l], conf_ln_b[l], w_conf_o[l], w_out[l],
              w_router, b_router, w_gate[l], w_up[l], w_down[l])
        h0p = jnp.zeros((BATCH, D_RNN), jnp.float32)
        lbp = jnp.zeros((BATCH, LRU_CONV_W - 1, D_RNN), xp.dtype)
        cbp = jnp.zeros((BATCH, CONF_CONV_W - 1, D_CONV), xp.dtype)
        xp, hp, lcp, ccp = layer(xp, c_prompt, 0, h0p, lbp, cbp, *lw)
        xs, hs, lcs, ccs = layer(xs, c_sample, PAST_LEN, state_lru_h[l], state_lru_conv[l],
                                 state_conf_conv[l], *lw)
        hp_list.append(hp); lcp_list.append(lcp); ccp_list.append(ccp)
        hs_list.append(hs); lcs_list.append(lcs); ccs_list.append(ccs)
    y_prompt = rmsnorm(xp, g_final)
    y_sample = rmsnorm(xs, g_final)
    return (y_prompt, y_sample,
            jnp.stack(hp_list), jnp.stack(lcp_list), jnp.stack(ccp_list),
            jnp.stack(hs_list), jnp.stack(lcs_list), jnp.stack(ccs_list))


_drawn_inputs = setup_inputs


def setup_inputs(seed=0):
    import zlib

    import numpy as np

    out = dict(_drawn_inputs(seed))
    spreads = {}
    factors = {'lru_ba': 8.0, 'lru_bx': 6.71, 'conf_conv_b': 6.421, 'conf_ln_b': 8.0}
    for name, (base, spread) in spreads.items():
        noise = np.random.default_rng([zlib.crc32(name.encode()), seed]).standard_normal(out[name].shape)
        drawn = base * np.exp(spread * noise) if base else spread * noise
        out[name] = __import__('jax').numpy.asarray(drawn.astype(out[name].dtype))
    for name, factor in factors.items():
        out[name] = (out[name] * factor).astype(out[name].dtype)
    return out
```

```python
from contextlib import ExitStack

import concourse.bass as bass
from concourse import mybir

F32 = mybir.dt.float32
BF16 = mybir.dt.bfloat16
I32 = mybir.dt.int32
ALU = mybir.AluOpType
ACT = mybir.ActivationFunctionType
AX = mybir.AxisListType.X

P = 128
D = 1024
KC = D // P
TP = 512
NS, TS = 8, 4
TSAMP = NS * TS
T = TP + TSAMP
HALF = T // 2
NSEQ = 1 + NS
TILES = [P, P, P, P, TSAMP]
NT = len(TILES)
GC = 4
GW = GC * P
CT = 32
W3, W30 = 3, 30
NE, NG, EG = 16, 4, 4
DE = D // 2
CAP = P
MORE = (T - 1) // P
AHEAD = 3
MAX_OVER = 2 * T * 4 // (4 * P + 1)
RMS_EPS, LN_EPS = 1e-6, 1e-5
assert MORE == 4

R_LCONV, R_H0, R_CW, R_LW = 0, 24, 32, 63
R_CB, R_LNG, R_LNB, R_BA, R_BX, R_LAM, R_GMIX, R_LB, R_BIN = 67, 68, 69, 70, 71, 72, 73, 74, 75
NVEC = 81
G_U, G_GATE, G_CA, G_CB, G_BL, G_BC = 0, 2, 4, 6, 8, 10


def weight_stream():
    s = [("ada", g) for g in range(4)]
    s += [("in", G_CA), ("ada", 4), ("in", G_CB), ("ada", 5), ("in", G_CA + 1), ("ada", 6), ("ada", 7)]
    s += [("in", G_CB + 1), ("ada", 8), ("ada", 9), ("in", G_U), ("ada", 10), ("in", G_U + 1), ("ada", 11)]
    s += [("in", G_GATE), ("in", G_GATE + 1)]
    s += [("in", G_BC), ("co", 0), ("in", G_BC + 1), ("co", 1)]
    s += [("in", G_BL), ("lo", 0), ("in", G_BL + 1), ("lo", 1)]
    s += [("wo", 0), ("wo", 1)]
    return s


def build(nc, a):
    stream = weight_stream()
    NSTREAM = len(stream)
    RING = 3
    assert NSTREAM % RING == 0
    with ExitStack() as ctx:
        def sb(name, shape, dt=F32):
            return ctx.enter_context(nc.sbuf_tensor(name, shape, dt))

        def sem(name):
            return ctx.enter_context(nc.semaphore(name))

        ring_a = sb("ring_a", [P, RING * KC * GW])
        region_c = sb("region_c", [P, 13080])
        region_b = sb("region_b", [P, 12288])
        region_d = sb("region_d", [P, 8704])
        region_e = sb("region_e", [P, 2176])

        def carve(region, at, dims):
            n = 1
            for d in dims:
                n *= d
            v = region[:, at:at + n]
            if len(dims) == 2:
                return v.rearrange("p (a b) -> p a b", a=dims[0])
            if len(dims) == 3:
                return v.rearrange("p (a b c) -> p a b c", a=dims[0], b=dims[1])
            return v

        wslot = [carve(ring_a, s * KC * GW, (KC, GW)) for s in range(RING)]
        xt = carve(region_c, 0, (NT, D))
        mod1 = carve(region_c, 5120, (4 * GW,))
        mod2 = carve(region_c, KC * T, (8 * GW,))
        dc = carve(region_c, 0, (KC, T))
        z = carve(region_c, KC * T, (KC, T))
        u = carve(region_c, 2 * KC * T, (KC, W3 + T))
        merged = carve(region_c, 2 * KC * T, (KC, T))
        hm = carve(region_b, 0, (KC, T))
        glu = carve(region_b, 4352, (KC, W30 + T))
        glu_s = region_b[:, 8944:8944 + KC * NS * (W30 + TS)].rearrange(
            "p (k s t) -> p k s t", k=KC, s=NS)
        sg = carve(region_b, 11120, (2, T))
        ln_mean = carve(region_b, 4352, (T,))
        ln_rstd = carve(region_b, 4352 + T, (T,))
        ln_sq = carve(region_b, 4352 + 2 * T, (2, T))
        x1 = carve(region_b, 4352, (NT, D))
        gt1_bc = carve(region_b, 0, (2, D))
        g2_bc = carve(region_b, 2 * D, (2, D))
        sh2_bc = carve(region_b, 9472, (2, D))
        last_glu = carve(region_b, 9472, (D,))
        last_u = carve(region_b, 9472 + D, (D,))
        vec = carve(region_d, 0, (D,))
        sconf = carve(region_d, D, (2, D))
        crow = carve(region_d, 3 * D, (D,))
        xc = carve(region_d, 0, (GC, T))
        tt = carve(region_d, GC * T, (GC, T))
        ii = carve(region_d, 2 * GC * T, (GC, T))
        rec = carve(region_d, 3 * GC * T, (GC, T))
        hf = carve(region_d, 0, (2, D))
        hft = carve(region_d, 2 * D, (2, KC, P))
        xg = carve(region_d, 0, (2, D))
        xgt = carve(region_d, 2 * D, (KC, P))
        act_g = carve(region_d, 3 * D, (DE,))
        act_t = carve(region_d, 3 * D + DE, (DE // P, P))
        yb = carve(region_d, 4 * D, (2, D))
        gt2_bc = carve(region_d, 6 * D, (2, D))
        last_h = carve(region_d, 0, (D,))
        prod = carve(region_e, 0, (TS, NS, 31))
        odd = region_e[:, 1024:1024 + TP]
        bg = carve(region_e, 0, (GC, T))
        u_s = region_e[:, 1728:2176].rearrange("p (k s t) -> p k s t", k=KC, s=NS)
        gffn_bc = carve(region_e, 0, (D,))
        gfin_bc = carve(region_e, D, (D,))
        ya = carve(ring_a, 0, (2, D))
        yc = carve(ring_a, 2 * D, (2, D))
        yo = carve(ring_a, 4 * D, (2, D))
        junk = carve(ring_a, 6 * D, (D,))
        regs = (ring_a, region_c)
        wg = [carve(r, 0, (KC, DE)) for r in regs]
        wu = [carve(r, 4096, (KC, DE)) for r in regs]
        wd = [carve(r, 8192, (DE // P, D)) for r in regs]

        ident = sb("ident", [P, P])
        ones = sb("ones", [P, P])
        tri = sb("tri", [P, P])
        rt = sb("rt", [P, KC, NVEC])
        sct = sb("sct", [P, KC, CT])
        sel = sb("sel", [P, CT])
        ada_tmp = region_d[:, 5 * D:6 * D].rearrange("p (s n) -> p s n", s=2)
        gate_w = [sb("wa_bd", [P, KC, P]), sb("wx_bd", [P, KC, P])]
        hlast = sb("hlast", [P, KC, 1 + TSAMP])
        modt = sb("modt", [P, 2 * KC, NSEQ])
        amod = sb("amod", [P, KC, NSEQ])
        sp4 = sb("sp4", [P, KC])
        spt = sb("spt", [P, 4, KC])
        ssq = sb("ssq", [P, NT])
        rstd = sb("rstd", [P, NT])
        nt1 = sb("nt1", [P, NT])
        eps_ln = sb("eps_ln", [P, 1])
        hst = sb("hst", [P, 2, GC * NS])
        iota_e = sb("iota_e", [P, NE])
        grp_e = sb("grp_e", [P, NE])
        iota_g = sb("iota_g", [P, NG])
        base_e = sb("base_e", [P, NE])
        slot_row = sb("slot_row", [P, P], BF16)
        tokid = sb("tokid", [P, NT, 2], BF16)
        valid = sb("valid", [P, NT])
        wr = sb("wr", [P, KC, NE])
        br = sb("br", [P, NE])
        zero_row = region_e[:, 0:D]
        iota_tmp = region_d[:, 8192:8192 + P].bitcast(I32)

        ps = ctx.enter_context(nc.psum_tensor("ps", [P, 8, 512], F32))

        mod_scr = nc.dram_tensor("mod_scr", (NSEQ, 6 * D), F32, kind="Internal").ap()
        hf_scr = nc.dram_tensor("hf_scr", (T, D), F32, kind="Internal").ap()
        y_scr = nc.dram_tensor("y_scr", ((NE + MAX_OVER) * CAP, D), F32, kind="Internal").ap()
        rb = region_b[:, 2 * D:2 * D + 8 * NT * NE].rearrange("p (j t e) -> p j t e", j=8, t=NT)
        lg, pr, m16, oh1, oh2, key, r6, r7 = (rb[:, j] for j in range(8))
        rank = lg
        rs = sb("rs", [P, 12, NT])
        gsb = region_b[:, 2 * D + 640:2 * D + 740].rearrange("p (j t g) -> p j t g", j=5, t=NT)
        selb = region_b[:, 2 * D + 740:2 * D + 820].rearrange("p (t e) -> p t e", t=NT)
        w12 = sb("w12", [P, 2, NT])
        slot_i = sb("slot_i", [P, 2, NT], I32)
        mb = region_b[:, 0:NT * P].bitcast(BF16).rearrange("p (s t r) -> p s t r", s=2, t=NT)
        idx_f = sb("idx_f", [P, 2, 2])
        idx_i = sb("idx_i", [P, NE], I32)
        idx_vf = sb("idx_vf", [P, 1])
        idx_vg = sb("idx_vg", [P, 1])
        idx_ov = sb("idx_ov", [P, 1], I32)
        cnt = sb("cnt", [P, NE])
        ovf = region_b[:, 3 * D:3 * D + NE * MORE].rearrange("p (e j) -> p e j", j=MORE)
        ovr = region_b[:, 3 * D + 64:3 * D + 64 + 3 * NE * MORE].rearrange("p (a c) -> p a c", a=3)
        ovi = sb("ovi", [P, NE * MORE])
        ovm = region_e[:, 0:2 * MAX_OVER * NE * MORE].rearrange("p (j k c) -> p j k c", j=2, k=MAX_OVER)
        ovk = sb("ovk", [P, MAX_OVER])
        ovt_f = sb("ovt_f", [P, 3, MAX_OVER])
        ovt = sb("ovt", [P, 1 + MAX_OVER], I32)
        ov4 = sb("ov4", [P, NE])
        ovkey = sb("ovkey", [P, NT])

        w_full = [sem(f"w_full{s}") for s in range(RING)]
        ada_ps = sem("ada_ps")
        ada_cp = sem("ada_cp")
        ada_sum = sem("ada_sum")
        sct_zero = sem("sct_zero")
        sel_mat = sem("sel_mat")
        crow_in = sem("crow_in")
        vec_in = sem("vec_in")
        sconf_in = sem("sconf_in")
        bd_in = sem("bd_in")
        bd_zero = sem("bd_zero")
        x_in = sem("x_in")
        bias_in = sem("bias_in")
        bias2_in = sem("bias2_in")
        ada_act = sem("ada_act")
        ssq_clear = sem("ssq_clear")
        x1_half = sem("x1_half")
        idx_cp = sem("idx_cp")
        ov_key = sem("ov_key")
        slot_ok = sem("slot_ok")
        y_clear = sem("y_clear")
        zero_ok = sem("zero_ok")
        consts = sem("consts")
        pool_step = sem("pool_step")
        dve_step = sem("dve_step")
        act_step = sem("act_step")
        csilu = sem("csilu")
        c_tr = sem("c_tr")
        sct_ok = sem("sct_ok")
        vec_tr = sem("vec_tr")
        rt_ok = sem("rt_ok")
        sconf_tr = sem("sconf_tr")
        sconf_ok = sem("sconf_ok")
        ada_ok = sem("ada_ok")
        modt_tr = sem("modt_tr")
        modt_ok = sem("modt_ok")
        xn_ok = sem("xn_ok")
        ssq_ok = sem("ssq_ok")
        rms_ask = sem("rms_ask")
        rms_sqrt = sem("rms_sqrt")
        rstd_ok = sem("rstd_ok")
        x_tr = sem("x_tr")
        hm_dve = sem("hm_dve")
        hm_act = sem("hm_act")
        pairs = sem("pairs")
        pair_act = sem("pair_act")
        pair_dve = sem("pair_dve")
        conv_new = sem("conv_new")
        prod_ok = sem("prod_ok")
        prod_used = sem("prod_used")
        conv_ok = sem("conv_ok")
        dc_ok = sem("dc_ok")
        us_ok = sem("us_ok")
        xc_ok = sem("xc_ok")
        sp_exp = sem("sp_exp")
        sp_ask = sem("sp_ask")
        sp_ok = sem("sp_ok")
        t_ok = sem("t_ok")
        t_copied = sem("t_copied")
        sqrt_ok = sem("sqrt_ok")
        z_ok = sem("z_ok")
        last_tr = sem("last_tr")
        last_sb = sem("last_sb")
        cent_ok = sem("cent_ok")
        sq_ok = sem("sq_ok")
        sq_used = sem("sq_used")
        ln_ok = sem("ln_ok")
        sn_ok = sem("sn_ok")
        merged_ok = sem("merged_ok")
        mod_store = sem("mod_store")
        bc_in = sem("bc_in")
        x1_in = sem("x1_in")
        out_ps = sem("out_ps")
        x1_ok = sem("x1_ok")
        hf_dve = sem("hf_dve")
        hf_sum = sem("hf_sum")
        hf_store = [sem(f"hf_store{s}") for s in range(2)]
        hft_tr = sem("hft_tr")
        hft_act = sem("hft_act")
        hft_dve = sem("hft_dve")
        lg_ps = sem("lg_ps")
        exp_ask = sem("exp_ask")
        exp_ok = sem("exp_ok")
        sel_ok = sem("sel_ok")
        rank_ps = sem("rank_ps")
        mb_ok = sem("mb_ok")
        idx_ps = sem("idx_ps")
        idx_ok = sem("idx_ok")
        ov_ok = sem("ov_ok")
        wg_full = [sem(f"wg_full{s}") for s in range(2)]
        wu_full = [sem(f"wu_full{s}") for s in range(2)]
        wd_full = [sem(f"wd_full{s}") for s in range(2)]
        xg_full = [sem(f"xg_full{s}") for s in range(2)]
        xgt_ps = sem("xgt_ps")
        xgt_act = sem("xgt_act")
        xgt_dve = sem("xgt_dve")
        gate_ps = sem("gate_ps")
        up_ps = sem("up_ps")
        silu_ok = sem("silu_ok")
        h_ok = sem("h_ok")
        ht_ps = sem("ht_ps")
        ht_ok = sem("ht_ok")
        y_ps = sem("y_ps")
        y_act = sem("y_act")
        y_dve = sem("y_dve")
        y_store = [sem(f"y_store{s}") for s in range(2)]
        ov_w = sem("ov_w")
        ov_idx = sem("ov_idx")
        ov_x = sem("ov_x")
        ov_pe = sem("ov_pe")
        ov_dve = sem("ov_dve")
        ov_act = sem("ov_act")
        ov_st = sem("ov_st")
        y_in = [sem(f"y_in{s}") for s in range(2)]
        fin_dve = sem("fin_dve")
        fin_act = sem("fin_act")
        fin_ok = sem("fin_ok")
        outs_done = sem("outs_done")
        last_out = sem("last_out")
        hrow_out = sem("hrow_out")
        y_out = [sem(f"y_out{s}") for s in range(2)]

        def cols(w, g):
            return w[0].rearrange("(k p) n -> p k n", p=P)[:, :, g * GW:(g + 1) * GW]

        source = {"ada": lambda g: cols(a["w_ada"], g), "in": lambda g: cols(a["w_in"], g),
                  "co": lambda g: cols(a["w_conf_o"], g), "lo": lambda g: cols(a["w_lru_o"], g),
                  "wo": lambda g: cols(a["w_out"], g)}
        first_of = {}
        for n, key_n in enumerate(stream):
            first_of[key_n] = n
        x_p, x_s = a["x_prompt"][0], a["x_sample"].rearrange("s t d -> (s t) d")

        def x_rows(t):
            return x_s if t == NT - 1 else x_p[t * P:(t + 1) * P, :]

        work = []
        for g in (G_CA, G_CB, G_CA + 1, G_CB + 1, G_U, G_U + 1, G_GATE, G_GATE + 1):
            work += [("in", g, m) for m in range(GC)]
            if g == G_GATE:
                work += [("mean", 0, 0)]
                work += [(x, 0, m) for m in range(GC) for x in ("r", "i")]
            if g == G_GATE + 1:
                work += [("var", 0, 0)]
        for h, w in ((0, "co"), (1, "co"), (0, "lo"), (1, "lo")):
            g = (G_BC if w == "co" else G_BL) + h
            work += [("in", g, m) for m in range(GC)] + [(w, h, m) for m in range(GC)]
            if (h, w) == (0, "co"):
                work += [(x, 1, m) for m in range(GC) for x in ("r", "i")]
        by_act = [w[0] not in ("co", "lo") for w in work]
        place = {w: n for n, w in enumerate(work)}
        ada_after = {place[("in", g, m)]: js for g, m, js in
                     ((G_CA, 3, (4,)), (G_CB, 3, (5,)), (G_CA + 1, 3, (6, 7)), (G_CB + 1, 3, (8, 9)),
                      (G_U, 3, (10,)), (G_U + 1, 1, (11,)))}

        def used(eng, n):
            kind, g = stream[n]
            if kind == "ada":
                eng.wait_ge(ada_ps, g + 1)
            elif kind == "wo":
                eng.wait_ge(out_ps, NT * (g + 1))
            else:
                eng.wait_ge(pairs, place[(kind, g, GC - 1)] + 1)

        def pair(n):
            return ps[:, 2 * (n % 2):2 * (n % 2) + 2, 0:HALF]

        def drained(eng, n):
            if n < 0:
                return
            if by_act[n]:
                eng.wait_ge(pair_act, sum(by_act[:n + 1]))
            else:
                eng.wait_ge(pair_dve, n + 1 - sum(by_act[:n + 1]))

        def two(v):
            return v.rearrange("p (h t) -> p h t", h=2)

        def seqs(v):
            return v.rearrange("p (s t) -> p s t", s=NS)

        class Chain:

            def __init__(self, eng, s):
                self.eng, self.s, self.n = eng, s, 0

            def do(self, ins):
                ins.then_inc(self.s, 1)
                self.n += 1
                return ins

            def wait(self):
                self.eng.wait_ge(self.s, self.n)

            def wait_but_one(self):
                self.eng.wait_ge(self.s, self.n - 1)

            def link(self, ins):
                self.do(ins)
                self.wait()

        LAST_DMAS = (1 + NS) + (1 + NS)

        block = ctx.enter_context(nc.Block())

        @block.sync
        def _(sp):
            sp.dma_start(crow[0:1, :], a["c_prompt"]).then_inc(crow_in, 16)
            sp.dma_start(crow[1:NSEQ, :], a["c_sample"]).then_inc(crow_in, 16)

            def load(n):
                if n >= RING:
                    used(sp, n - RING)
                kind, g = stream[n]
                sp.dma_start(wslot[n % RING], source[kind](g)).then_inc(w_full[n % RING], 16)

            load(0)
            sp.dma_start(mod1[0:NSEQ, :], a["b_ada"][:, 0:4 * GW].to_broadcast([NSEQ, 4 * GW]))\
              .then_inc(bias_in, 16)
            rows = [(R_LCONV, a["state_lru_conv"][0].rearrange("s j d -> (s j) d")),
                    (R_H0, a["state_lru_h"][0]), (R_CW, a["conf_conv_w"][0]), (R_LW, a["lru_conv_w"][0]),
                    (R_CB, a["conf_conv_b"]), (R_LNG, a["conf_ln_g"]), (R_LNB, a["conf_ln_b"]),
                    (R_BA, a["lru_ba"]), (R_BX, a["lru_bx"]), (R_LAM, a["lru_lambda"]),
                    (R_GMIX, a["g_mix"]), (R_LB, a["lru_conv_b"]),
                    (R_BIN, a["b_in"][0].rearrange("(r d) -> r d", d=D))]
            for r, src in rows:
                sp.dma_start(vec[r:r + src.shape[0], :], src).then_inc(vec_in, 16)
            load(1)
            for t in range(NT):
                sp.dma_start(xt[0:TILES[t], t, :], x_rows(t)).then_inc(x_in, 16)
            load(2)
            for h in range(2):
                sp.dma_start(sconf[0:120, h, :], a["state_conf_conv"][0, 4 * h:4 * h + 4]
                             .rearrange("s j d -> (s j) d")).then_inc(sconf_in, 16)
            sp.wait_ge(bd_zero, 2)
            for w, src in zip(gate_w, (a["lru_wa"], a["lru_wx"])):
                for b in range(2):
                    sp.dma_start(w[64 * b:64 * b + 64, :, 64 * b:64 * b + 64],
                                 src[0].rearrange("(c b) i j -> b i c j", b=2)[b]).then_inc(bd_in, 16)
            sp.dma_start(wr[:, :, :], a["w_router"].rearrange("(k p) n -> p k n", p=P)).then_inc(bd_in, 16)
            sp.dma_start(br[:, :], a["b_router"].rearrange("(o n) -> o n", o=1).to_broadcast([P, NE]))\
              .then_inc(bd_in, 16)
            sp.dma_start(a["ccs"][0, :, 0:W30 - TS, :], a["state_conf_conv"][0, :, TS:W30, :])\
              .then_inc(outs_done, 16)
            for n in range(3, 7):
                load(n)
            sp.wait_ge(zero_ok, 1)
            sp.dma_start(y_scr[NE * CAP:, :].rearrange("(t p) d -> p t d", p=CAP),
                         zero_row[0:CAP, :].unsqueeze(1).to_broadcast([CAP, MAX_OVER, D])).then_inc(y_clear, 16)
            sp.wait_ge(x_tr, NT)
            sp.wait_ge(modt_tr, 1)
            sp.dma_start(mod2[0:1, :], a["b_ada"][:, 4 * GW:]).then_inc(bias2_in, 16)
            for n in range(7, 20):
                load(n)
            sp.wait_ge(ada_act, 8)
            sp.dma_start(mod_scr[:, 2 * D:], mod2[0:NSEQ, :]).then_inc(mod_store, 16)
            for n in range(20, 28):
                load(n)
            sp.wait_ge(mod_store, 16)

            def spread(dst, j):
                src = mod_scr[:, j * D:(j + 1) * D]
                sp.dma_start(dst[:, 0, :], src[0:1, :].to_broadcast([P, D])).then_inc(bc_in, 16)
                sp.dma_start(dst[0:TSAMP, 1, :], src[1:NSEQ, :].unsqueeze(1).to_broadcast([NS, TS, D]))\
                  .then_inc(bc_in, 16)

            sp.wait_ge(sn_ok, KC)
            for t in range(NT):
                sp.dma_start(x1[0:TILES[t], t, :], x_rows(t)).then_inc(x1_in, 16)
            sp.wait_ge(last_out, 16 * LAST_DMAS)
            spread(sh2_bc, 3)
            sp.wait_ge(z_ok, 2)
            spread(gt2_bc, 5)
            load(28)
            load(29)
            spread(gt1_bc, 2)
            spread(g2_bc, 4)
            sp.wait_ge(merged_ok, KC)
            sp.dma_start(gffn_bc, a["g_ffn"].to_broadcast([P, D])).then_inc(bc_in, 16)
            sp.dma_start(gfin_bc, a["g_final"].rearrange("(o n) -> o n", o=1).to_broadcast([P, D]))\
              .then_inc(bc_in, 16)

            def load_expert(e, s, used):
                for w, src, full, q in ((wg, a["w_gate"], wg_full, gate_ps), (wu, a["w_up"], wu_full, up_ps),
                                        (wd, a["w_down"], wd_full, y_ps)):
                    if used is not None:
                        sp.wait_ge(q, used)
                    sp.dma_start(w[s], src[0, bass.ds(e, 1)].rearrange("e (k p) n -> p (e k) n", p=P))\
                      .then_inc(full[s], 16)

            used(sp, NSTREAM - 2)
            sp.dma_start(wg[0], a["w_gate"][0, 0].rearrange("(k p) n -> p k n", p=P)).then_inc(wg_full[0], 16)
            used(sp, NSTREAM - 1)
            sp.dma_start(wu[0], a["w_up"][0, 0].rearrange("(k p) n -> p k n", p=P)).then_inc(wu_full[0], 16)
            sp.dma_start(wd[0], a["w_down"][0, 0].rearrange("(k p) n -> p k n", p=P)).then_inc(wd_full[0], 16)
            load_expert(1, 1, None)
            with sp.Fori(1, NE // 2) as i:
                load_expert(i * 2, 0, i * 2 - 1)
                load_expert(i * 2 + 1, 1, i * 2)
            sp.wait_ge(y_dve, NE)
            sp.wait_ge(y_ps, NE)
            sp.wait_ge(ov_ok, 1)
            n_over = sp.value_load(ovt[0:1, MAX_OVER:MAX_OVER + 1], min_val=0, max_val=MAX_OVER)
            with sp.If(n_over > 0):
                with sp.Fori(0, n_over) as k:
                    e = sp.value_load(ovt[0:1, bass.ds(k, 1)], min_val=0, max_val=NE - 1)
                    sp.wait_ge(ov_key, k + 1)
                    for w, src in ((wg, a["w_gate"]), (wu, a["w_up"]), (wd, a["w_down"])):
                        sp.dma_start(w[0], src[0, bass.ds(e, 1)].rearrange("e (k p) n -> p (e k) n", p=P))\
                          .then_inc(ov_w, 16)
            with sp.Else():
                sp.nop()
            for t in range(NT):
                sp.wait_ge(fin_ok, t + 1)
                dst = a["yp"][0, t * P:(t + 1) * P, :] if t < NT - 1 else a["ys"].rearrange("s t d -> (s t) d")
                sp.dma_start(dst, yo[0:TILES[t], t % 2, :]).then_inc(y_out[t % 2], 16)
            sp.wait_ge(y_out[0], 16 * 3)
            sp.wait_ge(y_out[1], 16 * 2)
            sp.wait_ge(outs_done, 16)
            sp.wait_ge(last_out, 16 * LAST_DMAS)
            sp.wait_ge(hrow_out, 32)

        @block.gpsimd
        def _(pool):
            g = nc.gpsimd
            ch = Chain(pool, pool_step)
            ch.do(g.memset(ident[:, :], 0.0))
            ch.do(g.memset(tri[:, :], 0.0))
            ch.wait()
            g.affine_select(out=ident[:, :], in_=ident[:, :], compare_op=ALU.not_equal, fill=1.0,
                            base=0, pattern=[[-1, P]], channel_multiplier=1).then_inc(consts, 1)
            g.affine_select(out=tri[:, :], in_=tri[:, :], compare_op=ALU.is_ge, fill=1.0,
                            base=0, pattern=[[-1, P]], channel_multiplier=1).then_inc(consts, 1)
            g.memset(ones[:, :], 1.0).then_inc(consts, 1)
            g.memset(sct[:, :, :], 0.0).then_inc(sct_zero, 1)
            for w in gate_w:
                g.memset(w[:, :, :], 0.0).then_inc(bd_zero, 1)

            g.memset(zero_row, 0.0).then_inc(zero_ok, 1)

            def table(dst, pattern, n, cm=0, base=0):
                r = dst.shape[0]
                ch.link(g.iota(iota_tmp[0:r, 0:n], pattern=pattern, base=base, channel_multiplier=cm))
                ch.link(g.tensor_copy(dst, iota_tmp[0:r, 0:n]))

            table(iota_e[:, :], [[1, NE]], NE)
            table(grp_e[:, :], [[1, NG], [0, EG]], NE)
            table(iota_g[:, :], [[1, NG]], NG)
            table(base_e[:, :], [[CAP, NE]], NE)
            table(slot_row[:, :], [[1, P]], P)
            table(tokid[:, :, 0], [[0, NT]], NT, cm=1)
            table(tokid[:, :, 1], [[1, NT]], NT)
            table(ovi[:, :], [[1, NE * MORE]], NE * MORE)
            table(ovk[:, :], [[1, MAX_OVER]], MAX_OVER)
            table(ov4[:, :], [[MORE, NE]], NE)
            ch.link(g.memset(valid[:, :], 0.0))
            ch.link(g.memset(valid[:, 0:NT - 1], 1.0))
            ch.link(g.memset(valid[0:TSAMP, NT - 1:NT], 1.0))
            g.memset(eps_ln[:, :], LN_EPS).then_inc(consts, 1)
            pool.wait_ge(rt_ok, 1)
            for k in range(KC):
                g.tensor_copy(u_s[:, k, :, 0:W3], rt[:, k, R_LCONV:R_LCONV + NS * W3]
                              .rearrange("p (s j) -> p s j", j=W3)).then_inc(us_ok, 1)
            g.memset(u[:, :, 0:W3], 0.0).then_inc(us_ok, 1)
            g.memset(glu[:, :, 0:W30], 0.0).then_inc(conv_new, 1)
            def gate_glu(k):
                n = place[("in", G_CB + k // GC, k % GC)]
                pool.wait_ge(pair_act, sum(by_act[:n + 1]))
                g.tensor_tensor(glu[:, k, W30:], glu[:, k, W30:], sg[:, k % 2, :], ALU.mult).then_inc(conv_ok, 1)

            gate_glu(0)
            gate_glu(1)
            pool.wait_ge(y_clear, 16)
            pool.wait_ge(sconf_ok, 4)
            for k in range(KC):
                pool.wait_ge(conv_ok, k + 1)
                ch.link(g.tensor_copy(glu_s[:, k, :, W30:], seqs(glu[:, k, W30 + TP:])))
                if k:
                    pool.wait_ge(prod_used, k)
                taps = rt[:, k, R_CW:R_CW + 31].unsqueeze(1).to_broadcast([P, NS, 31])
                for s in range(TS):
                    ins = g.tensor_tensor(prod[:, s], glu_s[:, k, :, s:s + 31], taps, ALU.mult)
                ins.then_inc(prod_ok, 1)
                if k + 2 < KC:
                    gate_glu(k + 2)
            pool.wait_ge(last_sb, 1)
            g.dma_start(a["ccp"][0, 0], last_glu[0:W30, :]).then_inc(last_out, 16)
            for s in range(NS):
                g.dma_start(a["ccs"][0, s, W30 - TS:, :], last_glu[W30 + TS * s:W30 + TS * (s + 1), :])\
                 .then_inc(last_out, 16)
            pool.wait_ge(last_sb, 2)
            g.dma_start(a["lcp"][0, 0], last_u[0:W3, :]).then_inc(last_out, 16)
            for s in range(NS):
                r = W3 + TS * (s + 1)
                g.dma_start(a["lcs"][0, s], last_u[r - W3:r, :]).then_inc(last_out, 16)
            pool.wait_ge(last_sb, 3)
            g.dma_start(a["hp"][0], last_h[0:1, :]).then_inc(hrow_out, 16)
            g.dma_start(a["hs"][0], last_h[TS:TS * NS + 1:TS, :]).then_inc(hrow_out, 16)
            for t in range(NT):
                n = TILES[t]
                pool.wait_ge(hf_dve, t + 1)
                if t == 0:
                    pool.wait_ge(bc_in, 16 * 10)
                g.tensor_tensor(hf[0:n, t % 2, :], hf[0:n, t % 2, :], sh2_bc[0:n, t // 4, :], ALU.add)\
                 .then_inc(hf_sum, 1)
                pool.wait_ge(hf_sum, t + 1)
                g.dma_start(hf_scr[t * P:t * P + n, :], hf[0:n, t % 2, :]).then_inc(hf_store[t % 2], 16)
            pool.wait_ge(hf_store[0], 16 * 3)
            pool.wait_ge(hf_store[1], 16 * 2)

            def gather(e, s):
                g.indirect_dma_start(out=xg[:, s, :], out_offset=None, in_=hf_scr,
                                     in_offset=bass.IndirectOffsetOnAxis(ap=idx_i[:, e:e + 1], axis=0))\
                 .then_inc(xg_full[s], 16)

            def store(e, s):
                g.dma_start(y_scr[e * CAP:(e + 1) * CAP, :], yb[0:CAP, s, :]).then_inc(y_store[s], 16)

            pool.wait_ge(lg_ps, NT)
            for e in range(NE + 2):
                if e < NE:
                    if e >= 2:
                        pool.wait_ge(xgt_ps, e - 1)
                    pool.wait_ge(idx_ok, e + 1)
                    gather(e, e % 2)
                if e >= 2:
                    pool.wait_ge(y_act, e - 1)
                    pool.wait_ge(y_dve, e - 1)
                    store(e - 2, e % 2)
            pool.wait_ge(y_store[0], 16 * (NE // 2))
            pool.wait_ge(y_store[1], 16 * (NE // 2))
            pool.wait_ge(ov_ok, 1)
            n_over = pool.value_load(ovt[0:1, MAX_OVER:MAX_OVER + 1], min_val=0, max_val=MAX_OVER)
            with pool.If(n_over > 0):
                with pool.Fori(0, n_over) as k:
                    pool.wait_ge(ov_idx, k + 1)
                    g.tensor_tensor(idx_vg[:, :], idx_vf[:, :], ovk[:, 0:1], ALU.add)
                    pool.drain()
                    g.tensor_copy(idx_ov[:, :], idx_vg[:, :])
                    pool.drain()
                    g.indirect_dma_start(out=xg[:, 0, :], out_offset=None, in_=hf_scr,
                                         in_offset=bass.IndirectOffsetOnAxis(ap=idx_ov[:, :], axis=0))\
                     .then_inc(ov_x, 16)
                    pool.wait_ge(ov_dve, k * 4 + 4)
                    g.dma_start(y_scr[bass.ds((k + NE) * CAP, CAP), :], yb[0:CAP, 0, :]).then_inc(ov_st, 16)
                    pool.wait_ge(ov_st, k * 16 + 16)
            with pool.Else():
                pool.nop()
            pool.wait_ge(slot_ok, 2)
            for t in range(NT):
                n = TILES[t]
                if t >= 2:
                    pool.wait_ge(fin_dve, t - 1)
                for j, dst in enumerate((ya, yc)):
                    g.indirect_dma_start(out=dst[0:n, t % 2, :], out_offset=None, in_=y_scr,
                                         in_offset=bass.IndirectOffsetOnAxis(ap=slot_i[0:n, j, t:t + 1], axis=0))\
                     .then_inc(y_in[t % 2], 16)

        @block.scalar
        def _(act):
            s_ = nc.scalar
            ch = Chain(act, act_step)
            act.wait_ge(crow_in, 32)
            s_.activation(crow[0:NSEQ, :], crow[0:NSEQ, :], ACT.Silu).then_inc(csilu, 1)
            act.wait_ge(x_in, 16 * NT)
            junk1 = region_d[:, 4 * D:5 * D]
            act.wait_ge(ssq_clear, 1)
            for t in range(NT):
                n = TILES[t]
                s_.activation(junk1[0:n, :], xt[0:n, t, :], ACT.Square, accum_out=ssq[0:n, t:t + 1]).then_inc(ssq_ok, 1)
                act.wait_ge(ssq_ok, t + 1)
            act.wait_ge(sct_ok, 1)
            act.wait_ge(sp_ask, 1)
            s_.activation(spt[:, 1, :], spt[:, 0, :], ACT.Exp, scale=-1.0).then_inc(sp_exp, 1)
            act.wait_ge(rms_ask, 1)
            s_.activation(nt1[:, :], ssq[:, :], ACT.Sqrt).then_inc(rms_sqrt, 1)
            act.wait_ge(rstd_ok, 1)
            for t in range(NT):
                n = TILES[t]
                s_.activation(xt[0:n, t, :], xt[0:n, t, :], ACT.Copy, scale=rstd[0:n, t:t + 1]).then_inc(xn_ok, 1)
            act.wait_ge(modt_ok, 1)
            for t in range(NT - 1):
                act.wait_ge(x_tr, t + 1)
                for k in range(4, KC):
                    ins = s_.activation(hm[:, k, t * P:(t + 1) * P], ps[:, 5 + 2 * (t % 2), (k - 4) * P:(k - 3) * P],
                                        ACT.Identity, bias=modt[:, k, 0:1], scale=amod[:, k, 0:1])
                ins.then_inc(hm_act, 1)

            count = {"sg": 0, "sq": 0}

            def drain(n):
                kind, g, m = work[n]
                act.wait_ge(pairs, n + 1)
                if kind == "in":
                    k = (g % 2) * GC + m
                    bias = rt[:, k, R_BIN + g // 2:R_BIN + g // 2 + 1]
                    if g in (G_CA, G_CA + 1):
                        ins = s_.activation(two(glu[:, k, W30:]), pair(n), ACT.Identity, bias=bias)
                    elif g in (G_CB, G_CB + 1):
                        if k >= 2:
                            act.wait_ge(conv_ok, k - 1)
                        ins = s_.activation(two(sg[:, k % 2, :]), pair(n), ACT.Sigmoid, bias=bias)
                    elif g in (G_U, G_U + 1):
                        ins = s_.activation(two(u[:, k, W3:]), pair(n), ACT.Identity, bias=bias)
                    elif g in (G_GATE, G_GATE + 1):
                        ins = s_.activation(two(z[:, k, :]), pair(n), ACT.Gelu_apprx_tanh, bias=bias)
                    else:
                        if m == 0 and g == G_BL + 1:
                            act.wait_ge(merged_ok, GC)
                        elif m == 0 and g != G_BC:
                            act.wait_ge(pair_dve, GC if g == G_BC + 1 else 2 * GC)
                        elif m == GC - 1 and g == G_BC:
                            act.wait_ge(xc_ok, KC)
                        ins = s_.activation(two(bg[:, m, :]), pair(n), ACT.Sigmoid, bias=bias)
                elif kind == "r":
                    k = g * GC + m
                    ins = s_.activation(two(tt[:, m, :]), pair(n), ACT.Sigmoid, bias=rt[:, k, R_BA:R_BA + 1])
                elif kind == "i":
                    k = g * GC + m
                    ins = s_.activation(two(ii[:, m, :]), pair(n), ACT.Sigmoid, bias=rt[:, k, R_BX:R_BX + 1])
                elif kind == "mean":
                    act.wait_ge(last_tr, 1)
                    ins = s_.activation(two(ln_mean), pair(n), ACT.Copy, scale=1.0 / D)
                elif kind == "var":
                    ins = s_.activation(two(ln_rstd), pair(n), ACT.Sqrt, bias=eps_ln[:, :], scale=1.0 / D)
                ins.then_inc(pair_act, 1)

            def squares():
                act.wait_ge(cent_ok, 1)
                for k in range(KC):
                    if k >= 2:
                        act.wait_ge(sq_used, k - 1)
                    s_.activation(ln_sq[:, k % 2, :], dc[:, k, :], ACT.Square).then_inc(sq_ok, 1)

            act.wait_ge(consts, 4)
            for n in range(len(work)):
                if not by_act[n]:
                    continue
                kind, g, m = work[n]
                if (kind, g, m) == ("in", G_GATE, 0):
                    act.wait_ge(mod_store, 16)
                if (kind, g, m) == ("var", 0, 0):
                    squares()
                if (kind, g, m) == ("in", G_BC, 0):
                    act.wait_ge(ln_ok, 1)
                    for k in range(KC):
                        s_.activation(dc[:, k, :], dc[:, k, :], ACT.Silu, bias=rt[:, k, R_LNB:R_LNB + 1],
                                      scale=rt[:, k, R_LNG:R_LNG + 1]).then_inc(sn_ok, 1)
                drain(n)
                for j in ada_after.get(n - 1, ()):
                    act.wait_ge(ada_sum, j + 1)
                    s_.activation(mod2[0:NSEQ, (j - 4) * GW:(j - 3) * GW], ps[0:NSEQ, 4 + j % 2, :], ACT.Copy)\
                      .then_inc(ada_act, 1)
                for j in ada_after.get(n, ()):
                    act.wait_ge(ada_ps, j + 1)
                    act.wait_ge(ada_sum, j - 1)
                    s_.activation(ada_tmp[:, j % 2, :], ps[:, 6 + j % 2, :], ACT.Copy).then_inc(ada_cp, 1)
                if kind == "i" and m == GC - 1:
                    act.wait_ge(sp_ok, 1)
                    act.wait_ge(pair_act, sum(by_act[:n + 1]))
                    for c in range(GC):
                        ins = s_.activation(tt[:, c, :], tt[:, c, :], ACT.Tanh,
                                            scale=sp4[:, g * GC + c:g * GC + c + 1])
                    ins.then_inc(t_ok, 1)
                if (kind, g, m) in (("in", G_GATE + 1, 1), ("in", G_BC + 1, 1)):
                    act.wait_ge(t_copied, 1 if g == G_GATE + 1 else 2)
                    s_.activation(tt[:, :, :], tt[:, :, :], ACT.Sqrt).then_inc(sqrt_ok, 1)

            def hft_half(t):
                n = TILES[t]
                act.wait_ge(hft_tr, t + 1)
                if t >= 2:
                    act.wait_ge(lg_ps, t - 1)
                s_.activation(hft[:, t % 2, 4:KC, 0:n],
                              ps[:, 5, :].rearrange("p (k c) -> p k c", k=4)[:, :, 0:n], ACT.Copy).then_inc(hft_act, 1)

            for t in range(NT):
                n = TILES[t]
                act.wait_ge(x1_ok, t + 1)
                if t:
                    act.wait_ge(ssq_ok, NT + t)
                s_.activation(yb[0:n, 1, :], x1[0:n, t, :], ACT.Square, accum_out=ssq[0:n, t:t + 1]).then_inc(ssq_ok, 1)
                if t:
                    hft_half(t - 1)
                act.wait_ge(rms_ask, t + 2)
                s_.activation(nt1[0:n, t:t + 1], ssq[0:n, t:t + 1], ACT.Sqrt).then_inc(rms_sqrt, 1)
            hft_half(NT - 1)
            act.wait_ge(exp_ask, 1)
            s_.activation(lg, lg, ACT.Exp).then_inc(exp_ok, 1)

            def xgt_half(e):
                act.wait_ge(xgt_ps, e + 1)
                s_.activation(xgt[:, 4:KC, :], ps[:, 3, :].rearrange("p (k c) -> p k c", k=4), ACT.Copy)\
                  .then_inc(xgt_act, 1)

            def silu(e):
                act.wait_ge(gate_ps, e + 1)
                s_.activation(act_g, ps[:, 0, :], ACT.Silu).then_inc(silu_ok, 1)

            def y_half(e, s, stored=None):
                act.wait_ge(y_ps, e + 1)
                if stored is not None:
                    act.wait_ge(y_store[s], stored)
                s_.activation(yb[:, s, DE:], ps[:, 6, :], ACT.Copy).then_inc(y_act, 1)

            def turn(e):
                act.wait_ge(ht_ps, e + 1)
                s_.activation(act_t, ps[:, 4, :].rearrange("p (k c) -> p k c", k=DE // P), ACT.Copy)\
                  .then_inc(ht_ok, 1)

            xgt_half(0)
            silu(0)
            xgt_half(1)
            turn(0)
            silu(1)
            y_half(0, 0)
            xgt_half(2)
            turn(1)
            silu(2)
            y_half(1, 1)
            xgt_half(3)
            turn(2)
            with act.Fori(1, NE // 2 - 1) as i:
                for s in range(2):
                    e = i * 2 + 1 + s
                    silu(e)
                    y_half(e - 1, s, i * 16)
                    xgt_half(e + 1)
                    turn(e)
            silu(NE - 1)
            y_half(NE - 2, 0, 16 * (NE // 2 - 1))
            turn(NE - 1)
            y_half(NE - 1, 1, 16 * (NE // 2 - 1))

            act.wait_ge(ov_ok, 1)
            n_over = act.value_load(ovt[0:1, MAX_OVER:MAX_OVER + 1], min_val=0, max_val=MAX_OVER)
            with act.If(n_over > 0):
                with act.Fori(0, n_over) as k:
                    act.wait_ge(ov_pe, k * 5 + 3)
                    s_.activation(act_g, ps[:, 0, :], ACT.Silu).then_inc(ov_act, 1)
            with act.Else():
                act.nop()
            for t in range(NT):
                n = TILES[t]
                act.wait_ge(fin_dve, t + 1)
                if t:
                    act.wait_ge(fin_act, t)
                s_.activation(junk[0:n, :], x1[0:n, t, :], ACT.Square, accum_out=ssq[0:n, t:t + 1]).then_inc(fin_act, 1)
                act.wait_ge(rms_ask, NT + t + 2)
                s_.activation(nt1[0:n, t:t + 1], ssq[0:n, t:t + 1], ACT.Sqrt).then_inc(rms_sqrt, 1)

        @block.tensor
        def _(pe):
            mm, tr = nc.tensor.matmul, nc.tensor.transpose
            pe.wait_ge(consts, 3)
            pe.wait_ge(csilu, 1)
            for k in range(KC):
                ins = tr(ps[:, 4, k * NSEQ:(k + 1) * NSEQ], crow[0:NSEQ, k * P:(k + 1) * P], ident[0:NSEQ, 0:NSEQ])
            ins.then_inc(c_tr, 1)
            pe.wait_ge(vec_in, 16 * 13)
            for k in range(KC):
                ins = tr(ps[:, 5 + k // 4, (k % 4) * NVEC:(k % 4 + 1) * NVEC], vec[0:NVEC, k * P:(k + 1) * P],
                         ident[0:NVEC, 0:NVEC])
            ins.then_inc(vec_tr, 1)
            pe.wait_ge(sct_ok, 1)

            def ada(n, j):
                pe.wait_ge(w_full[n % RING], 16 * (n // RING + 1))
                if j >= 2:
                    pe.wait_ge(ada_cp, j - 1)
                for k in range(KC):
                    q = k % 4
                    ins = mm(ps[q * CT:(q + 1) * CT, j % 2 if j < 4 else 6 + j % 2, :], sct[:, k, :],
                             wslot[n % RING][:, k, :], start=(k < 4), stop=(k >= KC - 4))
                ins.then_inc(ada_ps, 1)

            def ada_add(j):
                pe.wait_ge(ada_cp, j + 1)
                if j in (2, 3):
                    pe.wait_ge(ada_ok, j - 1)
                if j >= 6:
                    pe.wait_ge(ada_act, j - 5)
                out = ps[0:CT, 2 + j % 2 if j < 4 else 4 + j % 2, :]
                if j >= 4:
                    mm(out, ones[0:1, 0:CT], mod2[0:1, (j - 4) * GW:(j - 3) * GW], start=True, stop=False)
                mm(out, sel[:, :], ada_tmp[:, j % 2, :], start=(j < 4), stop=True).then_inc(ada_sum, 1)

            pe.wait_ge(sel_mat, P // CT)
            for j in range(4):
                ada(j, j)
                if j:
                    ada_add(j - 1)
            ada_add(3)
            pe.wait_ge(sconf_in, 32)
            for b in range(4):
                if b == 0:
                    pe.wait_ge(rt_ok, 1)
                for j in range(4):
                    k, h = 2 * b + j // 2, j % 2
                    ins = tr(ps[:, 4 + b, j * 120:(j + 1) * 120], sconf[0:120, h, k * P:(k + 1) * P],
                             ident[0:120, 0:120])
                ins.then_inc(sconf_tr, 1)
            pe.wait_ge(ada_ok, 4)
            for j in range(2 * KC):
                ins = tr(ps[:, 2, j * NSEQ:(j + 1) * NSEQ], mod1[0:NSEQ, j * P:(j + 1) * P], ident[0:NSEQ, 0:NSEQ])
            ins.then_inc(modt_tr, 1)
            for t in range(NT):
                n = TILES[t]
                pe.wait_ge(xn_ok, t + 1)
                if t < 2:
                    pe.wait_ge(sconf_ok, 4)
                else:
                    pe.wait_ge(hm_dve, t - 1)
                    pe.wait_ge(hm_act, t - 1)
                for k in range(KC):
                    ins = tr(ps[:, 4 + 2 * (t % 2) + k // 4, (k % 4) * P:(k % 4) * P + n],
                             xt[0:n, t, k * P:(k + 1) * P], ident[0:n, 0:n])
                ins.then_inc(x_tr, 1)
            pe.wait_ge(hm_dve, NT)
            pe.wait_ge(hm_act, NT - 1)
            pe.wait_ge(modt_ok, 1)

            def chunk(n, w, m, rhs):
                for k in range(KC):
                    for h in range(2):
                        ins = mm(ps[:, 2 * (n % 2) + h, 0:HALF], w[:, k, m * P:(m + 1) * P],
                                 rhs[:, k, h * HALF:(h + 1) * HALF], start=(k == 0), stop=(k == KC - 1))
                return ins

            def rows_out(src, cols0, n, done):
                for k in range(KC):
                    ins = tr(ps[0:n, 4 + k // 4, (k % 4) * P:(k % 4 + 1) * P], src[:, k, cols0:cols0 + n], ident[:, :])
                ins.then_inc(last_tr, 1)

            rhs_of = {"in": hm, "co": dc, "lo": z}
            for n, (kind, g, m) in enumerate(work):
                if kind in rhs_of:
                    f = first_of[(kind, g)]
                    if m == 0:
                        pe.wait_ge(w_full[f % RING], 16 * (f // RING + 1))
                        if kind == "co":
                            pe.wait_ge(sn_ok, KC)
                        if kind == "lo":
                            pe.wait_ge(z_ok, 2)
                    drained(pe, n - 2)
                    ins = chunk(n, wslot[f % RING], m, rhs_of[kind])
                    ins.then_inc(pairs, 1)
                elif kind in ("r", "i"):
                    drained(pe, n - 2)
                    pe.wait_ge(xc_ok, g * GC + m + 1)
                    for h in range(2):
                        ins = mm(ps[:, 2 * (n % 2) + h, 0:HALF], gate_w[kind == "i"][:, g * GC + m, :],
                                 xc[:, m, h * HALF:(h + 1) * HALF], start=True, stop=True)
                    ins.then_inc(pairs, 1)
                elif kind == "mean":
                    drained(pe, n - 2)
                    pe.wait_ge(dc_ok, KC)
                    for k in range(KC):
                        for h in range(2):
                            ins = mm(ps[:, 2 * (n % 2) + h, 0:HALF], ones[:, :], dc[:, k, h * HALF:(h + 1) * HALF],
                                     start=(k == 0), stop=(k == KC - 1))
                    ins.then_inc(pairs, 1)
                    rows_out(glu, TP, 62, 0)
                elif kind == "var":
                    drained(pe, n - 2)
                    for k in range(KC):
                        pe.wait_ge(sq_ok, k + 1)
                        for h in range(2):
                            ins = mm(ps[:, 2 * (n % 2) + h, 0:HALF], ones[:, :], ln_sq[:, k % 2, h * HALF:(h + 1) * HALF],
                                     start=(k == 0), stop=(k == KC - 1))
                        if k < KC - 1:
                            ins.then_inc(sq_used, 1)
                    ins.then_inc(pairs, 1)
                    pe.wait_ge(last_sb, 1)
                    rows_out(u, TP, 35, 1)
                if (kind, g, m) == ("in", G_U, GC - 1):
                    pe.wait_ge(bd_in, 16 * 6)
                for j in ada_after.get(n - 1, ()):
                    pe.wait_ge(bias2_in, 16)
                    ada_add(j)
                for j in ada_after.get(n, ()):
                    ada(first_of[("ada", j)], j)
                if (kind, g, m) == ("lo", 0, 0):
                    pe.wait_ge(last_sb, 2)
                    rows_out(hlast, 0, 33, 2)
            drained(pe, len(work) - 1)
            drained(pe, len(work) - 2)
            pe.wait_ge(merged_ok, KC)

            def w_out(t):
                n = TILES[t]
                for h in range(2):
                    f = first_of[("wo", h)]
                    pe.wait_ge(w_full[f % RING], 16 * (f // RING + 1))
                    j = 2 * t + h
                    if j >= 4:
                        pe.wait_ge(x1_half, j - 3)
                    for k in range(KC):
                        ins = mm(ps[0:n, j % 4, :], merged[:, k, t * P:t * P + n], wslot[f % RING][:, k, :],
                                 start=(k == 0), stop=(k == KC - 1))
                    ins.then_inc(out_ps, 1)

            def hf_turn(t):
                n = TILES[t]
                pe.wait_ge(hf_sum, t + 1)
                if t:
                    pe.wait_ge(hft_act, t)
                    pe.wait_ge(hft_dve, t)
                for k in range(KC):
                    ins = tr(ps[:, 4 + k // 4, (k % 4) * P:(k % 4) * P + n], hf[0:n, t % 2, k * P:(k + 1) * P],
                             ident[0:n, 0:n])
                ins.then_inc(hft_tr, 1)

            def logits(t):
                n = TILES[t]
                pe.wait_ge(hft_act, t + 1)
                pe.wait_ge(hft_dve, t + 1)
                for k in range(KC):
                    ins = mm(ps[0:n, 6, t * NE:(t + 1) * NE], hft[:, t % 2, k, 0:n], wr[:, k, :],
                             start=(k == 0), stop=(k == KC - 1))
                ins.then_inc(lg_ps, 1)

            for t in range(NT):
                w_out(t)
                if t == 0:
                    pe.wait_ge(last_sb, 3)
                if t >= 2:
                    logits(t - 2)
                if t:
                    hf_turn(t - 1)
            logits(NT - 2)
            hf_turn(NT - 1)
            logits(NT - 1)
            pe.wait_ge(sel_ok, 1)
            for t in range(NT + 1):
                for q in range(min(t, NT - 1) + 1):
                    last = q == min(t, NT - 1)
                    w = tri if last and t < NT else ones
                    ins = mm(ps[:, 7, t * NE:(t + 1) * NE], w[:, :], selb[:, q, :], start=(q == 0), stop=last)
            ins.then_inc(rank_ps, 1)
            def index(e, s, first=False):
                pe.wait_ge(mb_ok, e + 1)
                if not first:
                    pe.wait_ge(idx_cp, e)
                for t in range(NT):
                    ins = mm(ps[:, 7, 256 + 2 * s:258 + 2 * s], mb[:, s, t, :], tokid[:, t, :], start=(t == 0), stop=(t == NT - 1))
                ins.then_inc(idx_ps, 1)

            for e in range(AHEAD):
                index(e, e % 2, first=(e == 0))

            def xg_turn(e, s, n16):
                pe.wait_ge(xg_full[s], n16)
                for k in range(KC):
                    ins = tr(ps[:, 2 + k // 4, (k % 4) * P:(k % 4 + 1) * P], xg[:, s, k * P:(k + 1) * P], ident[:, :])
                ins.then_inc(xgt_ps, 1)

            def gate_up(e, s, n16):
                pe.wait_ge(xgt_act, e + 1)
                pe.wait_ge(xgt_dve, e + 1)
                for w, full, b, out_s in ((wg, wg_full, 0, gate_ps), (wu, wu_full, 1, up_ps)):
                    pe.wait_ge(full[s], n16)
                    for k in range(KC):
                        ins = mm(ps[:, b, :], xgt[:, k, :], w[s][:, k, :], start=(k == 0), stop=(k == KC - 1))
                    ins.then_inc(out_s, 1)

            def h_turn(e):
                pe.wait_ge(h_ok, e + 1)
                for k in range(DE // P):
                    ins = tr(ps[:, 4, k * P:(k + 1) * P], act_g[:, k * P:(k + 1) * P], ident[:, :])
                ins.then_inc(ht_ps, 1)

            def down(e, s, n16, before=True):
                pe.wait_ge(ht_ok, e + 1)
                pe.wait_ge(wd_full[s], n16)
                if before:
                    pe.wait_ge(y_act, e)
                    pe.wait_ge(y_dve, e)
                for k in range(DE // P):
                    for h in range(2):
                        ins = mm(ps[:, 5 + h, :], act_t[:, k, :], wd[s][:, k, h * DE:(h + 1) * DE],
                                 start=(k == 0), stop=(k == DE // P - 1))
                ins.then_inc(y_ps, 1)

            def step(e, s, pair_n, index_too=True, down_before=True, turn_next=True):
                gate_up(e, s, 16 * pair_n)
                if index_too:
                    index(e + AHEAD, 1 - s)
                if down_before:
                    down(e - 1, 1 - s, 16 * (pair_n - 1 + s))
                if turn_next:
                    xg_turn(e + 1, 1 - s, 16 * (pair_n + s))
                h_turn(e)

            xg_turn(0, 0, 16)
            gate_up(0, 0, 16)
            index(AHEAD, 1)
            xg_turn(1, 1, 16)
            h_turn(0)
            gate_up(1, 1, 16)
            index(1 + AHEAD, 0)
            down(0, 0, 16, before=False)
            xg_turn(2, 0, 32)
            h_turn(1)
            step(2, 0, 2)
            with pe.Fori(1, 6) as i:
                step(i * 2 + 1, 1, i + 1)
                step(i * 2 + 2, 0, i + 2)
            step(13, 1, 7, index_too=False)
            step(14, 0, 8, index_too=False)
            step(15, 1, 8, index_too=False, turn_next=False)
            down(NE - 1, 1, 16 * (NE // 2))

            pe.wait_ge(ov_ok, 1)
            n_over = pe.value_load(ovt[0:1, MAX_OVER:MAX_OVER + 1], min_val=0, max_val=MAX_OVER)
            with pe.If(n_over > 0):
                with pe.Fori(0, n_over) as k:
                    pe.wait_ge(mb_ok, k + NE + 1)
                    for t in range(NT):
                        ins = mm(ps[:, 7, 0:2], mb[:, 0, t, :], tokid[:, t, :], start=(t == 0), stop=(t == NT - 1))
                    ins.then_inc(ov_pe, 1)
                    pe.wait_ge(ov_x, k * 16 + 16)
                    for c in range(KC):
                        ins = tr(ps[:, 2 + c // 4, (c % 4) * P:(c % 4 + 1) * P], xg[:, 0, c * P:(c + 1) * P], ident[:, :])
                    ins.then_inc(ov_pe, 1)
                    pe.wait_ge(ov_dve, k * 4 + 1)
                    pe.wait_ge(ov_w, k * 48 + 48)
                    for w, b in ((wg, 0), (wu, 1)):
                        for c in range(KC):
                            ins = mm(ps[:, b, :], xgt[:, c, :], w[0][:, c, :], start=(c == 0), stop=(c == KC - 1))
                    ins.then_inc(ov_pe, 1)
                    pe.wait_ge(ov_dve, k * 4 + 2)
                    for c in range(DE // P):
                        ins = tr(ps[:, 4, c * P:(c + 1) * P], act_g[:, c * P:(c + 1) * P], ident[:, :])
                    ins.then_inc(ov_pe, 1)
                    pe.wait_ge(ov_dve, k * 4 + 3)
                    for c in range(DE // P):
                        for h in range(2):
                            ins = mm(ps[:, 5 + h, :], act_t[:, c, :], wd[0][:, c, h * DE:(h + 1) * DE],
                                     start=(c == 0), stop=(c == DE // P - 1))
                    ins.then_inc(ov_pe, 1)
            with pe.Else():
                pe.nop()

        @block.vector
        def _(dve):
            v = nc.vector
            ch = Chain(dve, dve_step)
            v.memset(ssq[:, :], 1.0).then_inc(ssq_clear, 1)
            dve.wait_ge(consts, 3)
            for q in range(P // CT):
                v.tensor_copy(sel[q * CT:(q + 1) * CT, :], ident[q * CT:(q + 1) * CT, q * CT:(q + 1) * CT])\
                 .then_inc(sel_mat, 1)
            dve.wait_ge(c_tr, 1)
            dve.wait_ge(sct_zero, 1)
            v.tensor_copy(sct[:, :, 0:NSEQ], ps[:, 4, 0:KC * NSEQ].rearrange("p (k s) -> p k s", k=KC)).then_inc(sct_ok, 1)
            dve.wait_ge(vec_tr, 1)
            ch.link(v.tensor_copy(rt[:, 0:4, :], ps[:, 5, 0:4 * NVEC].rearrange("p (k r) -> p k r", k=4)))
            ch.do(v.tensor_copy(rt[:, 4:8, :], ps[:, 6, 0:4 * NVEC].rearrange("p (k r) -> p k r", k=4)))
            ch.wait()
            lam = rt[:, :, R_LAM]
            ch.link(v.tensor_scalar(spt[:, 0, :], lam, -1.0, None, ALU.mult))
            v.tensor_tensor(spt[:, 0, :], spt[:, 0, :], lam, ALU.max).then_inc(sp_ask, 1)
            v.tensor_copy(spt[:, 3, :], lam).then_inc(rt_ok, 1)
            def ada_copy(j):
                dve.wait_ge(ada_ps, j + 1)
                v.tensor_copy(ada_tmp[:, j % 2, :], ps[:, j % 2, :]).then_inc(ada_cp, 1)

            def ada_rows(j):
                dst = mod1[0:NSEQ, j * GW:(j + 1) * GW]
                dve.wait_ge(ada_sum, j + 1)
                dve.wait_ge(bias_in, 16)
                v.tensor_tensor(dst, ps[0:NSEQ, 2 + j % 2, :], dst, ALU.add).then_inc(ada_ok, 1)

            ada_copy(0)
            ada_copy(1)
            ada_rows(0)
            dve.wait_ge(ssq_ok, NT)
            v.tensor_scalar(ssq[:, :], ssq[:, :], 1.0 / D, RMS_EPS, ALU.mult, ALU.add).then_inc(rms_ask, 1)
            dve.wait_ge(rms_sqrt, 1)

            def newton(n, lo, hi):
                r, q, w = rstd[0:n, lo:hi], nt1[0:n, lo:hi], ssq[0:n, lo:hi]
                ch.link(v.reciprocal(r, q))
                ch.link(v.tensor_tensor(q, r, r, ALU.mult))
                ch.link(v.tensor_tensor(q, q, w, ALU.mult))
                ch.link(v.tensor_scalar(q, q, -0.5, 1.5, ALU.mult, ALU.add))
                return v.tensor_tensor(r, r, q, ALU.mult)

            newton(P, 0, NT).then_inc(rstd_ok, 1)
            dve.wait_ge(sp_exp, 1)
            e_, y_, y2, acc = spt[:, 1, :], spt[:, 0, :], spt[:, 2, :], sp4[:, :]
            ch.link(v.tensor_scalar(y2, e_, 2.0, None, ALU.add))
            ch.link(v.reciprocal(y2, y2))
            ch.link(v.tensor_tensor(y_, e_, y2, ALU.mult))
            ch.link(v.tensor_tensor(y2, y_, y_, ALU.mult))
            ch.link(v.tensor_scalar(acc, y2, 1.0 / 17, 1.0 / 15, ALU.mult, ALU.add))
            for c in (13, 11, 9, 7, 5, 3, 1):
                ch.link(v.tensor_tensor(acc, acc, y2, ALU.mult))
                ch.link(v.tensor_scalar(acc, acc, 1.0 / c, None, ALU.add))
            ch.link(v.tensor_tensor(acc, acc, y_, ALU.mult))
            ch.link(v.tensor_scalar(e_, spt[:, 3, :], -1.0, 0.0, ALU.mult, ALU.max))
            ch.link(v.scalar_tensor_tensor(acc, acc, 2.0, e_, ALU.mult, ALU.add))
            v.tensor_scalar(acc, acc, 4.0, None, ALU.mult).then_inc(sp_ok, 1)

            ada_copy(2)
            ada_rows(1)
            ada_copy(3)
            ada_rows(2)
            ada_rows(3)
            for b in range(4):
                dve.wait_ge(sconf_tr, b + 1)
                for k in range(2):
                    ins = v.tensor_copy(glu_s[:, 2 * b + k, :, 0:W30],
                                        ps[:, 4 + b, k * 240:(k + 1) * 240].rearrange("p (s j) -> p s j", s=NS))
                ins.then_inc(sconf_ok, 1)
            dve.wait_ge(modt_tr, 1)
            ch.link(v.tensor_copy(modt[:, :, :], ps[:, 2, 0:2 * KC * NSEQ].rearrange("p (j s) -> p j s", s=NSEQ)))
            for k in range(KC):
                ins = v.tensor_scalar(amod[:, k, :], modt[:, KC + k, :], 1.0, rt[:, k, R_GMIX:R_GMIX + 1], ALU.add, ALU.mult)
            ins.then_inc(modt_ok, 1)
            dve.wait_ge(modt_ok, 1)
            for t in range(NT - 1):
                dve.wait_ge(x_tr, t + 1)
                for k in range(4):
                    ins = v.tensor_scalar(hm[:, k, t * P:(t + 1) * P], ps[:, 4 + 2 * (t % 2), k * P:(k + 1) * P],
                                          amod[:, k, 0:1], modt[:, k, 0:1], ALU.mult, ALU.add)
                ins.then_inc(hm_dve, 1)
            dve.wait_ge(x_tr, NT)
            for k in range(KC):
                dst = seqs(hm[:, k, TP:])
                src = seqs(ps[:, 4 + k // 4, (k % 4) * P:(k % 4) * P + TSAMP])
                ch.do(v.tensor_tensor(dst, src, amod[:, k, 1:].unsqueeze(2).to_broadcast([P, NS, TS]), ALU.mult))
            ch.wait()
            for k in range(KC):
                dst = seqs(hm[:, k, TP:])
                ins = v.tensor_tensor(dst, dst, modt[:, k, 1:].unsqueeze(2).to_broadcast([P, NS, TS]), ALU.add)
            ins.then_inc(hm_dve, 1)

            def conformer(k):
                dve.wait_ge(conv_ok, k + 1)
                acc = (dc[:, k, 0:TP], odd)
                ch.do(v.tensor_scalar(acc[0], glu[:, k, 0:TP], rt[:, k, R_CW:R_CW + 1], rt[:, k, R_CB:R_CB + 1],
                                      ALU.mult, ALU.add))
                ch.do(v.tensor_scalar(acc[1], glu[:, k, 1:1 + TP], rt[:, k, R_CW + 1:R_CW + 2], None, ALU.mult))
                for j in range(2, 31):
                    ch.wait_but_one()
                    ch.do(v.scalar_tensor_tensor(acc[j % 2], glu[:, k, j:j + TP], rt[:, k, R_CW + j:R_CW + j + 1],
                                                 acc[j % 2], ALU.mult, ALU.add))
                ch.wait()
                ch.do(v.tensor_tensor(acc[0], acc[0], acc[1], ALU.add))
                dve.wait_ge(prod_ok, k + 1)
                out = dc[:, k, TP:].rearrange("p (s t) -> p t s", s=NS)
                v.tensor_reduce(out, prod, AX, ALU.add).then_inc(prod_used, 1)
                dve.wait_ge(prod_used, k + 1)
                v.tensor_scalar(dc[:, k, TP:], dc[:, k, TP:], rt[:, k, R_CB:R_CB + 1], None, ALU.add).then_inc(dc_ok, 1)

            def lru_conv(k):
                m = k % GC
                n = place[("in", G_U + k // GC, k % GC)]
                dve.wait_ge(pair_act, sum(by_act[:n + 1]))
                dve.wait_ge(us_ok, KC + 1)
                ch.do(v.tensor_copy(u_s[:, k, :, W3:], seqs(u[:, k, W3 + TP:])))
                acc, acs = xc[:, m, 0:TP], seqs(xc[:, m, TP:])
                ch.link(v.tensor_scalar(acc, u[:, k, 0:TP], rt[:, k, R_LW:R_LW + 1], rt[:, k, R_LB:R_LB + 1],
                                        ALU.mult, ALU.add))
                ch.link(v.tensor_scalar(acs, u_s[:, k, :, 0:TS], rt[:, k, R_LW:R_LW + 1], rt[:, k, R_LB:R_LB + 1],
                                        ALU.mult, ALU.add))
                for j in range(1, 4):
                    w = rt[:, k, R_LW + j:R_LW + j + 1]
                    ch.do(v.scalar_tensor_tensor(acc, u[:, k, j:j + TP], w, acc, ALU.mult, ALU.add))
                    ins = v.scalar_tensor_tensor(acs, u_s[:, k, :, j:j + TS], w, acs, ALU.mult, ALU.add)
                    if j < 3:
                        ch.link(ins)
                ins.then_inc(xc_ok, 1)

            def lru(g):
                last = place[("i", g, GC - 1)]
                dve.wait_ge(pair_act, sum(by_act[:last + 1]))
                ch.do(v.tensor_tensor(ii, ii, xc, ALU.mult))
                dve.wait_ge(t_ok, g + 1)
                ch.link(v.tensor_scalar(rec, tt, 1.0, None, ALU.add))
                v.reciprocal(rec, rec).then_inc(t_copied, 1)
                dve.wait_ge(t_copied, g + 1)
                ch.link(v.tensor_copy(hst[:, 0, 0:GC], ii[:, :, 0]))
                dve.wait_ge(sqrt_ok, g + 1)
                ch.link(v.scalar_tensor_tensor(tt, tt, 2.0, rec, ALU.mult, ALU.mult))
                ch.link(v.tensor_tensor(ii, ii, tt, ALU.mult))
                ch.do(v.tensor_scalar(rec, rec, 2.0, -1.0, ALU.mult, ALU.add))
                ch.link(v.tensor_copy(ii[:, :, 0], hst[:, 0, 0:GC]))
                for m in range(GC):
                    ch.do(v.tensor_tensor_scan(xc[:, m, 0:TP], rec[:, m, 0:TP], ii[:, m, 0:TP], 0.0, ALU.mult, ALU.add))

                def step(x, s):
                    return x[:, :, TP:].rearrange("p m (s t) -> p m s t", s=NS)[:, :, :, s]

                prev = rt[:, g * GC:(g + 1) * GC, R_H0:R_H0 + NS]
                for s in range(TS):
                    ch.link(v.tensor_tensor(step(xc, s), step(rec, s), prev, ALU.mult))
                    ch.link(v.tensor_tensor(step(xc, s), step(xc, s), step(ii, s), ALU.add))
                    prev = step(xc, s)
                ch.do(v.tensor_copy(hlast[:, g * GC:(g + 1) * GC, :], xc[:, :, TP - 1:]))
                gate = place[("in", G_GATE + g, GC - 1)]
                dve.wait_ge(pair_act, sum(by_act[:gate + 1]))
                zz = z[:, g * GC:(g + 1) * GC, :]
                v.tensor_tensor(zz, zz, xc, ALU.mult).then_inc(z_ok, 1)

            def last_rows(i, n, bank_rows):
                dve.wait_ge(last_tr, i + 1)
                dst = (last_glu, last_u, last_h)[i]
                if i == 2:
                    dve.wait_ge(z_ok, 2)
                for h in range(2):
                    ins = v.tensor_copy(dst[0:n, h * 512:(h + 1) * 512], ps[0:n, 4 + h, :])
                ins.then_inc(last_sb, 1)

            dve.wait_ge(conv_new, 1)
            for k in range(KC):
                conformer(k)
            for k in range(GC):
                lru_conv(k)
            n = place[("mean", 0, 0)]
            dve.wait_ge(pair_act, sum(by_act[:n + 1]))
            v.tensor_tensor(dc, dc, ln_mean.unsqueeze(1).to_broadcast([P, KC, T]), ALU.subtract).then_inc(cent_ok, 1)
            last_rows(0, 62, 0)
            lru(0)
            n = place[("var", 0, 0)]
            dve.wait_ge(pair_act, sum(by_act[:n + 1]))
            ch.link(v.reciprocal(ln_rstd, ln_rstd))
            v.tensor_tensor(dc, dc, ln_rstd.unsqueeze(1).to_broadcast([P, KC, T]), ALU.mult).then_inc(ln_ok, 1)
            for k in range(GC, KC):
                if k == GC:
                    dve.wait_ge(z_ok, 1)
                lru_conv(k)
            last_rows(1, 35, 1)

            def gated(w, h, m):
                n = place[(w, h, m)]
                k = h * GC + m
                dve.wait_ge(pairs, n + 1)
                act_n = place[("in", (G_BC if w == "co" else G_BL) + h, m)]
                dve.wait_ge(pair_act, sum(by_act[:act_n + 1]))
                if w == "co":
                    if k == 0:
                        dve.wait_ge(last_tr, 2)
                    v.tensor_tensor(two(merged[:, k, :]), pair(n), two(bg[:, m, :]), ALU.mult).then_inc(pair_dve, 1)
                else:
                    v.tensor_tensor(two(bg[:, m, :]), pair(n), two(bg[:, m, :]), ALU.mult).then_inc(pair_dve, 1)
                    drained(dve, n)
                    v.tensor_tensor(merged[:, k, :], merged[:, k, :], bg[:, m, :], ALU.add).then_inc(merged_ok, 1)

            for w, h in (("co", 0), ("co", 1), ("lo", 0), ("lo", 1)):
                for m in range(GC):
                    gated(w, h, m)
                if (w, h) == ("co", 0):
                    lru(1)
                if (w, h) == ("lo", 0):
                    last_rows(2, 33, 2)

            dve.wait_ge(x1_in, 16 * NT)
            dve.wait_ge(bc_in, 16 * 10)
            def residual(t):
                n = TILES[t]
                for h in range(2):
                    j = 2 * t + h
                    dve.wait_ge(out_ps, j + 1)
                    tmp = yb[0:n, 0, h * 512:(h + 1) * 512]
                    v.tensor_tensor(tmp, ps[0:n, j % 4, :], gt1_bc[0:n, t // 4, h * 512:(h + 1) * 512], ALU.mult)\
                     .then_inc(x1_half, 1)
                    dve.wait_ge(x1_half, j + 1)
                    xh = x1[0:n, t, h * 512:(h + 1) * 512]
                    ins = v.tensor_tensor(xh, xh, tmp, ALU.add)
                    if h == 0:
                        ch.link(ins)
                ins.then_inc(x1_ok, 1)
                dve.wait_ge(x1_ok, t + 1)

            def hf_norm(t):
                n = TILES[t]
                dve.wait_ge(ssq_ok, NT + t + 1)
                v.tensor_scalar(ssq[0:n, t:t + 1], ssq[0:n, t:t + 1], 1.0 / D, RMS_EPS, ALU.mult, ALU.add)\
                 .then_inc(rms_ask, 1)
                dve.wait_ge(rms_sqrt, t + 2)
                ch.link(newton(n, t, t + 1))
                if t == 0:
                    dve.wait_ge(hrow_out, 32)
                if t >= 2:
                    dve.wait_ge(hf_store[t % 2], 16 * (t // 2))
                    dve.wait_ge(hft_tr, t - 1)
                v.scalar_tensor_tensor(hf[0:n, t % 2, :], x1[0:n, t, :], rstd[0:n, t:t + 1], g2_bc[0:n, t // 4, :],
                                       ALU.mult, ALU.mult).then_inc(hf_dve, 1)

            def hf_turn(t):
                n = TILES[t]
                dve.wait_ge(hft_tr, t + 1)
                if t >= 2:
                    dve.wait_ge(lg_ps, t - 1)
                v.tensor_copy(hft[:, t % 2, 0:4, 0:n],
                              ps[:, 4, :].rearrange("p (k c) -> p k c", k=4)[:, :, 0:n]).then_inc(hft_dve, 1)

            for t in range(NT):
                residual(t)
                if t == 0:
                    dve.wait_ge(bc_in, 16 * 10)
                    for j in range(2):
                        n = (P, TSAMP)[j]
                        ch.link(v.scalar_tensor_tensor(g2_bc[0:n, j, :], g2_bc[0:n, j, :], 1.0, gffn_bc[0:n, :],
                                                       ALU.add, ALU.mult))
                else:
                    hf_turn(t - 1)
                hf_norm(t)
            hf_turn(NT - 1)
            dve.wait_ge(hf_dve, NT)
            ch.link(v.memset(lg, 0.0))
            for t in range(NT):
                n = TILES[t]
                dve.wait_ge(lg_ps, NT)
                ch.do(v.tensor_tensor(lg[0:n, t, :], ps[0:n, 6, t * NE:(t + 1) * NE], br[0:n, :], ALU.add))
            ch.wait()

            def c16(x):
                return x.unsqueeze(2).to_broadcast([P, NT, NE])

            def row16(x):
                return x[:, :].unsqueeze(1).to_broadcast([P, NT, NE])

            r = [rs[:, j, :] for j in range(12)]
            ch.link(v.tensor_reduce(r[0], lg, AX, ALU.max))
            v.tensor_tensor(lg, lg, c16(r[0]), ALU.subtract).then_inc(exp_ask, 1)
            dve.wait_ge(exp_ok, 1)
            ch.link(v.tensor_reduce(r[0], lg, AX, ALU.add))
            ch.link(v.reciprocal(r[0], r[0]))
            ch.link(v.tensor_tensor(pr, lg, c16(r[0]), ALU.mult))
            quad = pr.rearrange("p t (g e) -> p t g e", e=EG)
            h1, l1, h2, l2, gs = (gsb[:, j] for j in range(5))
            ch.do(v.tensor_tensor(h1, quad[:, :, :, 0], quad[:, :, :, 1], ALU.max))
            ch.do(v.tensor_tensor(l1, quad[:, :, :, 0], quad[:, :, :, 1], ALU.min))
            ch.do(v.tensor_tensor(h2, quad[:, :, :, 2], quad[:, :, :, 3], ALU.max))
            ch.link(v.tensor_tensor(l2, quad[:, :, :, 2], quad[:, :, :, 3], ALU.min))
            ch.do(v.tensor_tensor(gs, h1, h2, ALU.max))
            ch.do(v.tensor_tensor(l1, l1, l2, ALU.max))
            ch.link(v.tensor_tensor(h1, h1, h2, ALU.min))
            ch.link(v.tensor_tensor(l1, l1, h1, ALU.max))
            ch.link(v.tensor_tensor(gs, gs, l1, ALU.add))
            ch.link(v.tensor_reduce(r[1], gs, AX, ALU.max))
            ch.link(v.tensor_tensor(h1, gs, r[1].unsqueeze(2).to_broadcast([P, NT, NG]), ALU.is_lt))
            ch.link(v.scalar_tensor_tensor(h1, h1, 100.0, iota_g[:, :].unsqueeze(1).to_broadcast([P, NT, NG]),
                                           ALU.mult, ALU.add))
            ch.link(v.tensor_reduce(r[2], h1, AX, ALU.min))
            ch.link(v.tensor_tensor(m16, row16(grp_e), c16(r[2]), ALU.is_equal))
            ch.link(v.tensor_tensor(r6, pr, m16, ALU.mult))
            ch.link(v.scalar_tensor_tensor(pr, m16, 1.0, r6, ALU.subtract, ALU.add))
            for best, idx, oh in ((r[3], r[4], oh1), (r[5], r[6], oh2)):
                ch.link(v.tensor_reduce(best, pr, AX, ALU.max))
                ch.link(v.tensor_tensor(r6, pr, c16(best), ALU.is_lt))
                ch.link(v.scalar_tensor_tensor(r6, r6, 100.0, row16(iota_e), ALU.mult, ALU.add))
                ch.link(v.tensor_reduce(idx, r6, AX, ALU.min))
                ch.link(v.tensor_tensor(oh, row16(iota_e), c16(idx), ALU.is_equal))
                ch.link(v.scalar_tensor_tensor(pr, oh, -10.0, pr, ALU.mult, ALU.add))
            ch.link(v.tensor_tensor(selb[:, :, :], oh1, oh2, ALU.add))
            v.tensor_tensor(selb[:, :, :], selb[:, :, :], c16(valid[:, :]), ALU.mult).then_inc(sel_ok, 1)
            ch.link(v.tensor_tensor(r[7], r[3], r[5], ALU.add))
            ch.link(v.reciprocal(r[7], r[7]))
            ch.do(v.tensor_tensor(w12[:, 0, :], r[3], r[7], ALU.mult))
            ch.do(v.tensor_tensor(w12[:, 1, :], r[5], r[7], ALU.mult))
            dve.wait_ge(rank_ps, 1)
            ch.do(v.tensor_copy(cnt[:, :], ps[:, 7, NT * NE:(NT + 1) * NE]))
            ch.link(v.tensor_copy(rank, ps[:, 7, 0:NT * NE].rearrange("p (t e) -> p t e", t=NT)))
            ch.link(v.tensor_tensor(key, rank, selb[:, :, :], ALU.mult))
            ch.link(v.tensor_scalar(r7, selb[:, :, :], 10000.0, -10000.0, ALU.mult, ALU.add))
            ch.link(v.tensor_tensor(key, key, r7, ALU.add))
            def row_masks(e, s):
                for t in range(NT):
                    ins = v.tensor_scalar(mb[:, s, t, :], slot_row[:, :], key[:, t, bass.ds(e, 1)], None, ALU.is_equal)
                ins.then_inc(mb_ok, 1)

            def row_index(e, s):
                dve.wait_ge(idx_ps, e + 1)
                v.tensor_copy(idx_f[:, s, :], ps[:, 7, 256 + 2 * s:258 + 2 * s]).then_inc(idx_cp, 1)
                dve.wait_ge(idx_cp, e + 1)
                v.scalar_tensor_tensor(idx_i[:, bass.ds(e, 1)], idx_f[:, s, 1:2], float(P), idx_f[:, s, 0:1],
                                       ALU.mult, ALU.add).then_inc(idx_ok, 1)

            row_masks(0, 0)
            for e in range(AHEAD):
                row_masks(e + 1, 1 - e % 2)
                row_index(e, e % 2)

            def xgt_half(e):
                dve.wait_ge(xgt_ps, e + 1)
                v.tensor_copy(xgt[:, 0:4, :], ps[:, 2, :].rearrange("p (k c) -> p k c", k=4)).then_inc(xgt_dve, 1)

            def hidden(e):
                dve.wait_ge(up_ps, e + 1)
                dve.wait_ge(silu_ok, e + 1)
                v.tensor_tensor(act_g, act_g, ps[:, 1, :], ALU.mult).then_inc(h_ok, 1)

            def y_half(e, s, stored=None):
                dve.wait_ge(y_ps, e + 1)
                if stored is not None:
                    dve.wait_ge(y_store[s], stored)
                v.tensor_copy(yb[:, s, 0:DE], ps[:, 5, :]).then_inc(y_dve, 1)

            def step(e, s, index_too=True, masks_too=True, y_before=True, stored=None, turn_next=True):
                hidden(e)
                if index_too:
                    row_index(e + AHEAD, 1 - s)
                if y_before:
                    y_half(e - 1, 1 - s, stored)
                if turn_next:
                    xgt_half(e + 1)
                if masks_too:
                    row_masks(e + AHEAD + 1, s)

            xgt_half(0)
            step(0, 0, y_before=False)
            step(1, 1)
            step(2, 0)
            for j in range(MORE):
                ch.do(v.tensor_scalar(ovf[:, :, j], cnt[:, :], float(CAP * (j + 1)), None, ALU.is_gt))
            ch.wait()
            flags = ovf[:, :, :].rearrange("p e j -> p (e j)")
            ch.link(v.memset(ovr[:, 0, :], 1.0))
            ch.link(v.tensor_tensor_scan(ovr[:, 1, :], ovr[:, 0, :], flags, 0.0, ALU.mult, ALU.add))
            ch.link(v.tensor_copy(ovt[:, MAX_OVER:MAX_OVER + 1], ovr[:, 1, NE * MORE - 1:NE * MORE]))
            ch.link(v.tensor_tensor(ovr[:, 0, :], ovr[:, 1, :], flags, ALU.mult))
            ch.link(v.tensor_scalar(ovr[:, 0, :], ovr[:, 0, :], -1.0, None, ALU.add))
            big, small = [P, MAX_OVER, NE * MORE], [P, MAX_OVER, NE]
            ch.link(v.tensor_tensor(ovm[:, 0], ovr[:, 0, :].unsqueeze(1).to_broadcast(big),
                                    ovk[:, :].unsqueeze(2).to_broadcast(big), ALU.is_equal))
            ch.link(v.tensor_tensor(ovm[:, 1], ovm[:, 0], ovi[:, :].unsqueeze(1).to_broadcast(big), ALU.mult))
            code, first, exp_ = (ovt_f[:, j, :] for j in range(3))
            ch.link(v.tensor_reduce(code, ovm[:, 1], AX, ALU.add))
            ch.link(v.tensor_tensor(ovm[:, 1, :, 0:NE], code.unsqueeze(2).to_broadcast(small),
                                    ov4[:, :].unsqueeze(1).to_broadcast(small), ALU.is_ge))
            ch.link(v.tensor_reduce(exp_, ovm[:, 1, :, 0:NE], AX, ALU.add))
            ch.link(v.tensor_scalar(exp_, exp_, -1.0, None, ALU.add))
            ch.link(v.scalar_tensor_tensor(first, exp_, -float(MORE), code, ALU.mult, ALU.add))
            ch.link(v.tensor_scalar(first, first, float(CAP), float(CAP), ALU.mult, ALU.add))
            v.tensor_copy(ovt[:, 0:MAX_OVER], exp_).then_inc(ov_ok, 1)
            start, step_ = ovr[:, 1, :].rearrange("p (e j) -> p e j", j=MORE), ovr[:, 2, :].rearrange("p (e j) -> p e j", j=MORE)
            ch.link(v.tensor_scalar(ovr[:, 1, :], ovr[:, 1, :], float(CAP), float(CAP * (NE - 1)), ALU.mult, ALU.add))
            for j in range(MORE):
                ch.do(v.tensor_scalar(start[:, :, j], start[:, :, j], -float(CAP * (j + 1)), None, ALU.add))
            ch.wait()
            ch.do(v.tensor_tensor(step_[:, :, 0], start[:, :, 0], base_e[:, :], ALU.subtract))
            for j in range(1, MORE):
                ch.do(v.tensor_tensor(step_[:, :, j], start[:, :, j], start[:, :, j - 1], ALU.subtract))
            ch.link(v.tensor_tensor(r6, rank, row16(base_e), ALU.add))
            for j in range(MORE):
                ch.link(v.tensor_scalar(r7, rank, float(CAP * (j + 1)), None, ALU.is_ge))
                ch.link(v.tensor_tensor(r7, r7, step_[:, :, j].unsqueeze(1).to_broadcast([P, NT, NE]), ALU.mult))
                ch.link(v.tensor_tensor(r6, r6, r7, ALU.add))
            for j, oh in enumerate((oh1, oh2)):
                ch.link(v.tensor_tensor(r7, oh, r6, ALU.mult))
                ch.link(v.tensor_reduce(r[8], r7, AX, ALU.add))
                v.tensor_copy(slot_i[:, j, :], r[8]).then_inc(slot_ok, 1)
                dve.wait_ge(slot_ok, j + 1)

            with dve.Fori(1, 5) as i:
                step(i * 2 + 1, 1, stored=i * 16)
                step(i * 2 + 2, 0, stored=i * 16)
            step(11, 1, stored=16 * 5)
            step(12, 0, masks_too=False, stored=16 * 5)
            step(13, 1, index_too=False, masks_too=False, stored=16 * 6)
            step(14, 0, index_too=False, masks_too=False, stored=16 * 6)
            step(15, 1, index_too=False, masks_too=False, stored=16 * 7, turn_next=False)
            y_half(NE - 1, 1, 16 * (NE // 2 - 1))

            dve.wait_ge(ov_ok, 1)
            n_over = dve.value_load(ovt[0:1, MAX_OVER:MAX_OVER + 1], min_val=0, max_val=MAX_OVER)
            with dve.If(n_over > 0):
                with dve.Fori(0, n_over) as k:
                    e = dve.value_load(ovt[0:1, bass.ds(k, 1)], min_val=0, max_val=NE - 1)
                    v.tensor_scalar(ovkey[:, :], key[:, :, bass.ds(e, 1)].rearrange("p t o -> p (t o)"),
                                    ovt_f[:, 1, bass.ds(k, 1)], None, ALU.subtract).then_inc(ov_key, 1)
                    dve.wait_ge(ov_key, k + 1)
                    for t in range(NT):
                        ins = v.tensor_scalar(mb[:, 0, t, :], slot_row[:, :], ovkey[:, t:t + 1], None, ALU.is_equal)
                    ins.then_inc(mb_ok, 1)
                    dve.wait_ge(ov_pe, k * 5 + 1)
                    v.tensor_copy(idx_f[:, 0, :], ps[:, 7, 0:2]).then_inc(idx_cp, 1)
                    dve.wait_ge(idx_cp, k + NE + 1)
                    v.scalar_tensor_tensor(idx_vf[:, :], idx_f[:, 0, 1:2], float(P), idx_f[:, 0, 0:1],
                                           ALU.mult, ALU.add).then_inc(ov_idx, 1)
                    dve.wait_ge(ov_pe, k * 5 + 2)
                    v.tensor_copy(xgt[:, :, :], ps[:, 2:4, :].rearrange("p b (k c) -> p (b k) c", k=4)).then_inc(ov_dve, 1)
                    dve.wait_ge(ov_pe, k * 5 + 3)
                    dve.wait_ge(ov_act, k + 1)
                    v.tensor_tensor(act_g, act_g, ps[:, 1, :], ALU.mult).then_inc(ov_dve, 1)
                    dve.wait_ge(ov_pe, k * 5 + 4)
                    v.tensor_copy(act_t, ps[:, 4, :].rearrange("p (k c) -> p k c", k=DE // P)).then_inc(ov_dve, 1)
                    dve.wait_ge(ov_pe, k * 5 + 5)
                    v.tensor_copy(yb[:, 0, :].rearrange("p (h n) -> p h n", h=2), ps[:, 5:7, :]).then_inc(ov_dve, 1)
            with dve.Else():
                dve.nop()

            def finish(t):
                n = TILES[t]
                dve.wait_ge(fin_act, t + 1)
                v.tensor_scalar(ssq[0:n, t:t + 1], ssq[0:n, t:t + 1], 1.0 / D, RMS_EPS, ALU.mult, ALU.add)\
                 .then_inc(rms_ask, 1)
                dve.wait_ge(rms_sqrt, NT + t + 2)
                ch.link(newton(n, t, t + 1))
                if t >= 2:
                    dve.wait_ge(y_out[t % 2], 16 * (t // 2))
                v.scalar_tensor_tensor(yo[0:n, t % 2, :], x1[0:n, t, :], rstd[0:n, t:t + 1], gfin_bc[0:n, :],
                                       ALU.mult, ALU.mult).then_inc(fin_ok, 1)

            for t in range(NT):
                n = TILES[t]
                y1, y2_, xr = ya[0:n, t % 2, :], yc[0:n, t % 2, :], x1[0:n, t, :]
                dve.wait_ge(y_in[t % 2], 32 * (t // 2 + 1))
                ch.link(v.tensor_scalar(y1, y1, w12[0:n, 0, t:t + 1], None, ALU.mult))
                ch.link(v.scalar_tensor_tensor(y1, y2_, w12[0:n, 1, t:t + 1], y1, ALU.mult, ALU.add))
                ch.link(v.tensor_tensor(y1, y1, gt2_bc[0:n, t // 4, :], ALU.mult))
                v.tensor_tensor(xr, xr, y1, ALU.add).then_inc(fin_dve, 1)
                if t:
                    finish(t - 1)
            finish(NT - 1)


_INS = ['x_prompt', 'x_sample', 'state_lru_h', 'state_lru_conv', 'state_conf_conv', 'c_prompt', 'c_sample',
        'w_ada', 'b_ada', 'g_mix', 'g_ffn', 'w_in', 'b_in', 'lru_conv_w', 'lru_conv_b', 'lru_wa', 'lru_ba',
        'lru_wx', 'lru_bx', 'lru_lambda', 'w_lru_o', 'conf_conv_w', 'conf_conv_b', 'conf_ln_g', 'conf_ln_b',
        'w_conf_o', 'w_out', 'w_router', 'b_router', 'w_gate', 'w_up', 'w_down', 'g_final']
_OUTS = [('yp', (1, 512, 1024)), ('ys', (8, 4, 1024)), ('hp', (1, 1, 1024)), ('lcp', (1, 1, 3, 1024)),
         ('ccp', (1, 1, 30, 1024)), ('hs', (1, 8, 1024)), ('lcs', (1, 8, 3, 1024)), ('ccs', (1, 8, 30, 1024))]


def kernel(**inputs):
    import numpy as _np
    import concourse.bacc as _bacc
    from concourse.bass_utils import run_bass_kernel_spmd as _run

    nc = _bacc.Bacc("TRN2", target_bir_lowering=False, num_devices=1)
    arrays, aps = {}, {}
    for name in _INS:
        x = _np.ascontiguousarray(inputs[name])
        arrays[f"in_{name}"] = x
        aps[name] = nc.dram_tensor(f"in_{name}", x.shape, mybir.dt.from_np(x.dtype), kind="ExternalInput").ap()
    for name, shape in _OUTS:
        aps[name] = nc.dram_tensor(f"out_{name}", shape, F32, kind="ExternalOutput").ap()
    build(nc, aps)
    r = _run(nc, [arrays], core_ids=[0])
    return tuple(r.results[0][f"out_{name}"] for name, _ in _OUTS)
```

```python
from contextlib import ExitStack

import concourse.bass as bass
from concourse import mybir

F32 = mybir.dt.float32
F32R = mybir.dt.float32r
BF16 = mybir.dt.bfloat16
I32 = mybir.dt.int32
ALU = mybir.AluOpType
ACT = mybir.ActivationFunctionType
AX = mybir.AxisListType.X

P = 128
D = 1024
KC = D // P
TP = 512
NS, TS = 8, 4
TSAMP = NS * TS
T = TP + TSAMP
HALF = T // 2
NSEQ = 1 + NS
TILES = [P, P, P, P, TSAMP]
NT = len(TILES)
GC = 4
GW = GC * P
CT = 32
W3, W30 = 3, 30
NE, NG, EG = 16, 4, 4
DE = D // 2
CAP = P
MORE = (T - 1) // P
AHEAD = 3
MAX_OVER = 2 * T * 4 // (4 * P + 1)
RMS_EPS, LN_EPS = 1e-6, 1e-5
assert MORE == 4

R_LCONV, R_H0, R_CW, R_LW = 0, 24, 32, 63
R_CB, R_LNG, R_LNB, R_BA, R_BX, R_LAM, R_GMIX, R_LB, R_BIN = 67, 68, 69, 70, 71, 72, 73, 74, 75
NVEC = 81
G_U, G_GATE, G_CA, G_CB, G_BL, G_BC = 0, 2, 4, 6, 8, 10


def weight_stream():
    s = [("in", g) for g in (G_CA, G_CB, G_CA + 1, G_CB + 1, G_U, G_U + 1, G_GATE, G_GATE + 1)]
    s += [("in", G_BC), ("co", 0), ("in", G_BC + 1), ("co", 1)]
    s += [("in", G_BL), ("lo", 0), ("in", G_BL + 1), ("lo", 1)]
    return [(kind, g, c) for kind, g in s for c in range(2)]


def build(nc, a):
    stream = weight_stream()
    split_no, split_at = {}, []
    for n, (kind, g, c) in enumerate(stream):
        if kind in ("in", "lo"):
            split_no[n] = len(split_at)
            split_at.append(n)
    HW = GW // 2
    PIECE = KC * HW
    with ExitStack() as ctx:
        def sb(name, shape, dt=F32):
            return ctx.enter_context(nc.sbuf_tensor(name, shape, dt))

        def sem(name):
            return ctx.enter_context(nc.semaphore(name))

        with ExitStack() as under:
            under.enter_context(nc.sbuf_tensor("raw_place", [P, 2 * PIECE], F32))
            w_hi = under.enter_context(nc.sbuf_tensor("w_hi", [P, 2, KC, HW], F32R))
            w_lo = under.enter_context(nc.sbuf_tensor("w_lo", [P, 2, KC, HW], F32R))
        with ExitStack() as under:
            under.enter_context(nc.sbuf_tensor("gate_up_place", [P, 4 * PIECE], F32))
            wd_hi = under.enter_context(nc.sbuf_tensor("wd_hi", [P, DE // P, D], F32R))
        ring_a = sb("ring_a", [P, 6 * PIECE])
        with ExitStack() as under:
            z_hi = under.enter_context(nc.sbuf_tensor("z_hi", [P, KC, T], F32R))
        with ExitStack() as under:
            under.enter_context(nc.sbuf_tensor("gate_up_place2", [P, 4 * PIECE], F32))
            wd_lo = under.enter_context(nc.sbuf_tensor("wd_lo", [P, DE // P, D], F32R))
        region_c = sb("region_c", [P, 13080])
        with ExitStack() as under:
            hm_hi = under.enter_context(nc.sbuf_tensor("hm_hi", [P, KC, T], F32R))
            z_lo = under.enter_context(nc.sbuf_tensor("z_lo", [P, KC, T], F32R))
        region_b = sb("region_b", [P, 12288])
        with ExitStack() as under:
            hm_lo = under.enter_context(nc.sbuf_tensor("hm_lo", [P, KC, T], F32R))
        with ExitStack() as under:
            under.enter_context(nc.sbuf_tensor("xg_place", [P, 3 * D + DE], F32))
            act_hi = under.enter_context(nc.sbuf_tensor("act_hi", [P, DE // P, P], F32R))
            under.enter_context(nc.sbuf_tensor("yb_place", [P, 4 * D], F32))
            act_lo = under.enter_context(nc.sbuf_tensor("act_lo", [P, DE // P, P], F32R))
        region_d = sb("region_d", [P, 8704])
        region_e = sb("region_e", [P, 2176])

        def carve(region, at, dims):
            n = 1
            for d in dims:
                n *= d
            v = region[:, at:at + n]
            if len(dims) == 2:
                return v.rearrange("p (a b) -> p a b", a=dims[0])
            if len(dims) == 3:
                return v.rearrange("p (a b c) -> p a b c", a=dims[0], b=dims[1])
            return v

        raw = [carve(ring_a, s * PIECE, (KC, HW)) for s in range(2)]
        ada_w = [carve(ring_a, 2 * PIECE, (KC, GW)), carve(ring_a, 4 * PIECE, (KC, GW)),
                 carve(region_c, 2 * KC * T, (KC, GW)), carve(ring_a, 2 * PIECE, (KC, GW))]
        ada_h = [carve(region_c, 2 * KC * T + c * PIECE, (KC // 2, GW)) for c in range(2)]
        wo = [carve(region_c, KC * T, (KC, GW)), carve(ring_a, 0, (KC, GW))]
        xt = carve(region_c, 0, (NT, D))
        mod1 = carve(region_c, 5120, (4 * GW,))
        mod2 = carve(region_c, KC * T, (8 * GW,))
        dc = carve(region_c, 0, (KC, T))
        z = carve(region_c, KC * T, (KC, T))
        u = carve(region_c, 2 * KC * T, (KC, W3 + T))
        merged = carve(region_c, 2 * KC * T, (KC, T))
        hm = carve(region_b, 4352, (KC, T))
        glu = carve(region_b, 4352, (KC, W30 + T))
        glu_s = region_b[:, 8944:8944 + KC * NS * (W30 + TS)].rearrange(
            "p (k s t) -> p k s t", k=KC, s=NS)
        sg = carve(region_b, 11120, (2, T))
        ln_mean = carve(region_d, 6528, (T,))
        ln_rstd = carve(region_d, 6528 + T, (T,))
        ln_sq = carve(region_d, 6528 + 2 * T, (2, T))
        tt = carve(region_b, 4352, (GC, T))
        ii = carve(region_b, 4352 + GC * T, (GC, T))
        rec = carve(region_b, 4352 + 2 * GC * T, (GC, T))
        x1 = carve(region_b, 4352, (NT, D))
        gt1_bc = carve(region_b, 0, (2, D))
        g2_bc = carve(region_b, 2 * D, (2, D))
        sh2_bc = carve(region_b, 9472, (2, D))
        last_glu = carve(region_b, 10880, (D,))
        vec = carve(region_d, 0, (D,))
        sconf = carve(region_d, 6 * D, (2, D))
        crow = carve(region_d, 3 * D, (D,))
        xc = carve(region_d, 4352, (GC, T))
        last_u = carve(region_d, 7616, (D,))
        hf = carve(region_d, 0, (2, D))
        hft = carve(region_d, 2 * D, (2, KC, P))
        xg = carve(region_d, 0, (2, D))
        xgt = carve(region_d, 2 * D, (KC, P))
        act_g = carve(region_d, 3 * D, (DE,))
        act_t = carve(region_d, 3 * D + DE, (DE // P, P))
        yb = carve(region_d, 4 * D, (2, D))
        gt2_bc = carve(region_d, 6 * D, (2, D))
        last_h = carve(region_d, 4352, (D,))
        prod = carve(region_e, 0, (TS, NS, 31))
        odd = [region_e[:, 1024:1024 + TP] if k % 2 == 0 or k == KC - 1 else dc[:, KC - 1, 0:TP] for k in range(KC)]
        bg = [carve(region_e, m * T, (T,)) for m in range(GC - 1)] + [carve(region_d, 6528, (T,))]
        u_s = region_e[:, 1728:2176].rearrange("p (k s t) -> p k s t", k=KC, s=NS)
        gffn_bc = carve(region_e, 0, (D,))
        gfin_bc = carve(region_e, D, (D,))
        ya = carve(ring_a, 0, (NT, D))
        yc = carve(ring_a, NT * D, (NT, D))
        yo = carve(region_c, 0, (2, D))
        junk = carve(region_c, 2 * D, (D,))
        wd_raw = [carve(region_b, 9472, (D,)), carve(region_b, 9472 + D, (D,)),
                  carve(region_b, NT * P, (D,)), carve(region_e, 0, (D,))]
        regs = (ring_a, region_c)
        wg = [carve(r, 0, (KC, DE)) for r in regs]
        wu = [carve(r, 4096, (KC, DE)) for r in regs]
        wd = [carve(r, 8192, (DE // P, D)) for r in regs]

        ident = sb("ident", [P, P])
        ones = sb("ones", [P, P])
        tri = sb("tri", [P, P], BF16)
        ones_b = sb("ones_b", [P, P], BF16)
        rt = sb("rt", [P, KC, NVEC])
        sct = sb("sct", [P, KC, CT])
        sel = sb("sel", [P, CT])
        ada_tmp = region_d[:, 5 * D:6 * D].rearrange("p (s n) -> p s n", s=2)
        gate_w = [sb("wa_bd", [P, KC, P]), sb("wx_bd", [P, KC, P])]
        hlast = sb("hlast", [P, KC, 1 + TSAMP])
        modt = sb("modt", [P, 2 * KC, NSEQ])
        amod = sb("amod", [P, KC, NSEQ])
        sp4 = sb("sp4", [P, KC])
        spt = sb("spt", [P, 4, KC])
        ssq = sb("ssq", [P, NT])
        rstd = sb("rstd", [P, NT])
        nt1 = sb("nt1", [P, NT])
        eps_ln = sb("eps_ln", [P, 1])
        hst = sb("hst", [P, 2, GC * NS])
        iota_e = sb("iota_e", [P, NE])
        grp_e = sb("grp_e", [P, NE])
        iota_g = sb("iota_g", [P, NG])
        base_e = sb("base_e", [P, NE])
        slot_row = sb("slot_row", [P, P], BF16)
        tokid = sb("tokid", [P, NT, 2], BF16)
        valid = sb("valid", [P, NT])
        wr = sb("wr", [P, KC, NE])
        br = sb("br", [P, NE])
        zero_row = region_e[:, 0:D]
        iota_tmp = region_d[:, 8192:8192 + P].bitcast(I32)

        ps = ctx.enter_context(nc.psum_tensor("ps", [P, 8, 512], F32))

        mod_scr = nc.dram_tensor("mod_scr", (NSEQ, 6 * D), F32, kind="Internal").ap()
        hf_scr = nc.dram_tensor("hf_scr", (T, D), F32, kind="Internal").ap()
        y_scr = nc.dram_tensor("y_scr", ((NE + MAX_OVER) * CAP, D), F32, kind="Internal").ap()
        rb = region_b[:, 2 * D:2 * D + 8 * NT * NE].rearrange("p (j t e) -> p j t e", j=8, t=NT)
        lg, pr, m16, oh1, oh2, key, r6, r7 = (rb[:, j] for j in range(8))
        rank = lg
        rs = sb("rs", [P, 12, NT])
        gsb = region_b[:, 2 * D + 640:2 * D + 740].rearrange("p (j t g) -> p j t g", j=5, t=NT)
        sel_b = region_b[:, 2 * D + 820:2 * D + 860].bitcast(BF16).rearrange("p (t e) -> p t e", t=NT)
        selb = region_b[:, 2 * D + 740:2 * D + 820].rearrange("p (t e) -> p t e", t=NT)
        w12 = sb("w12", [P, 2, NT])
        slot_i = sb("slot_i", [P, 2, NT], I32)
        mb = region_b[:, 0:NT * P].bitcast(BF16).rearrange("p (s t r) -> p s t r", s=2, t=NT)
        idx_f = sb("idx_f", [P, 2, 2])
        idx_i = sb("idx_i", [P, NE], I32)
        idx_vf = sb("idx_vf", [P, 1])
        idx_vg = sb("idx_vg", [P, 1])
        idx_ov = sb("idx_ov", [P, 1], I32)
        cnt = sb("cnt", [P, NE])
        ovf = region_b[:, 3 * D:3 * D + NE * MORE].rearrange("p (e j) -> p e j", j=MORE)
        ovr = region_b[:, 3 * D + 64:3 * D + 64 + 3 * NE * MORE].rearrange("p (a c) -> p a c", a=3)
        ovi = sb("ovi", [P, NE * MORE])
        ovm = [x.rearrange("p (k c) -> p k c", k=MAX_OVER) for x in
               (region_b[:, 11520:11520 + MAX_OVER * NE * MORE], region_c[:, 12288:12288 + MAX_OVER * NE * MORE])]
        ovk = sb("ovk", [P, MAX_OVER])
        ovt_f = sb("ovt_f", [P, 3, MAX_OVER])
        ovt = sb("ovt", [P, 1 + MAX_OVER], I32)
        ov4 = sb("ov4", [P, NE])
        ovkey = sb("ovkey", [P, NT])

        raw_full = [sem(f"raw_full{s}") for s in range(2)]
        w_hi_ok = sem("w_hi_ok")
        w_lo_ok = sem("w_lo_ok")
        ada_in = [sem(f"ada_in{j}") for j in range(4)]
        ada_half = [sem(f"ada_half{c}") for c in range(2)]
        ada_read = sem("ada_read")
        wo_full = [sem(f"wo_full{h}") for h in range(2)]
        z_hi_ok = sem("z_hi_ok")
        z_lo_ok = sem("z_lo_ok")
        hm_hi_ok = sem("hm_hi_ok")
        hm_lo_ok = sem("hm_lo_ok")
        ada_ps = sem("ada_ps")
        ada_cp = sem("ada_cp")
        ada_sum = sem("ada_sum")
        sct_zero = sem("sct_zero")
        sel_mat = sem("sel_mat")
        crow_in = sem("crow_in")
        vec_in = sem("vec_in")
        sconf_in = sem("sconf_in")
        bd_in = sem("bd_in")
        bd_zero = sem("bd_zero")
        x_in = sem("x_in")
        bias_in = sem("bias_in")
        bias2_in = sem("bias2_in")
        ada_act = sem("ada_act")
        ssq_clear = sem("ssq_clear")
        x1_half = sem("x1_half")
        idx_cp = sem("idx_cp")
        ov_key = sem("ov_key")
        slot_ok = sem("slot_ok")
        y_clear = sem("y_clear")
        zero_ok = sem("zero_ok")
        consts = sem("consts")
        pool_step = sem("pool_step")
        dve_step = sem("dve_step")
        act_step = sem("act_step")
        csilu = sem("csilu")
        c_tr = sem("c_tr")
        sct_ok = sem("sct_ok")
        vec_tr = sem("vec_tr")
        rt_ok = sem("rt_ok")
        sconf_tr = sem("sconf_tr")
        sconf_ok = sem("sconf_ok")
        ada_ok = sem("ada_ok")
        modt_tr = sem("modt_tr")
        modt_ok = sem("modt_ok")
        xn_ok = sem("xn_ok")
        ssq_ok = sem("ssq_ok")
        rms_ask = sem("rms_ask")
        rms_sqrt = sem("rms_sqrt")
        rstd_ok = sem("rstd_ok")
        x_tr = sem("x_tr")
        hm_dve = sem("hm_dve")
        hm_act = sem("hm_act")
        pairs = sem("pairs")
        pair_act = sem("pair_act")
        pair_dve = sem("pair_dve")
        conv_new = sem("conv_new")
        prod_ok = sem("prod_ok")
        prod_used = sem("prod_used")
        conv_ok = sem("conv_ok")
        tap_ok = sem("tap_ok")
        dc_ok = sem("dc_ok")
        us_ok = sem("us_ok")
        xc_ok = sem("xc_ok")
        sp_exp = sem("sp_exp")
        sp_ask = sem("sp_ask")
        sp_ok = sem("sp_ok")
        t_ok = sem("t_ok")
        t_copied = sem("t_copied")
        sqrt_ok = sem("sqrt_ok")
        z_ok = sem("z_ok")
        last_tr = sem("last_tr")
        last_sb = sem("last_sb")
        cent_ok = sem("cent_ok")
        sq_ok = sem("sq_ok")
        sq_used = sem("sq_used")
        ln_ok = sem("ln_ok")
        sn_ok = sem("sn_ok")
        merged_ok = sem("merged_ok")
        mod_store = sem("mod_store")
        bc_in = sem("bc_in")
        bc2_in = sem("bc2_in")
        x1_in = sem("x1_in")
        out_ps = sem("out_ps")
        x1_ok = sem("x1_ok")
        hf_dve = sem("hf_dve")
        hf_sum = sem("hf_sum")
        hf_store = [sem(f"hf_store{s}") for s in range(2)]
        hft_tr = sem("hft_tr")
        hft_act = sem("hft_act")
        hft_dve = sem("hft_dve")
        lg_ps = sem("lg_ps")
        exp_ask = sem("exp_ask")
        exp_ok = sem("exp_ok")
        sel_ok = sem("sel_ok")
        rank_ps = sem("rank_ps")
        mb_ok = sem("mb_ok")
        idx_ps = sem("idx_ps")
        idx_ok = sem("idx_ok")
        ov_ok = sem("ov_ok")
        wg_full = [sem(f"wg_full{s}") for s in range(2)]
        wu_full = [sem(f"wu_full{s}") for s in range(2)]
        wd_full = [sem(f"wd_full{q}") for q in range(4)]
        wd_hi_ok = sem("wd_hi_ok")
        wd_lo_ok = sem("wd_lo_ok")
        ht_lo_ok = sem("ht_lo_ok")
        xg_full = [sem(f"xg_full{s}") for s in range(2)]
        xgt_ps = sem("xgt_ps")
        xgt_act = sem("xgt_act")
        xgt_dve = sem("xgt_dve")
        gate_ps = sem("gate_ps")
        up_ps = sem("up_ps")
        silu_ok = sem("silu_ok")
        h_ok = sem("h_ok")
        ht_ps = sem("ht_ps")
        ht_ok = sem("ht_ok")
        y_ps = sem("y_ps")
        y_act = sem("y_act")
        y_dve = sem("y_dve")
        y_store = [sem(f"y_store{s}") for s in range(2)]
        ov_w = sem("ov_w")
        ov_idx = sem("ov_idx")
        ov_x = sem("ov_x")
        ov_pe = sem("ov_pe")
        ov_dve = sem("ov_dve")
        ov_act = sem("ov_act")
        ov_st = sem("ov_st")
        y_in = [sem(f"y_in{t}") for t in range(NT)]
        y_scaled = sem("y_scaled")
        fin_dve = sem("fin_dve")
        fin_act = sem("fin_act")
        fin_ok = sem("fin_ok")
        outs_done = sem("outs_done")
        last_out = sem("last_out")
        hrow_out = sem("hrow_out")
        y_out = [sem(f"y_out{s}") for s in range(2)]

        def cols(w, g):
            return w[0].rearrange("(k p) n -> p k n", p=P)[:, :, g * GW:(g + 1) * GW]

        source = {"in": a["w_in"], "co": a["w_conf_o"], "lo": a["w_lru_o"]}
        piece_of = {key_n: n for n, key_n in enumerate(stream)}
        x_p, x_s = a["x_prompt"][0], a["x_sample"].rearrange("s t d -> (s t) d")

        def x_rows(t):
            return x_s if t == NT - 1 else x_p[t * P:(t + 1) * P, :]

        work = []
        for g in (G_CA, G_CB, G_CA + 1, G_CB + 1, G_U, G_U + 1, G_GATE, G_GATE + 1):
            work += [("in", g, m) for m in range(GC)]
            if g == G_GATE + 1:
                work += [("mean", 0, 0)]
                work += [(x, 0, m) for m in range(GC) for x in ("r", "i")]
                work += [("var", 0, 0)]
        for h, w in ((0, "co"), (1, "co"), (0, "lo"), (1, "lo")):
            g = (G_BC if w == "co" else G_BL) + h
            for m in range(GC):
                work += [("in", g, m)]
                if (h, w, m) == (1, "co", 1):
                    work += [(x, 1, c) for c in range(GC) for x in ("r", "i")]
            work += [(w, h, m) for m in range(GC)]
        by_act = [w[0] not in ("co", "lo") for w in work]
        place = {w: n for n, w in enumerate(work)}
        ada_after = {2 * i + 1: 4 + i for i in range(8)}

        def last_use(n):
            kind, g, c = stream[n]
            return place[(kind, g, 2 * c + 1)]

        split_after = {}
        for q in range(2, len(split_at)):
            at = max([last_use(split_at[q - 2])] + [last_use(m) for m in range(split_at[q] - 1) if m not in split_no])
            split_after.setdefault(at, []).append(q)

        def pair(n):
            return ps[:, 2 * (n % 2):2 * (n % 2) + 2, 0:HALF]

        def drained(eng, n):
            if n < 0:
                return
            if by_act[n]:
                eng.wait_ge(pair_act, sum(by_act[:n + 1]))
            else:
                eng.wait_ge(pair_dve, n + 1 - sum(by_act[:n + 1]))

        def two(v):
            return v.rearrange("p (h t) -> p h t", h=2)

        def seqs(v):
            return v.rearrange("p (s t) -> p s t", s=NS)

        class Chain:

            def __init__(self, eng, s):
                self.eng, self.s, self.n = eng, s, 0

            def do(self, ins):
                ins.then_inc(self.s, 1)
                self.n += 1
                return ins

            def wait(self):
                self.eng.wait_ge(self.s, self.n)

            def wait_but_one(self):
                self.eng.wait_ge(self.s, self.n - 1)

            def link(self, ins):
                self.do(ins)
                self.wait()

        LAST_DMAS = (1 + NS) + (1 + NS)

        block = ctx.enter_context(nc.Block())

        @block.sync
        def _(sp):
            sp.dma_start(crow[0:1, :], a["c_prompt"]).then_inc(crow_in, 16)
            sp.dma_start(crow[1:NSEQ, :], a["c_sample"]).then_inc(crow_in, 16)

            def load(n):
                kind, g, c = stream[n]
                if n >= 2:
                    if n - 2 in split_no:
                        sp.wait_ge(w_lo_ok, split_no[n - 2] + 1)
                    else:
                        sp.wait_ge(pairs, last_use(n - 2) + 1)
                sp.dma_start(raw[n % 2], source[kind][0].rearrange("(k p) n -> p k n", p=P)
                             [:, :, g * GW + c * HW:g * GW + (c + 1) * HW]).then_inc(raw_full[n % 2], 16)

            def load_ada(j):
                sp.dma_start(ada_w[j], cols(a["w_ada"], j)).then_inc(ada_in[j], 16)

            def load_ada_halves(j):
                for c in range(2):
                    if j == 4:
                        sp.wait_ge(ada_ps, 3)
                    else:
                        sp.wait_ge(*((ada_read, j - 4) if c == 0 else (ada_ps, j)))
                    sp.dma_start(ada_h[c], cols(a["w_ada"], j)[:, c * KC // 2:(c + 1) * KC // 2, :])\
                      .then_inc(ada_half[c], 16)

            load_ada(0)
            sp.dma_start(mod1[0:NSEQ, :], a["b_ada"][:, 0:4 * GW].to_broadcast([NSEQ, 4 * GW]))\
              .then_inc(bias_in, 16)
            rows = [(R_LCONV, a["state_lru_conv"][0].rearrange("s j d -> (s j) d")),
                    (R_H0, a["state_lru_h"][0]), (R_CW, a["conf_conv_w"][0]), (R_LW, a["lru_conv_w"][0]),
                    (R_CB, a["conf_conv_b"]), (R_LNG, a["conf_ln_g"]), (R_LNB, a["conf_ln_b"]),
                    (R_BA, a["lru_ba"]), (R_BX, a["lru_bx"]), (R_LAM, a["lru_lambda"]),
                    (R_GMIX, a["g_mix"]), (R_LB, a["lru_conv_b"]),
                    (R_BIN, a["b_in"][0].rearrange("(r d) -> r d", d=D))]
            for r, src in rows:
                sp.dma_start(vec[r:r + src.shape[0], :], src).then_inc(vec_in, 16)
            load_ada(1)
            for t in range(NT):
                sp.dma_start(xt[0:TILES[t], t, :], x_rows(t)).then_inc(x_in, 16)
            load_ada(2)
            sp.wait_ge(ada_ps, 1)
            load_ada(3)
            for h in range(2):
                sp.dma_start(sconf[0:120, h, :], a["state_conf_conv"][0, 4 * h:4 * h + 4]
                             .rearrange("s j d -> (s j) d")).then_inc(sconf_in, 16)
            load(0)
            load(1)
            load_ada_halves(4)
            sp.wait_ge(bd_zero, 2)
            for w, src in zip(gate_w, (a["lru_wa"], a["lru_wx"])):
                for b in range(2):
                    sp.dma_start(w[64 * b:64 * b + 64, :, 64 * b:64 * b + 64],
                                 src[0].rearrange("(c b) i j -> b i c j", b=2)[b]).then_inc(bd_in, 16)
            sp.dma_start(wr[:, :, :], a["w_router"].rearrange("(k p) n -> p k n", p=P)).then_inc(bd_in, 16)
            sp.dma_start(br[:, :], a["b_router"].rearrange("(o n) -> o n", o=1).to_broadcast([P, NE]))\
              .then_inc(bd_in, 16)
            sp.dma_start(a["ccs"][0, :, 0:W30 - TS, :], a["state_conf_conv"][0, :, TS:W30, :])\
              .then_inc(outs_done, 16)
            sp.wait_ge(zero_ok, 1)
            sp.dma_start(y_scr[NE * CAP:, :].rearrange("(t p) d -> p t d", p=CAP),
                         zero_row[0:CAP, :].unsqueeze(1).to_broadcast([CAP, MAX_OVER, D])).then_inc(y_clear, 16)
            sp.wait_ge(x_tr, NT)
            sp.wait_ge(modt_tr, 1)
            sp.dma_start(mod2[0:1, :], a["b_ada"][:, 4 * GW:]).then_inc(bias2_in, 16)
            load(2)
            for j in range(5, 12):
                load_ada_halves(j)
                load(j - 2)
            sp.wait_ge(ada_act, 8)
            sp.dma_start(mod_scr[:, 2 * D:], mod2[0:NSEQ, :]).then_inc(mod_store, 16)
            rows_at = piece_of[("in", G_BL, 1)] + 1
            for n in range(10, rows_at):
                load(n)
            sp.wait_ge(last_sb, 1)
            sp.dma_start(a["ccp"][0, 0], last_glu[0:W30, :]).then_inc(last_out, 16)
            for s in range(NS):
                sp.dma_start(a["ccs"][0, s, W30 - TS:, :], last_glu[W30 + TS * s:W30 + TS * (s + 1), :])\
                  .then_inc(last_out, 16)
            sp.wait_ge(last_sb, 2)
            sp.dma_start(a["lcp"][0, 0], last_u[0:W3, :]).then_inc(last_out, 16)
            for s in range(NS):
                r = W3 + TS * (s + 1)
                sp.dma_start(a["lcs"][0, s], last_u[r - W3:r, :]).then_inc(last_out, 16)
            for n in range(rows_at, len(stream)):
                load(n)
            sp.wait_ge(mod_store, 16)

            def spread(dst, j, done):
                src = mod_scr[:, j * D:(j + 1) * D]
                sp.dma_start(dst[:, 0, :], src[0:1, :].to_broadcast([P, D])).then_inc(done, 16)
                sp.dma_start(dst[0:TSAMP, 1, :], src[1:NSEQ, :].unsqueeze(1).to_broadcast([NS, TS, D]))\
                  .then_inc(done, 16)

            sp.wait_ge(last_out, 16 * LAST_DMAS)
            sp.wait_ge(z_ok, 2)
            spread(sh2_bc, 3, bc_in)
            sp.wait_ge(z_lo_ok, 2)
            sp.dma_start(wo[0], cols(a["w_out"], 0)).then_inc(wo_full[0], 16)
            sp.wait_ge(w_lo_ok, len(split_at))
            sp.dma_start(wo[1], cols(a["w_out"], 1)).then_inc(wo_full[1], 16)
            sp.wait_ge(pairs, place[("in", G_BL + 1, GC - 1)] + 1)
            spread(gt1_bc, 2, bc_in)
            spread(g2_bc, 4, bc_in)
            sp.wait_ge(last_sb, 3)
            sp.dma_start(a["hp"][0], last_h[0:1, :]).then_inc(hrow_out, 16)
            sp.dma_start(a["hs"][0], last_h[TS:TS * NS + 1:TS, :]).then_inc(hrow_out, 16)
            sp.wait_ge(pairs, len(work))
            for t in range(NT):
                sp.dma_start(x1[0:TILES[t], t, :], x_rows(t)).then_inc(x1_in, 16)
            sp.wait_ge(merged_ok, KC)
            spread(gt2_bc, 5, bc2_in)
            sp.dma_start(gffn_bc, a["g_ffn"].to_broadcast([P, D])).then_inc(bc2_in, 16)
            sp.dma_start(gfin_bc, a["g_final"].rearrange("(o n) -> o n", o=1).to_broadcast([P, D]))\
              .then_inc(bc2_in, 16)

            QD = DE // P

            def load_half(w, src, full, e, s):
                sp.dma_start(w[s], src[0, bass.ds(e, 1)].rearrange("e (k p) n -> p (e k) n", p=P)).then_inc(full[s], 16)

            def load_quarter(e, q):
                sp.dma_start(wd_raw[q], a["w_down"][0, bass.ds(e, 1)].rearrange("e (k p) n -> p (e k) n", p=P)[:, q, :])\
                  .then_inc(wd_full[q], 16)

            def refill(e, s, gate_up_too=True):
                if gate_up_too:
                    sp.wait_ge(gate_ps, e + 1)
                    load_half(wg, a["w_gate"], wg_full, e + 2, s)
                    sp.wait_ge(up_ps, e + 1)
                    load_half(wu, a["w_up"], wu_full, e + 2, s)
                for q in range(QD):
                    sp.wait_ge(wd_lo_ok, e * QD + q + 1)
                    load_quarter(e + 1, q)

            sp.dma_start(wu[0], a["w_up"][0, 0].rearrange("(k p) n -> p k n", p=P)).then_inc(wu_full[0], 16)
            sp.wait_ge(out_ps, 2 * NT)
            sp.dma_start(wg[0], a["w_gate"][0, 0].rearrange("(k p) n -> p k n", p=P)).then_inc(wg_full[0], 16)
            sp.wait_ge(hf_store[0], 16 * 3)
            sp.wait_ge(hf_store[1], 16 * 2)
            for q in range(QD):
                load_quarter(0, q)
            sp.dma_start(wg[1], a["w_gate"][0, 1].rearrange("(k p) n -> p k n", p=P)).then_inc(wg_full[1], 16)
            sp.wait_ge(xg_full[0], 16)
            sp.dma_start(wu[1], a["w_up"][0, 1].rearrange("(k p) n -> p k n", p=P)).then_inc(wu_full[1], 16)
            with sp.Fori(0, NE // 2 - 1) as i:
                refill(i * 2, 0)
                refill(i * 2 + 1, 1)
            refill(NE - 2, 0, gate_up_too=False)
            sp.wait_ge(y_dve, NE)
            sp.wait_ge(y_ps, NE)
            sp.wait_ge(ov_ok, 1)
            n_over = sp.value_load(ovt[0:1, MAX_OVER:MAX_OVER + 1], min_val=0, max_val=MAX_OVER)
            with sp.If(n_over > 0):
                with sp.Fori(0, n_over) as k:
                    e = sp.value_load(ovt[0:1, bass.ds(k, 1)], min_val=0, max_val=NE - 1)
                    sp.wait_ge(ov_key, k + 1)
                    for w, src in ((wg, a["w_gate"]), (wu, a["w_up"]), (wd, a["w_down"])):
                        sp.dma_start(w[0], src[0, bass.ds(e, 1)].rearrange("e (k p) n -> p (e k) n", p=P))\
                          .then_inc(ov_w, 16)
            with sp.Else():
                sp.nop()
            for t in range(NT):
                sp.wait_ge(fin_ok, t + 1)
                dst = a["yp"][0, t * P:(t + 1) * P, :] if t < NT - 1 else a["ys"].rearrange("s t d -> (s t) d")
                sp.dma_start(dst, yo[0:TILES[t], t % 2, :]).then_inc(y_out[t % 2], 16)
            sp.wait_ge(y_out[0], 16 * 3)
            sp.wait_ge(y_out[1], 16 * 2)
            sp.wait_ge(outs_done, 16)
            sp.wait_ge(last_out, 16 * LAST_DMAS)
            sp.wait_ge(hrow_out, 32)

        @block.gpsimd
        def _(pool):
            g = nc.gpsimd
            ch = Chain(pool, pool_step)
            ch.do(g.memset(ident[:, :], 0.0))
            ch.do(g.memset(tri[:, :], 0.0))
            ch.wait()
            g.affine_select(out=ident[:, :], in_=ident[:, :], compare_op=ALU.not_equal, fill=1.0,
                            base=0, pattern=[[-1, P]], channel_multiplier=1).then_inc(consts, 1)
            g.affine_select(out=tri[:, :], in_=tri[:, :], compare_op=ALU.is_ge, fill=1.0,
                            base=0, pattern=[[-1, P]], channel_multiplier=1).then_inc(consts, 1)
            g.memset(ones_b[:, :], 1.0)
            g.memset(ones[:, :], 1.0).then_inc(consts, 1)
            g.memset(sct[:, :, :], 0.0).then_inc(sct_zero, 1)
            for w in gate_w:
                g.memset(w[:, :, :], 0.0).then_inc(bd_zero, 1)

            g.memset(zero_row, 0.0).then_inc(zero_ok, 1)

            def table(dst, pattern, n, cm=0, base=0):
                r = dst.shape[0]
                ch.link(g.iota(iota_tmp[0:r, 0:n], pattern=pattern, base=base, channel_multiplier=cm))
                ch.link(g.tensor_copy(dst, iota_tmp[0:r, 0:n]))

            table(iota_e[:, :], [[1, NE]], NE)
            table(grp_e[:, :], [[1, NG], [0, EG]], NE)
            table(iota_g[:, :], [[1, NG]], NG)
            table(base_e[:, :], [[CAP, NE]], NE)
            table(slot_row[:, :], [[1, P]], P)
            table(tokid[:, :, 0], [[0, NT]], NT, cm=1)
            table(tokid[:, :, 1], [[1, NT]], NT)
            table(ovi[:, :], [[1, NE * MORE]], NE * MORE)
            table(ovk[:, :], [[1, MAX_OVER]], MAX_OVER)
            table(ov4[:, :], [[MORE, NE]], NE)
            ch.link(g.memset(valid[:, :], 0.0))
            ch.link(g.memset(valid[:, 0:NT - 1], 1.0))
            ch.link(g.memset(valid[0:TSAMP, NT - 1:NT], 1.0))
            g.memset(eps_ln[:, :], LN_EPS).then_inc(consts, 1)
            pool.wait_ge(rt_ok, 1)
            for k in range(KC):
                g.tensor_copy(u_s[:, k, :, 0:W3], rt[:, k, R_LCONV:R_LCONV + NS * W3]
                              .rearrange("p (s j) -> p s j", j=W3)).then_inc(us_ok, 1)
            def gate_glu(k):
                n = place[("in", G_CB + k // GC, k % GC)]
                pool.wait_ge(pair_act, sum(by_act[:n + 1]))
                g.tensor_tensor(glu[:, k, W30:], glu[:, k, W30:], sg[:, k % 2, :], ALU.mult).then_inc(conv_ok, 1)

            def split_lo(q):
                pool.wait_ge(w_hi_ok, q + 1)
                g.tensor_tensor(w_lo[:, q % 2], raw[split_at[q] % 2], w_hi[:, q % 2].bitcast(F32), ALU.subtract)\
                 .then_inc(w_lo_ok, 1)

            def products(k):
                pool.wait_ge(conv_ok, k + 1)
                ch.link(g.tensor_copy(glu_s[:, k, :, W30:], seqs(glu[:, k, W30 + TP:])))
                if k:
                    pool.wait_ge(prod_used, k)
                taps = rt[:, k, R_CW:R_CW + 31].unsqueeze(1).to_broadcast([P, NS, 31])
                for s in range(TS):
                    ins = g.tensor_tensor(prod[:, s], glu_s[:, k, :, s:s + 31], taps, ALU.mult)
                ins.then_inc(prod_ok, 1)

            split_lo(0)
            split_lo(1)
            pool.wait_ge(hm_lo_ok, NT)
            g.memset(glu[:, :, 0:W30], 0.0).then_inc(conv_new, 1)
            split_lo(2)
            split_lo(3)
            pool.wait_ge(y_clear, 16)
            pool.wait_ge(sconf_ok, 4)
            gate_glu(0)
            products(0)
            gate_glu(1)
            split_lo(4)
            gate_glu(2)
            split_lo(5)
            gate_glu(3)
            products(1)
            split_lo(6)
            products(2)
            split_lo(7)
            gate_glu(4)
            split_lo(8)
            gate_glu(5)
            products(3)
            gate_glu(6)
            split_lo(9)
            gate_glu(7)
            pool.wait_ge(ada_ps, 12)
            g.memset(u[:, :, 0:W3], 0.0).then_inc(us_ok, 1)
            products(4)
            split_lo(10)
            split_lo(11)
            products(5)
            split_lo(12)
            split_lo(13)
            products(6)
            split_lo(14)
            split_lo(15)
            products(7)
            for q in range(16, len(split_at)):
                split_lo(q)
            for t in range(NT):
                n = TILES[t]
                pool.wait_ge(hf_dve, t + 1)
                if t == 0:
                    pool.wait_ge(bc_in, 16 * 6)
                if t < NT - 1:
                    g.tensor_tensor(hf[0:n, t % 2, :], hf[0:n, t % 2, :], sh2_bc[0:n, t // 4, :], ALU.add)\
                     .then_inc(hf_sum, 1)
                pool.wait_ge(hf_sum, t + 1)
                g.dma_start(hf_scr[t * P:t * P + n, :], hf[0:n, t % 2, :]).then_inc(hf_store[t % 2], 16)
            pool.wait_ge(hf_store[0], 16 * 3)
            pool.wait_ge(hf_store[1], 16 * 2)

            def gather(e, s):
                g.indirect_dma_start(out=xg[:, s, :], out_offset=None, in_=hf_scr,
                                     in_offset=bass.IndirectOffsetOnAxis(ap=idx_i[:, e:e + 1], axis=0))\
                 .then_inc(xg_full[s], 16)

            def store(e, s):
                g.dma_start(y_scr[e * CAP:(e + 1) * CAP, :], yb[0:CAP, s, :]).then_inc(y_store[s], 16)

            pool.wait_ge(lg_ps, NT)
            for e in range(NE + 2):
                if e < NE:
                    if e >= 2:
                        pool.wait_ge(xgt_ps, e - 1)
                    pool.wait_ge(idx_ok, e + 1)
                    gather(e, e % 2)
                if e >= 2:
                    pool.wait_ge(y_act, e - 1)
                    pool.wait_ge(y_dve, e - 1)
                    store(e - 2, e % 2)
            pool.wait_ge(y_store[0], 16 * (NE // 2))
            pool.wait_ge(y_store[1], 16 * (NE // 2))
            pool.wait_ge(ov_ok, 1)
            n_over = pool.value_load(ovt[0:1, MAX_OVER:MAX_OVER + 1], min_val=0, max_val=MAX_OVER)
            with pool.If(n_over > 0):
                with pool.Fori(0, n_over) as k:
                    pool.wait_ge(ov_idx, k + 1)
                    g.tensor_tensor(idx_vg[:, :], idx_vf[:, :], ovk[:, 0:1], ALU.add)
                    pool.drain()
                    g.tensor_copy(idx_ov[:, :], idx_vg[:, :])
                    pool.drain()
                    g.indirect_dma_start(out=xg[:, 0, :], out_offset=None, in_=hf_scr,
                                         in_offset=bass.IndirectOffsetOnAxis(ap=idx_ov[:, :], axis=0))\
                     .then_inc(ov_x, 16)
                    pool.wait_ge(ov_dve, k * 4 + 4)
                    g.dma_start(y_scr[bass.ds((k + NE) * CAP, CAP), :], yb[0:CAP, 0, :]).then_inc(ov_st, 16)
                    pool.wait_ge(ov_st, k * 16 + 16)
            with pool.Else():
                pool.nop()
            pool.wait_ge(slot_ok, 2)
            for t in range(NT):
                n = TILES[t]
                for j, dst in enumerate((ya, yc)):
                    g.indirect_dma_start(out=dst[0:n, t, :], out_offset=None, in_=y_scr,
                                         in_offset=bass.IndirectOffsetOnAxis(ap=slot_i[0:n, j, t:t + 1], axis=0))\
                     .then_inc(y_in[t], 16)

        @block.scalar
        def _(act):
            s_ = nc.scalar
            ch = Chain(act, act_step)
            act.wait_ge(crow_in, 32)
            s_.activation(crow[0:NSEQ, :], crow[0:NSEQ, :], ACT.Silu).then_inc(csilu, 1)
            act.wait_ge(x_in, 16 * NT)
            junk1 = region_d[:, 4 * D:5 * D]
            act.wait_ge(ssq_clear, 1)
            for t in range(NT):
                n = TILES[t]
                s_.activation(junk1[0:n, :], xt[0:n, t, :], ACT.Square, accum_out=ssq[0:n, t:t + 1]).then_inc(ssq_ok, 1)
                act.wait_ge(ssq_ok, t + 1)
            act.wait_ge(sct_ok, 1)
            act.wait_ge(sp_ask, 1)
            s_.activation(spt[:, 1, :], spt[:, 0, :], ACT.Exp, scale=-1.0).then_inc(sp_exp, 1)
            act.wait_ge(rms_ask, 1)
            s_.activation(nt1[:, :], ssq[:, :], ACT.Sqrt).then_inc(rms_sqrt, 1)
            act.wait_ge(rstd_ok, 1)
            for t in range(NT):
                n = TILES[t]
                s_.activation(xt[0:n, t, :], xt[0:n, t, :], ACT.Copy, scale=rstd[0:n, t:t + 1]).then_inc(xn_ok, 1)
            def split_hi(q):
                n = split_at[q]
                act.wait_ge(raw_full[n % 2], 16 * (n // 2 + 1))
                if q >= 2:
                    act.wait_ge(pairs, last_use(split_at[q - 2]) + 1)
                else:
                    act.wait_ge(ada_ps, 4)
                s_.activation(w_hi[:, q % 2], raw[n % 2], ACT.Copy).then_inc(w_hi_ok, 1)


            split_hi(0)
            act.wait_ge(modt_ok, 1)

            def hm_first(t):
                act.wait_ge(hm_dve, t + 1)
                act.wait_ge(hm_act, min(t + 1, NT - 1))
                ts = slice(t * P, t * P + TILES[t])
                s_.activation(hm_hi[:, :, ts], hm[:, :, ts], ACT.Copy).then_inc(hm_hi_ok, 1)

            for t in range(NT - 1):
                act.wait_ge(x_tr, t + 1)
                for k in range(4, KC):
                    ins = s_.activation(hm[:, k, t * P:(t + 1) * P], ps[:, 5 + 2 * (t % 2), (k - 4) * P:(k - 3) * P],
                                        ACT.Identity, bias=modt[:, k, 0:1], scale=amod[:, k, 0:1])
                ins.then_inc(hm_act, 1)
                if t:
                    hm_first(t - 1)
            hm_first(NT - 2)
            hm_first(NT - 1)
            split_hi(1)

            def drain(n):
                kind, g, m = work[n]
                act.wait_ge(pairs, n + 1)
                if kind == "in":
                    k = (g % 2) * GC + m
                    bias = rt[:, k, R_BIN + g // 2:R_BIN + g // 2 + 1]
                    if g in (G_CA, G_CA + 1):
                        ins = s_.activation(two(glu[:, k, W30:]), pair(n), ACT.Identity, bias=bias)
                    elif g in (G_CB, G_CB + 1):
                        if k >= 2:
                            act.wait_ge(conv_ok, k - 1)
                        ins = s_.activation(two(sg[:, k % 2, :]), pair(n), ACT.Sigmoid, bias=bias)
                    elif g in (G_U, G_U + 1):
                        ins = s_.activation(two(u[:, k, W3:]), pair(n), ACT.Identity, bias=bias)
                    elif g in (G_GATE, G_GATE + 1):
                        ins = s_.activation(two(z[:, k, :]), pair(n), ACT.Gelu_apprx_tanh, bias=bias)
                    else:
                        if m == 0 and g == G_BL + 1:
                            act.wait_ge(merged_ok, GC)
                        elif m == 0 and g != G_BC:
                            act.wait_ge(pair_dve, GC if g == G_BC + 1 else 2 * GC)
                        ins = s_.activation(two(bg[m]), pair(n), ACT.Sigmoid, bias=bias)
                elif kind == "r":
                    k = g * GC + m
                    act.wait_ge(last_tr, 1)
                    ins = s_.activation(two(tt[:, m, :]), pair(n), ACT.Sigmoid, bias=rt[:, k, R_BA:R_BA + 1])
                elif kind == "i":
                    k = g * GC + m
                    ins = s_.activation(two(ii[:, m, :]), pair(n), ACT.Sigmoid, bias=rt[:, k, R_BX:R_BX + 1])
                elif kind == "mean":
                    ins = s_.activation(two(ln_mean), pair(n), ACT.Copy, scale=1.0 / D)
                elif kind == "var":
                    ins = s_.activation(two(ln_rstd), pair(n), ACT.Sqrt, bias=eps_ln[:, :], scale=1.0 / D)
                ins.then_inc(pair_act, 1)

            def squares():
                act.wait_ge(cent_ok, 1)
                for k in range(KC):
                    if k >= 2:
                        act.wait_ge(sq_used, k - 1)
                    s_.activation(ln_sq[:, k % 2, :], dc[:, k, :], ACT.Square).then_inc(sq_ok, 1)

            def first_taps(k):
                act.wait_ge(conv_ok, k + 1)
                act.wait_ge(conv_new, 1)
                if k >= 2:
                    act.wait_ge(dc_ok, k - 1)
                taps = rt[:, k, R_CW:R_CW + 2]
                ins = s_.activation(dc[:, k, 0:TP], glu[:, k, 0:TP], ACT.Identity, bias=rt[:, k, R_CB:R_CB + 1],
                                    scale=taps[:, 0:1])
                if k < KC - 1:
                    ins = s_.activation(odd[k], glu[:, k, 1:1 + TP], ACT.Copy, scale=taps[:, 1:2])
                ins.then_inc(tap_ok, 1)

            taps_after = {6: 1, 8: 2, 10: 3, 13: 4, 17: 5, 20: 6, 22: 7}

            def root(g):
                act.wait_ge(t_copied, g + 1)
                s_.activation(tt, tt, ACT.Sqrt).then_inc(sqrt_ok, 1)

            act.wait_ge(consts, 4)
            for n in range(len(work)):
                if not by_act[n]:
                    for q in split_after.get(n, ()):
                        split_hi(q)
                    if work[n] == ("co", 1, 0):
                        root(1)
                    continue
                kind, g, m = work[n]
                if (kind, g, m) == ("in", G_GATE, 0):
                    act.wait_ge(mod_store, 16)
                if (kind, g, m) == ("var", 0, 0):
                    squares()
                if (kind, g, m) == ("in", G_BC, 2):
                    act.wait_ge(ln_ok, 1)
                    for k in range(KC):
                        s_.activation(dc[:, k, :], dc[:, k, :], ACT.Silu, bias=rt[:, k, R_LNB:R_LNB + 1],
                                      scale=rt[:, k, R_LNG:R_LNG + 1]).then_inc(sn_ok, 1)
                drain(n)
                if n - 1 in ada_after:
                    j = ada_after[n - 1]
                    act.wait_ge(ada_sum, j + 1)
                    s_.activation(mod2[0:NSEQ, (j - 4) * GW:(j - 3) * GW], ps[0:NSEQ, 4 + j % 2, :], ACT.Copy)\
                      .then_inc(ada_act, 1)
                if n in ada_after:
                    j = ada_after[n]
                    act.wait_ge(ada_ps, j + 1)
                    act.wait_ge(ada_sum, j - 1)
                    s_.activation(ada_tmp[:, j % 2, :], ps[:, 6 + j % 2, :], ACT.Copy).then_inc(ada_cp, 1)
                for q in split_after.get(n, ()):
                    split_hi(q)
                if n in taps_after:
                    first_taps(taps_after[n])
                if (kind, g, m) == ("in", G_BL, 1):
                    act.wait_ge(pairs, place[("co", 1, GC - 1)] + 1)
                    for h in range(2):
                        act.wait_ge(z_ok, h + 1)
                        hs = slice(h * GC, (h + 1) * GC)
                        s_.activation(z_hi[:, hs], z[:, hs], ACT.Copy).then_inc(z_hi_ok, 1)
                if kind == "i" and m == GC - 1:
                    act.wait_ge(sp_ok, 1)
                    act.wait_ge(pair_act, sum(by_act[:n + 1]))
                    for c in range(GC):
                        ins = s_.activation(tt[:, c, :], tt[:, c, :], ACT.Tanh,
                                            scale=sp4[:, g * GC + c:g * GC + c + 1])
                    ins.then_inc(t_ok, 1)
                if (kind, g, m) == ("in", G_BC, GC - 1):
                    root(0)

            def hft_half(t):
                n = TILES[t]
                act.wait_ge(hft_tr, t + 1)
                if t >= 2:
                    act.wait_ge(lg_ps, t - 1)
                s_.activation(hft[:, t % 2, 4:KC, 0:n],
                              ps[:, 5, :].rearrange("p (k c) -> p k c", k=4)[:, :, 0:n], ACT.Copy).then_inc(hft_act, 1)

            for t in range(NT):
                n = TILES[t]
                act.wait_ge(x1_ok, t + 1)
                if t:
                    act.wait_ge(ssq_ok, NT + t)
                s_.activation(yb[0:n, 1, :], x1[0:n, t, :], ACT.Square, accum_out=ssq[0:n, t:t + 1]).then_inc(ssq_ok, 1)
                if t:
                    hft_half(t - 1)
                act.wait_ge(rms_ask, t + 2)
                s_.activation(nt1[0:n, t:t + 1], ssq[0:n, t:t + 1], ACT.Sqrt).then_inc(rms_sqrt, 1)
            hft_half(NT - 1)
            act.wait_ge(exp_ask, 1)
            s_.activation(lg, lg, ACT.Exp).then_inc(exp_ok, 1)

            def xgt_half(e):
                act.wait_ge(xgt_ps, e + 1)
                s_.activation(xgt[:, 4:KC, :], ps[:, 3, :].rearrange("p (k c) -> p k c", k=4), ACT.Copy)\
                  .then_inc(xgt_act, 1)

            def silu(e):
                act.wait_ge(gate_ps, e + 1)
                s_.activation(act_g, ps[:, 0, :], ACT.Silu).then_inc(silu_ok, 1)

            def y_half(e, s, stored=None):
                act.wait_ge(y_ps, e + 1)
                if stored is not None:
                    act.wait_ge(y_store[s], stored)
                s_.activation(yb[:, s, DE:], ps[:, 6, :], ACT.Copy).then_inc(y_act, 1)

            def turn(e):
                act.wait_ge(ht_ps, e + 1)
                s_.activation(act_hi[:, :, :], ps[:, 4, :].rearrange("p (k c) -> p k c", k=DE // P), ACT.Copy)\
                  .then_inc(ht_ok, 1)
                for q in range(DE // P):
                    act.wait_ge(wd_full[q], e * 16 + 16)
                    s_.activation(wd_hi[:, q, :], wd_raw[q], ACT.Copy).then_inc(wd_hi_ok, 1)

            xgt_half(0)
            silu(0)
            xgt_half(1)
            turn(0)
            silu(1)
            y_half(0, 0)
            xgt_half(2)
            turn(1)
            silu(2)
            y_half(1, 1)
            xgt_half(3)
            turn(2)
            with act.Fori(1, NE // 2 - 1) as i:
                for s in range(2):
                    e = i * 2 + 1 + s
                    silu(e)
                    y_half(e - 1, s, i * 16)
                    xgt_half(e + 1)
                    turn(e)
            silu(NE - 1)
            y_half(NE - 2, 0, 16 * (NE // 2 - 1))
            turn(NE - 1)
            y_half(NE - 1, 1, 16 * (NE // 2 - 1))

            act.wait_ge(ov_ok, 1)
            n_over = act.value_load(ovt[0:1, MAX_OVER:MAX_OVER + 1], min_val=0, max_val=MAX_OVER)
            with act.If(n_over > 0):
                with act.Fori(0, n_over) as k:
                    act.wait_ge(ov_pe, k * 5 + 3)
                    s_.activation(act_g, ps[:, 0, :], ACT.Silu).then_inc(ov_act, 1)
            with act.Else():
                act.nop()
            def scale_first(t):
                n = TILES[t]
                act.wait_ge(y_in[t], 32)
                s_.activation(ya[0:n, t, :], ya[0:n, t, :], ACT.Copy, scale=w12[0:n, 0, t:t + 1]).then_inc(y_scaled, 1)

            act.wait_ge(slot_ok, 2)
            scale_first(0)
            for t in range(NT):
                n = TILES[t]
                if t < NT - 1:
                    scale_first(t + 1)
                act.wait_ge(fin_dve, t + 1)
                if t:
                    act.wait_ge(fin_act, t)
                s_.activation(junk[0:n, :], x1[0:n, t, :], ACT.Square, accum_out=ssq[0:n, t:t + 1]).then_inc(fin_act, 1)
                act.wait_ge(rms_ask, NT + t + 2)
                s_.activation(nt1[0:n, t:t + 1], ssq[0:n, t:t + 1], ACT.Sqrt).then_inc(rms_sqrt, 1)

        @block.tensor
        def _(pe):
            mm, tr = nc.tensor.matmul, nc.tensor.transpose
            pe.wait_ge(consts, 3)
            pe.wait_ge(csilu, 1)
            for k in range(KC):
                ins = tr(ps[:, 4, k * NSEQ:(k + 1) * NSEQ], crow[0:NSEQ, k * P:(k + 1) * P], ident[0:NSEQ, 0:NSEQ])
            ins.then_inc(c_tr, 1)
            pe.wait_ge(vec_in, 16 * 13)
            for k in range(KC):
                ins = tr(ps[:, 5 + k // 4, (k % 4) * NVEC:(k % 4 + 1) * NVEC], vec[0:NVEC, k * P:(k + 1) * P],
                         ident[0:NVEC, 0:NVEC])
            ins.then_inc(vec_tr, 1)
            pe.wait_ge(sct_ok, 1)

            def ada(j):
                if j >= 2:
                    pe.wait_ge(ada_cp, j - 1)
                if j < 4:
                    pe.wait_ge(ada_in[j], 16)
                if j == 4:
                    pe.wait_ge(sconf_ok, 4)
                for k in range(KC):
                    q = k % 4
                    if j >= 4 and q == 0:
                        pe.wait_ge(ada_half[k // 4], 16 * (j - 3))
                    w = ada_w[j][:, k, :] if j < 4 else ada_h[k // 4][:, q, :]
                    ins = mm(ps[q * CT:(q + 1) * CT, j % 2 if j < 4 else 6 + j % 2, :], sct[:, k, :], w,
                             start=(k < 4), stop=(k >= KC - 4))
                    if j >= 4 and k == 3:
                        ins.then_inc(ada_read, 1)
                ins.then_inc(ada_ps, 1)

            def ada_add(j):
                pe.wait_ge(ada_cp, j + 1)
                if j in (2, 3):
                    pe.wait_ge(ada_ok, j - 1)
                if j >= 6:
                    pe.wait_ge(ada_act, j - 5)
                out = ps[0:CT, 2 + j % 2 if j < 4 else 4 + j % 2, :]
                if j >= 4:
                    mm(out, ones[0:1, 0:CT], mod2[0:1, (j - 4) * GW:(j - 3) * GW], start=True, stop=False)
                mm(out, sel[:, :], ada_tmp[:, j % 2, :], start=(j < 4), stop=True).then_inc(ada_sum, 1)

            pe.wait_ge(sel_mat, P // CT)
            for j in range(4):
                ada(j)
                if j:
                    ada_add(j - 1)
            ada_add(3)
            def x_turn(t):
                n = TILES[t]
                pe.wait_ge(xn_ok, t + 1)
                if t < 2:
                    pe.wait_ge(rt_ok, 1)
                else:
                    pe.wait_ge(hm_dve, t - 1)
                    pe.wait_ge(hm_act, t - 1)
                for k in range(KC):
                    ins = tr(ps[:, 4 + 2 * (t % 2) + k // 4, (k % 4) * P:(k % 4) * P + n],
                             xt[0:n, t, k * P:(k + 1) * P], ident[0:n, 0:n])
                ins.then_inc(x_tr, 1)

            x_turn(0)
            x_turn(1)
            pe.wait_ge(ada_ok, 4)
            for j in range(2 * KC):
                ins = tr(ps[:, 2, j * NSEQ:(j + 1) * NSEQ], mod1[0:NSEQ, j * P:(j + 1) * P], ident[0:NSEQ, 0:NSEQ])
            ins.then_inc(modt_tr, 1)
            for t in range(2, NT):
                x_turn(t)
            pe.wait_ge(sconf_in, 32)
            for b in range(4):
                if b == 0:
                    pe.wait_ge(hm_dve, NT)
                    pe.wait_ge(hm_act, NT - 1)
                for j in range(4):
                    k, h = 2 * b + j // 2, j % 2
                    ins = tr(ps[:, 4 + b, j * 120:(j + 1) * 120], sconf[0:120, h, k * P:(k + 1) * P],
                             ident[0:120, 0:120])
                ins.then_inc(sconf_tr, 1)
            pe.wait_ge(hm_lo_ok, NT)

            def chunk(n, w, m, rhs):
                for k in range(KC):
                    for h in range(2):
                        ins = mm(ps[:, 2 * (n % 2) + h, 0:HALF], w[:, k, m * P:(m + 1) * P],
                                 rhs[:, k, h * HALF:(h + 1) * HALF], start=(k == 0), stop=(k == KC - 1))
                return ins

            def chunk_split(n, q, m, x_hi, x_lo):
                for k in range(KC):
                    for w, xs in ((w_hi, (x_hi, x_lo)), (w_lo, (x_hi,))):
                        for x in xs:
                            for h in range(2):
                                ins = mm(ps[:, 2 * (n % 2) + h, 0:HALF], w[:, q % 2, k, m * P:(m + 1) * P],
                                         x[:, k, h * HALF:(h + 1) * HALF], start=(k == 0 and w is w_hi and x is x_hi),
                                         stop=(k == KC - 1 and w is w_lo))
                return ins

            def rows_out(src, cols0, n):
                for k in range(KC):
                    ins = tr(ps[0:n, 4 + k // 4, (k % 4) * P:(k % 4 + 1) * P], src[:, k, cols0:cols0 + n], ident[:, :])
                ins.then_inc(last_tr, 1)

            for n, (kind, g, m) in enumerate(work):
                if kind in ("in", "co", "lo"):
                    f = piece_of[(kind, g, m // 2)]
                    if f in split_no:
                        pe.wait_ge(w_lo_ok, split_no[f] + 1)
                    else:
                        pe.wait_ge(raw_full[f % 2], 16 * (f // 2 + 1))
                    if kind == "co" and m == 0:
                        pe.wait_ge(sn_ok, KC)
                    if kind == "lo" and m == 0:
                        pe.wait_ge(z_lo_ok, 2)
                    drained(pe, n - 2)
                    if kind == "in":
                        ins = chunk_split(n, split_no[f], m % 2, hm_hi, hm_lo)
                    elif kind == "lo":
                        ins = chunk_split(n, split_no[f], m % 2, z_hi, z_lo)
                    else:
                        ins = chunk(n, raw[f % 2], m % 2, dc)
                    ins.then_inc(pairs, 1)
                elif kind in ("r", "i"):
                    drained(pe, n - 2)
                    pe.wait_ge(xc_ok, g * GC + m + 1)
                    for h in range(2):
                        ins = mm(ps[:, 2 * (n % 2) + h, 0:HALF], gate_w[kind == "i"][:, g * GC + m, :],
                                 xc[:, m, h * HALF:(h + 1) * HALF], start=True, stop=True)
                    ins.then_inc(pairs, 1)
                elif kind == "mean":
                    drained(pe, n - 2)
                    pe.wait_ge(dc_ok, KC)
                    for k in range(KC):
                        for h in range(2):
                            ins = mm(ps[:, 2 * (n % 2) + h, 0:HALF], ones[:, :], dc[:, k, h * HALF:(h + 1) * HALF],
                                     start=(k == 0), stop=(k == KC - 1))
                    ins.then_inc(pairs, 1)
                    rows_out(glu, TP, 62)
                elif kind == "var":
                    drained(pe, n - 2)
                    for k in range(KC):
                        pe.wait_ge(sq_ok, k + 1)
                        for h in range(2):
                            ins = mm(ps[:, 2 * (n % 2) + h, 0:HALF], ones[:, :], ln_sq[:, k % 2, h * HALF:(h + 1) * HALF],
                                     start=(k == 0), stop=(k == KC - 1))
                        if k < KC - 1:
                            ins.then_inc(sq_used, 1)
                    ins.then_inc(pairs, 1)
                    pe.wait_ge(last_sb, 1)
                    rows_out(u, TP, 35)
                if (kind, g, m) == ("in", G_U, GC - 1):
                    pe.wait_ge(bd_in, 16 * 6)
                if n - 1 in ada_after:
                    pe.wait_ge(bias2_in, 16)
                    ada_add(ada_after[n - 1])
                if n in ada_after:
                    ada(ada_after[n])
                if (kind, g, m) == ("lo", 0, 0):
                    pe.wait_ge(last_sb, 2)
                    rows_out(hlast, 0, 33)
            drained(pe, len(work) - 1)
            drained(pe, len(work) - 2)
            pe.wait_ge(merged_ok, KC)

            def w_out(t):
                n = TILES[t]
                for h in range(2):
                    pe.wait_ge(wo_full[h], 16)
                    j = 2 * t + h
                    if j >= 4:
                        pe.wait_ge(x1_half, j - 3)
                    for k in range(KC):
                        ins = mm(ps[0:n, j % 4, :], merged[:, k, t * P:t * P + n], wo[h][:, k, :],
                                 start=(k == 0), stop=(k == KC - 1))
                    ins.then_inc(out_ps, 1)

            def hf_turn(t):
                n = TILES[t]
                pe.wait_ge(hf_sum, t + 1)
                if t:
                    pe.wait_ge(hft_act, t)
                    pe.wait_ge(hft_dve, t)
                for k in range(KC):
                    ins = tr(ps[:, 4 + k // 4, (k % 4) * P:(k % 4) * P + n], hf[0:n, t % 2, k * P:(k + 1) * P],
                             ident[0:n, 0:n])
                ins.then_inc(hft_tr, 1)

            def logits(t):
                n = TILES[t]
                pe.wait_ge(hft_act, t + 1)
                pe.wait_ge(hft_dve, t + 1)
                for k in range(KC):
                    ins = mm(ps[0:n, 6, t * NE:(t + 1) * NE], hft[:, t % 2, k, 0:n], wr[:, k, :],
                             start=(k == 0), stop=(k == KC - 1))
                ins.then_inc(lg_ps, 1)

            for t in range(NT):
                w_out(t)
                if t == 0:
                    pe.wait_ge(last_sb, 3)
                if t >= 2:
                    logits(t - 2)
                if t:
                    hf_turn(t - 1)
            logits(NT - 2)
            hf_turn(NT - 1)
            logits(NT - 1)
            pe.wait_ge(sel_ok, 1)
            for t in range(NT + 1):
                for q in range(min(t, NT - 1) + 1):
                    last = q == min(t, NT - 1)
                    w = tri if last and t < NT else ones_b
                    ins = mm(ps[:, 7, t * NE:(t + 1) * NE], w[:, :], sel_b[:, q, :], start=(q == 0), stop=last)
            ins.then_inc(rank_ps, 1)
            def index(e, s, first=False):
                pe.wait_ge(mb_ok, e + 1)
                if not first:
                    pe.wait_ge(idx_cp, e)
                for t in range(NT):
                    ins = mm(ps[:, 7, 256 + 2 * s:258 + 2 * s], mb[:, s, t, :], tokid[:, t, :], start=(t == 0), stop=(t == NT - 1))
                ins.then_inc(idx_ps, 1)

            for e in range(AHEAD):
                index(e, e % 2, first=(e == 0))

            def xg_turn(e, s, n16):
                pe.wait_ge(xg_full[s], n16)
                for k in range(KC):
                    ins = tr(ps[:, 2 + k // 4, (k % 4) * P:(k % 4 + 1) * P], xg[:, s, k * P:(k + 1) * P], ident[:, :])
                ins.then_inc(xgt_ps, 1)

            def gate_up(e, s, n16):
                pe.wait_ge(xgt_act, e + 1)
                pe.wait_ge(xgt_dve, e + 1)
                for w, full, b, out_s in ((wg, wg_full, 0, gate_ps), (wu, wu_full, 1, up_ps)):
                    pe.wait_ge(full[s], n16)
                    for k in range(KC):
                        ins = mm(ps[:, b, :], xgt[:, k, :], w[s][:, k, :], start=(k == 0), stop=(k == KC - 1))
                    ins.then_inc(out_s, 1)

            def h_turn(e):
                pe.wait_ge(h_ok, e + 1)
                for k in range(DE // P):
                    ins = tr(ps[:, 4, k * P:(k + 1) * P], act_g[:, k * P:(k + 1) * P], ident[:, :])
                ins.then_inc(ht_ps, 1)

            def down(e, s, n16, before=True):
                pe.wait_ge(ht_lo_ok, e + 1)
                if before:
                    pe.wait_ge(y_act, e)
                    pe.wait_ge(y_dve, e)
                for k in range(DE // P):
                    pe.wait_ge(wd_lo_ok, e * (DE // P) + k + 1)
                    for x, w in ((act_hi, wd_hi), (act_lo, wd_hi), (act_hi, wd_lo)):
                        for h in range(2):
                            ins = mm(ps[:, 5 + h, :], x[:, k, :], w[:, k, h * DE:(h + 1) * DE],
                                     start=(k == 0 and x is act_hi and w is wd_hi),
                                     stop=(k == DE // P - 1 and w is wd_lo))
                ins.then_inc(y_ps, 1)

            def step(e, s, pair_n, index_too=True, down_before=True, turn_next=True):
                gate_up(e, s, 16 * pair_n)
                if index_too:
                    index(e + AHEAD, 1 - s)
                if down_before:
                    down(e - 1, 1 - s, 16 * (pair_n - 1 + s))
                if turn_next:
                    xg_turn(e + 1, 1 - s, 16 * (pair_n + s))
                h_turn(e)

            xg_turn(0, 0, 16)
            gate_up(0, 0, 16)
            index(AHEAD, 1)
            xg_turn(1, 1, 16)
            h_turn(0)
            gate_up(1, 1, 16)
            index(1 + AHEAD, 0)
            down(0, 0, 16, before=False)
            xg_turn(2, 0, 32)
            h_turn(1)
            step(2, 0, 2)
            with pe.Fori(1, 6) as i:
                step(i * 2 + 1, 1, i + 1)
                step(i * 2 + 2, 0, i + 2)
            step(13, 1, 7, index_too=False)
            step(14, 0, 8, index_too=False)
            step(15, 1, 8, index_too=False, turn_next=False)
            down(NE - 1, 1, 16 * (NE // 2))

            pe.wait_ge(ov_ok, 1)
            n_over = pe.value_load(ovt[0:1, MAX_OVER:MAX_OVER + 1], min_val=0, max_val=MAX_OVER)
            with pe.If(n_over > 0):
                with pe.Fori(0, n_over) as k:
                    pe.wait_ge(mb_ok, k + NE + 1)
                    for t in range(NT):
                        ins = mm(ps[:, 7, 0:2], mb[:, 0, t, :], tokid[:, t, :], start=(t == 0), stop=(t == NT - 1))
                    ins.then_inc(ov_pe, 1)
                    pe.wait_ge(ov_x, k * 16 + 16)
                    for c in range(KC):
                        ins = tr(ps[:, 2 + c // 4, (c % 4) * P:(c % 4 + 1) * P], xg[:, 0, c * P:(c + 1) * P], ident[:, :])
                    ins.then_inc(ov_pe, 1)
                    pe.wait_ge(ov_dve, k * 4 + 1)
                    pe.wait_ge(ov_w, k * 48 + 48)
                    for w, b in ((wg, 0), (wu, 1)):
                        for c in range(KC):
                            ins = mm(ps[:, b, :], xgt[:, c, :], w[0][:, c, :], start=(c == 0), stop=(c == KC - 1))
                    ins.then_inc(ov_pe, 1)
                    pe.wait_ge(ov_dve, k * 4 + 2)
                    for c in range(DE // P):
                        ins = tr(ps[:, 4, c * P:(c + 1) * P], act_g[:, c * P:(c + 1) * P], ident[:, :])
                    ins.then_inc(ov_pe, 1)
                    pe.wait_ge(ov_dve, k * 4 + 3)
                    for c in range(DE // P):
                        for h in range(2):
                            ins = mm(ps[:, 5 + h, :], act_t[:, c, :], wd[0][:, c, h * DE:(h + 1) * DE],
                                     start=(c == 0), stop=(c == DE // P - 1))
                    ins.then_inc(ov_pe, 1)
            with pe.Else():
                pe.nop()

        @block.vector
        def _(dve):
            v = nc.vector
            ch = Chain(dve, dve_step)
            v.memset(ssq[:, :], 1.0).then_inc(ssq_clear, 1)
            dve.wait_ge(consts, 3)
            for q in range(P // CT):
                v.tensor_copy(sel[q * CT:(q + 1) * CT, :], ident[q * CT:(q + 1) * CT, q * CT:(q + 1) * CT])\
                 .then_inc(sel_mat, 1)
            dve.wait_ge(c_tr, 1)
            dve.wait_ge(sct_zero, 1)
            v.tensor_copy(sct[:, :, 0:NSEQ], ps[:, 4, 0:KC * NSEQ].rearrange("p (k s) -> p k s", k=KC)).then_inc(sct_ok, 1)
            dve.wait_ge(vec_tr, 1)
            ch.link(v.tensor_copy(rt[:, 0:4, :], ps[:, 5, 0:4 * NVEC].rearrange("p (k r) -> p k r", k=4)))
            ch.do(v.tensor_copy(rt[:, 4:8, :], ps[:, 6, 0:4 * NVEC].rearrange("p (k r) -> p k r", k=4)))
            ch.wait()
            lam = rt[:, :, R_LAM]
            ch.link(v.tensor_scalar(spt[:, 0, :], lam, -1.0, None, ALU.mult))
            v.tensor_tensor(spt[:, 0, :], spt[:, 0, :], lam, ALU.max).then_inc(sp_ask, 1)
            v.tensor_copy(spt[:, 3, :], lam).then_inc(rt_ok, 1)
            def ada_copy(j):
                dve.wait_ge(ada_ps, j + 1)
                v.tensor_copy(ada_tmp[:, j % 2, :], ps[:, j % 2, :]).then_inc(ada_cp, 1)

            def ada_rows(j):
                dst = mod1[0:NSEQ, j * GW:(j + 1) * GW]
                dve.wait_ge(ada_sum, j + 1)
                dve.wait_ge(bias_in, 16)
                v.tensor_tensor(dst, ps[0:NSEQ, 2 + j % 2, :], dst, ALU.add).then_inc(ada_ok, 1)

            ada_copy(0)
            ada_copy(1)
            ada_rows(0)
            dve.wait_ge(ssq_ok, NT)
            v.tensor_scalar(ssq[:, :], ssq[:, :], 1.0 / D, RMS_EPS, ALU.mult, ALU.add).then_inc(rms_ask, 1)
            dve.wait_ge(rms_sqrt, 1)

            def newton(n, lo, hi):
                r, q, w = rstd[0:n, lo:hi], nt1[0:n, lo:hi], ssq[0:n, lo:hi]
                ch.link(v.reciprocal(r, q))
                ch.link(v.tensor_tensor(q, r, r, ALU.mult))
                ch.link(v.scalar_tensor_tensor(q, q, -0.5, w, ALU.mult, ALU.mult))
                return v.scalar_tensor_tensor(r, q, 1.5, r, ALU.add, ALU.mult)

            newton(P, 0, NT).then_inc(rstd_ok, 1)
            dve.wait_ge(sp_exp, 1)
            e_, y_, y2, acc = spt[:, 1, :], spt[:, 0, :], spt[:, 2, :], sp4[:, :]
            ch.link(v.tensor_scalar(y2, e_, 2.0, None, ALU.add))
            ch.link(v.reciprocal(y2, y2))
            ch.link(v.tensor_tensor(y_, e_, y2, ALU.mult))
            ch.link(v.tensor_tensor(y2, y_, y_, ALU.mult))
            ch.link(v.tensor_scalar(acc, y2, 1.0 / 17, 1.0 / 15, ALU.mult, ALU.add))
            for c in (13, 11, 9, 7, 5, 3, 1):
                ch.link(v.tensor_tensor(acc, acc, y2, ALU.mult))
                ch.link(v.tensor_scalar(acc, acc, 1.0 / c, None, ALU.add))
            ch.link(v.tensor_tensor(acc, acc, y_, ALU.mult))
            ch.link(v.tensor_scalar(e_, spt[:, 3, :], -1.0, 0.0, ALU.mult, ALU.max))
            ch.link(v.scalar_tensor_tensor(acc, acc, 2.0, e_, ALU.mult, ALU.add))
            v.tensor_scalar(acc, acc, 4.0, None, ALU.mult).then_inc(sp_ok, 1)

            ada_copy(2)
            ada_rows(1)
            ada_copy(3)
            ada_rows(2)
            ada_rows(3)
            dve.wait_ge(modt_tr, 1)
            ch.link(v.tensor_copy(modt[:, :, :], ps[:, 2, 0:2 * KC * NSEQ].rearrange("p (j s) -> p j s", s=NSEQ)))
            ins = v.scalar_tensor_tensor(amod[:, :, :], modt[:, KC:, :], 1.0,
                                         rt[:, :, R_GMIX:R_GMIX + 1].to_broadcast([P, KC, NSEQ]), ALU.add, ALU.mult)
            ins.then_inc(modt_ok, 1)
            dve.wait_ge(modt_ok, 1)
            def hm_second(t):
                dve.wait_ge(hm_hi_ok, t + 1)
                ts = slice(t * P, t * P + TILES[t])
                v.tensor_tensor(hm_lo[:, :, ts], hm[:, :, ts], hm_hi[:, :, ts].bitcast(F32), ALU.subtract)\
                 .then_inc(hm_lo_ok, 1)

            for t in range(NT - 1):
                dve.wait_ge(x_tr, t + 1)
                for k in range(4):
                    ins = v.tensor_scalar(hm[:, k, t * P:(t + 1) * P], ps[:, 4 + 2 * (t % 2), k * P:(k + 1) * P],
                                          amod[:, k, 0:1], modt[:, k, 0:1], ALU.mult, ALU.add)
                ins.then_inc(hm_dve, 1)
                if t:
                    hm_second(t - 1)
            dve.wait_ge(x_tr, NT)
            def per_step(x):
                return x.unsqueeze(3).to_broadcast([P, x.shape[1], NS, TS])

            samples = hm[:, :, TP:].rearrange("p k (s t) -> p k s t", s=NS)
            for b in range(2):
                ks = slice(b * GC, (b + 1) * GC)
                src = ps[:, 4 + b, :].rearrange("p (k c) -> p k c", k=GC)[:, :, 0:TSAMP]
                ch.do(v.tensor_tensor(samples[:, ks], src.rearrange("p k (s t) -> p k s t", s=NS),
                                      per_step(amod[:, ks, 1:]), ALU.mult))
            ch.wait()
            v.tensor_tensor(samples, samples, per_step(modt[:, 0:KC, 1:]), ALU.add).then_inc(hm_dve, 1)
            hm_second(NT - 2)
            hm_second(NT - 1)
            for b in range(4):
                dve.wait_ge(sconf_tr, b + 1)
                for k in range(2):
                    ins = v.tensor_copy(glu_s[:, 2 * b + k, :, 0:W30],
                                        ps[:, 4 + b, k * 240:(k + 1) * 240].rearrange("p (s j) -> p s j", s=NS))
                ins.then_inc(sconf_ok, 1)

            def conformer(k):
                dve.wait_ge(conv_ok, k + 1)
                acc = (dc[:, k, 0:TP], odd[k])
                if k == 0:
                    ch.do(v.tensor_scalar(acc[0], glu[:, k, 0:TP], rt[:, k, R_CW:R_CW + 1], rt[:, k, R_CB:R_CB + 1],
                                          ALU.mult, ALU.add))
                if k in (0, KC - 1):
                    ch.do(v.tensor_scalar(acc[1], glu[:, k, 1:1 + TP], rt[:, k, R_CW + 1:R_CW + 2], None, ALU.mult))
                if k:
                    dve.wait_ge(tap_ok, k)
                for j in range(2, 31):
                    ch.wait_but_one()
                    ch.do(v.scalar_tensor_tensor(acc[j % 2], glu[:, k, j:j + TP], rt[:, k, R_CW + j:R_CW + j + 1],
                                                 acc[j % 2], ALU.mult, ALU.add))
                ch.wait()
                ch.do(v.tensor_tensor(acc[0], acc[0], acc[1], ALU.add))
                dve.wait_ge(prod_ok, k + 1)
                out = dc[:, k, TP:].rearrange("p (s t) -> p t s", s=NS)
                v.tensor_reduce(out, prod, AX, ALU.add).then_inc(prod_used, 1)
                dve.wait_ge(prod_used, k + 1)
                v.tensor_scalar(dc[:, k, TP:], dc[:, k, TP:], rt[:, k, R_CB:R_CB + 1], None, ALU.add).then_inc(dc_ok, 1)

            def lru_conv(k):
                m = k % GC
                n = place[("in", G_U + k // GC, k % GC)]
                dve.wait_ge(pair_act, sum(by_act[:n + 1]))
                dve.wait_ge(us_ok, KC + 1)
                ch.do(v.tensor_copy(u_s[:, k, :, W3:], seqs(u[:, k, W3 + TP:])))
                acc, acs = xc[:, m, 0:TP], seqs(xc[:, m, TP:])
                ch.link(v.tensor_scalar(acc, u[:, k, 0:TP], rt[:, k, R_LW:R_LW + 1], rt[:, k, R_LB:R_LB + 1],
                                        ALU.mult, ALU.add))
                ch.link(v.tensor_scalar(acs, u_s[:, k, :, 0:TS], rt[:, k, R_LW:R_LW + 1], rt[:, k, R_LB:R_LB + 1],
                                        ALU.mult, ALU.add))
                for j in range(1, 4):
                    w = rt[:, k, R_LW + j:R_LW + j + 1]
                    ch.do(v.scalar_tensor_tensor(acc, u[:, k, j:j + TP], w, acc, ALU.mult, ALU.add))
                    ins = v.scalar_tensor_tensor(acs, u_s[:, k, :, j:j + TS], w, acs, ALU.mult, ALU.add)
                    if j < 3:
                        ch.link(ins)
                ins.then_inc(xc_ok, 1)

            def lru_1(g):
                last = place[("i", g, GC - 1)]
                dve.wait_ge(pair_act, sum(by_act[:last + 1]))
                ch.do(v.tensor_tensor(ii, ii, xc, ALU.mult))
                dve.wait_ge(t_ok, g + 1)
                ch.link(v.tensor_scalar(rec, tt, 1.0, None, ALU.add))
                v.reciprocal(rec, rec).then_inc(t_copied, 1)
                dve.wait_ge(t_copied, g + 1)

            def lru_2(g):
                ch.link(v.tensor_copy(hst[:, 0, 0:GC], ii[:, :, 0]))
                dve.wait_ge(sqrt_ok, g + 1)
                ch.link(v.scalar_tensor_tensor(tt, tt, 2.0, rec, ALU.mult, ALU.mult))
                ch.link(v.tensor_tensor(ii, ii, tt, ALU.mult))

            def lru_3(g):
                ch.do(v.tensor_scalar(rec, rec, 2.0, -1.0, ALU.mult, ALU.add))
                ch.link(v.tensor_copy(ii[:, :, 0], hst[:, 0, 0:GC]))
                for m in range(GC):
                    ch.do(v.tensor_tensor_scan(xc[:, m, 0:TP], rec[:, m, 0:TP], ii[:, m, 0:TP], 0.0, ALU.mult, ALU.add))

            def lru_4(g):
                def step(x, s):
                    return x[:, :, TP:].rearrange("p m (s t) -> p m s t", s=NS)[:, :, :, s]

                prev = rt[:, g * GC:(g + 1) * GC, R_H0:R_H0 + NS]
                for s in range(TS):
                    ch.link(v.tensor_tensor(step(xc, s), step(rec, s), prev, ALU.mult))
                    ch.link(v.tensor_tensor(step(xc, s), step(xc, s), step(ii, s), ALU.add))
                    prev = step(xc, s)
                ch.do(v.tensor_copy(hlast[:, g * GC:(g + 1) * GC, :], xc[:, :, TP - 1:]))
                gate = place[("in", G_GATE + g, GC - 1)]
                dve.wait_ge(pair_act, sum(by_act[:gate + 1]))
                zz = z[:, g * GC:(g + 1) * GC, :]
                v.tensor_tensor(zz, zz, xc, ALU.mult).then_inc(z_ok, 1)

            def last_rows(i, n):
                dve.wait_ge(last_tr, i + 1)
                dst = (last_glu, last_u, last_h)[i]
                if i == 2:
                    dve.wait_ge(z_ok, 2)
                for h in range(2):
                    ins = v.tensor_copy(dst[0:n, h * 512:(h + 1) * 512], ps[0:n, 4 + h, :])
                ins.then_inc(last_sb, 1)

            dve.wait_ge(conv_new, 1)
            for k in range(KC):
                conformer(k)
            dve.wait_ge(ada_sum, 12)
            for k in range(GC):
                lru_conv(k)
            n = place[("mean", 0, 0)]
            dve.wait_ge(pair_act, sum(by_act[:n + 1]))
            v.tensor_tensor(dc, dc, ln_mean.unsqueeze(1).to_broadcast([P, KC, T]), ALU.subtract).then_inc(cent_ok, 1)
            last_rows(0, 62)
            n = place[("var", 0, 0)]
            dve.wait_ge(pair_act, sum(by_act[:n + 1]))
            ch.link(v.reciprocal(ln_rstd, ln_rstd))
            v.tensor_tensor(dc, dc, ln_rstd.unsqueeze(1).to_broadcast([P, KC, T]), ALU.mult).then_inc(ln_ok, 1)

            def gated(w, h, m):
                n = place[(w, h, m)]
                k = h * GC + m
                dve.wait_ge(pairs, n + 1)
                act_n = place[("in", (G_BC if w == "co" else G_BL) + h, m)]
                dve.wait_ge(pair_act, sum(by_act[:act_n + 1]))
                if w == "co":
                    if k == 0:
                        dve.wait_ge(last_tr, 2)
                    v.tensor_tensor(two(merged[:, k, :]), pair(n), two(bg[m]), ALU.mult).then_inc(pair_dve, 1)
                else:
                    v.tensor_tensor(two(bg[m]), pair(n), two(bg[m]), ALU.mult).then_inc(pair_dve, 1)
                    drained(dve, n)
                    v.tensor_tensor(merged[:, k, :], merged[:, k, :], bg[m], ALU.add).then_inc(merged_ok, 1)

            lru_1(0)
            gated("co", 0, 0)
            lru_2(0)
            gated("co", 0, 1)
            lru_3(0)
            gated("co", 0, 2)
            lru_4(0)
            gated("co", 0, 3)
            dve.wait_ge(z_ok, 1)
            for k in range(GC, KC):
                lru_conv(k)
            last_rows(1, 35)
            lru_1(1)
            gated("co", 1, 0)
            lru_2(1)
            gated("co", 1, 1)
            lru_3(1)
            gated("co", 1, 2)
            lru_4(1)
            gated("co", 1, 3)
            for h in range(2):
                dve.wait_ge(z_hi_ok, h + 1)
                hs = slice(h * GC, (h + 1) * GC)
                v.tensor_tensor(z_lo[:, hs], z[:, hs], z_hi[:, hs].bitcast(F32), ALU.subtract).then_inc(z_lo_ok, 1)
            for h in range(2):
                for m in range(GC):
                    gated("lo", h, m)
                if h == 0:
                    last_rows(2, 33)

            dve.wait_ge(x1_in, 16 * NT)
            dve.wait_ge(bc_in, 16 * 6)
            dve.wait_ge(hrow_out, 32)

            def residual(t):
                n = TILES[t]
                for h in range(2):
                    j = 2 * t + h
                    dve.wait_ge(out_ps, j + 1)
                    tmp = yb[0:n, 0, h * 512:(h + 1) * 512]
                    v.tensor_tensor(tmp, ps[0:n, j % 4, :], gt1_bc[0:n, t // 4, h * 512:(h + 1) * 512], ALU.mult)\
                     .then_inc(x1_half, 1)
                    dve.wait_ge(x1_half, j + 1)
                    xh = x1[0:n, t, h * 512:(h + 1) * 512]
                    ins = v.tensor_tensor(xh, xh, tmp, ALU.add)
                    if h == 0:
                        ch.link(ins)
                ins.then_inc(x1_ok, 1)
                dve.wait_ge(x1_ok, t + 1)

            def hf_norm(t):
                n = TILES[t]
                dve.wait_ge(ssq_ok, NT + t + 1)
                v.tensor_scalar(ssq[0:n, t:t + 1], ssq[0:n, t:t + 1], 1.0 / D, RMS_EPS, ALU.mult, ALU.add)\
                 .then_inc(rms_ask, 1)
                dve.wait_ge(rms_sqrt, t + 2)
                ch.link(newton(n, t, t + 1))
                if t >= 2:
                    dve.wait_ge(hf_store[t % 2], 16 * (t // 2))
                    dve.wait_ge(hft_tr, t - 1)
                v.scalar_tensor_tensor(hf[0:n, t % 2, :], x1[0:n, t, :], rstd[0:n, t:t + 1], g2_bc[0:n, t // 4, :],
                                       ALU.mult, ALU.mult).then_inc(hf_dve, 1)
                if t == NT - 1:
                    dve.wait_ge(hf_dve, NT)
                    dve.wait_ge(hf_sum, NT - 1)
                    v.tensor_tensor(hf[0:n, t % 2, :], hf[0:n, t % 2, :], sh2_bc[0:n, t // 4, :], ALU.add)\
                     .then_inc(hf_sum, 1)

            def hf_turn(t):
                n = TILES[t]
                dve.wait_ge(hft_tr, t + 1)
                if t >= 2:
                    dve.wait_ge(lg_ps, t - 1)
                v.tensor_copy(hft[:, t % 2, 0:4, 0:n],
                              ps[:, 4, :].rearrange("p (k c) -> p k c", k=4)[:, :, 0:n]).then_inc(hft_dve, 1)

            for t in range(NT):
                residual(t)
                if t == 0:
                    dve.wait_ge(bc2_in, 16 * 4)
                    for j in range(2):
                        n = (P, TSAMP)[j]
                        ch.link(v.scalar_tensor_tensor(g2_bc[0:n, j, :], g2_bc[0:n, j, :], 1.0, gffn_bc[0:n, :],
                                                       ALU.add, ALU.mult))
                else:
                    hf_turn(t - 1)
                hf_norm(t)
            hf_turn(NT - 1)
            dve.wait_ge(hf_dve, NT)
            ch.link(v.memset(lg, 0.0))
            dve.wait_ge(lg_ps, NT)
            ch.do(v.tensor_tensor(lg[:, 0:NT - 1, :], ps[:, 6, 0:(NT - 1) * NE].rearrange("p (t e) -> p t e", e=NE),
                                  br[:, :].unsqueeze(1).to_broadcast([P, NT - 1, NE]), ALU.add))
            ch.do(v.tensor_tensor(lg[0:TSAMP, NT - 1, :], ps[0:TSAMP, 6, (NT - 1) * NE:NT * NE], br[0:TSAMP, :], ALU.add))
            ch.wait()

            def c16(x):
                return x.unsqueeze(2).to_broadcast([P, NT, NE])

            def row16(x):
                return x[:, :].unsqueeze(1).to_broadcast([P, NT, NE])

            r = [rs[:, j, :] for j in range(12)]
            ch.link(v.tensor_reduce(r[0], lg, AX, ALU.max))
            v.tensor_tensor(lg, lg, c16(r[0]), ALU.subtract).then_inc(exp_ask, 1)
            dve.wait_ge(exp_ok, 1)
            ch.link(v.tensor_reduce(r[0], lg, AX, ALU.add))
            ch.link(v.reciprocal(r[0], r[0]))
            ch.link(v.tensor_tensor(pr, lg, c16(r[0]), ALU.mult))
            quad = pr.rearrange("p t (g e) -> p t g e", e=EG)
            h1, l1, h2, l2, gs = (gsb[:, j] for j in range(5))
            ch.do(v.tensor_tensor(h1, quad[:, :, :, 0], quad[:, :, :, 1], ALU.max))
            ch.do(v.tensor_tensor(l1, quad[:, :, :, 0], quad[:, :, :, 1], ALU.min))
            ch.do(v.tensor_tensor(h2, quad[:, :, :, 2], quad[:, :, :, 3], ALU.max))
            ch.link(v.tensor_tensor(l2, quad[:, :, :, 2], quad[:, :, :, 3], ALU.min))
            ch.do(v.tensor_tensor(gs, h1, h2, ALU.max))
            ch.do(v.tensor_tensor(l1, l1, l2, ALU.max))
            ch.link(v.tensor_tensor(h1, h1, h2, ALU.min))
            ch.link(v.tensor_tensor(l1, l1, h1, ALU.max))
            ch.link(v.tensor_tensor(gs, gs, l1, ALU.add))
            ch.link(v.tensor_reduce(r[1], gs, AX, ALU.max))
            ch.link(v.tensor_tensor(h1, gs, r[1].unsqueeze(2).to_broadcast([P, NT, NG]), ALU.is_lt))
            ch.link(v.scalar_tensor_tensor(h1, h1, 100.0, iota_g[:, :].unsqueeze(1).to_broadcast([P, NT, NG]),
                                           ALU.mult, ALU.add))
            ch.link(v.tensor_reduce(r[2], h1, AX, ALU.min))
            ch.link(v.tensor_tensor(m16, row16(grp_e), c16(r[2]), ALU.is_equal))
            ch.link(v.tensor_tensor(r6, pr, m16, ALU.mult))
            ch.link(v.scalar_tensor_tensor(pr, m16, 1.0, r6, ALU.subtract, ALU.add))
            for best, idx, oh in ((r[3], r[4], oh1), (r[5], r[6], oh2)):
                ch.link(v.tensor_reduce(best, pr, AX, ALU.max))
                ch.link(v.tensor_tensor(r6, pr, c16(best), ALU.is_lt))
                ch.link(v.scalar_tensor_tensor(r6, r6, 100.0, row16(iota_e), ALU.mult, ALU.add))
                ch.link(v.tensor_reduce(idx, r6, AX, ALU.min))
                ch.link(v.tensor_tensor(oh, row16(iota_e), c16(idx), ALU.is_equal))
                ch.link(v.scalar_tensor_tensor(pr, oh, -10.0, pr, ALU.mult, ALU.add))
            ch.link(v.tensor_tensor(selb[:, :, :], oh1, oh2, ALU.add))
            ch.link(v.tensor_tensor(selb[:, :, :], selb[:, :, :], c16(valid[:, :]), ALU.mult))
            v.tensor_copy(sel_b, selb[:, :, :]).then_inc(sel_ok, 1)
            ch.link(v.tensor_tensor(r[7], r[3], r[5], ALU.add))
            ch.link(v.reciprocal(r[7], r[7]))
            ch.do(v.tensor_tensor(w12[:, 0, :], r[3], r[7], ALU.mult))
            ch.do(v.tensor_tensor(w12[:, 1, :], r[5], r[7], ALU.mult))
            dve.wait_ge(rank_ps, 1)
            ch.do(v.tensor_copy(cnt[:, :], ps[:, 7, NT * NE:(NT + 1) * NE]))
            ch.link(v.tensor_copy(rank, ps[:, 7, 0:NT * NE].rearrange("p (t e) -> p t e", t=NT)))
            ch.link(v.tensor_tensor(key, rank, selb[:, :, :], ALU.mult))
            ch.link(v.tensor_scalar(r7, selb[:, :, :], 10000.0, -10000.0, ALU.mult, ALU.add))
            ch.link(v.tensor_tensor(key, key, r7, ALU.add))
            def row_masks(e, s):
                for t in range(NT):
                    ins = v.tensor_scalar(mb[:, s, t, :], slot_row[:, :], key[:, t, bass.ds(e, 1)], None, ALU.is_equal)
                ins.then_inc(mb_ok, 1)

            def row_index(e, s):
                dve.wait_ge(idx_ps, e + 1)
                v.tensor_copy(idx_f[:, s, :], ps[:, 7, 256 + 2 * s:258 + 2 * s]).then_inc(idx_cp, 1)
                dve.wait_ge(idx_cp, e + 1)
                v.scalar_tensor_tensor(idx_i[:, bass.ds(e, 1)], idx_f[:, s, 1:2], float(P), idx_f[:, s, 0:1],
                                       ALU.mult, ALU.add).then_inc(idx_ok, 1)

            row_masks(0, 0)
            for e in range(AHEAD):
                row_masks(e + 1, 1 - e % 2)
                row_index(e, e % 2)

            def xgt_half(e):
                dve.wait_ge(xgt_ps, e + 1)
                v.tensor_copy(xgt[:, 0:4, :], ps[:, 2, :].rearrange("p (k c) -> p k c", k=4)).then_inc(xgt_dve, 1)

            def hidden(e):
                dve.wait_ge(up_ps, e + 1)
                dve.wait_ge(silu_ok, e + 1)
                v.tensor_tensor(act_g, act_g, ps[:, 1, :], ALU.mult).then_inc(h_ok, 1)

            def y_half(e, s, stored=None):
                dve.wait_ge(y_ps, e + 1)
                if stored is not None:
                    dve.wait_ge(y_store[s], stored)
                v.tensor_copy(yb[:, s, 0:DE], ps[:, 5, :]).then_inc(y_dve, 1)

            def step(e, s, index_too=True, masks_too=True, y_before=True, stored=None, turn_next=True):
                hidden(e)
                if index_too:
                    row_index(e + AHEAD, 1 - s)
                if y_before:
                    y_half(e - 1, 1 - s, stored)
                if turn_next:
                    xgt_half(e + 1)
                if masks_too:
                    row_masks(e + AHEAD + 1, s)
                dve.wait_ge(ht_ok, e + 1)
                v.tensor_tensor(act_lo[:, :, :], ps[:, 4, :].rearrange("p (k c) -> p k c", k=DE // P),
                                act_hi[:, :, :].bitcast(F32), ALU.subtract).then_inc(ht_lo_ok, 1)
                for q in range(DE // P):
                    dve.wait_ge(wd_hi_ok, e * (DE // P) + q + 1)
                    v.tensor_tensor(wd_lo[:, q, :], wd_raw[q], wd_hi[:, q, :].bitcast(F32), ALU.subtract)\
                     .then_inc(wd_lo_ok, 1)

            xgt_half(0)
            step(0, 0, y_before=False)
            step(1, 1)
            step(2, 0)
            for j in range(MORE):
                ch.do(v.tensor_scalar(ovf[:, :, j], cnt[:, :], float(CAP * (j + 1)), None, ALU.is_gt))
            ch.wait()
            flags = ovf[:, :, :].rearrange("p e j -> p (e j)")
            ch.link(v.memset(ovr[:, 0, :], 1.0))
            ch.link(v.tensor_tensor_scan(ovr[:, 1, :], ovr[:, 0, :], flags, 0.0, ALU.mult, ALU.add))
            ch.link(v.tensor_copy(ovt[:, MAX_OVER:MAX_OVER + 1], ovr[:, 1, NE * MORE - 1:NE * MORE]))
            ch.link(v.tensor_tensor(ovr[:, 0, :], ovr[:, 1, :], flags, ALU.mult))
            ch.link(v.tensor_scalar(ovr[:, 0, :], ovr[:, 0, :], -1.0, None, ALU.add))
            big, small = [P, MAX_OVER, NE * MORE], [P, MAX_OVER, NE]
            ch.link(v.tensor_tensor(ovm[0], ovr[:, 0, :].unsqueeze(1).to_broadcast(big),
                                    ovk[:, :].unsqueeze(2).to_broadcast(big), ALU.is_equal))
            ch.link(v.tensor_tensor(ovm[1], ovm[0], ovi[:, :].unsqueeze(1).to_broadcast(big), ALU.mult))
            code, first, exp_ = (ovt_f[:, j, :] for j in range(3))
            ch.link(v.tensor_reduce(code, ovm[1], AX, ALU.add))
            ch.link(v.tensor_tensor(ovm[1][:, :, 0:NE], code.unsqueeze(2).to_broadcast(small),
                                    ov4[:, :].unsqueeze(1).to_broadcast(small), ALU.is_ge))
            ch.link(v.tensor_reduce(exp_, ovm[1][:, :, 0:NE], AX, ALU.add))
            ch.link(v.tensor_scalar(exp_, exp_, -1.0, None, ALU.add))
            ch.link(v.scalar_tensor_tensor(first, exp_, -float(MORE), code, ALU.mult, ALU.add))
            ch.link(v.tensor_scalar(first, first, float(CAP), float(CAP), ALU.mult, ALU.add))
            v.tensor_copy(ovt[:, 0:MAX_OVER], exp_).then_inc(ov_ok, 1)
            start, step_ = ovr[:, 1, :].rearrange("p (e j) -> p e j", j=MORE), ovr[:, 2, :].rearrange("p (e j) -> p e j", j=MORE)
            ch.link(v.tensor_scalar(ovr[:, 1, :], ovr[:, 1, :], float(CAP), float(CAP * (NE - 1)), ALU.mult, ALU.add))
            for j in range(MORE):
                ch.do(v.tensor_scalar(start[:, :, j], start[:, :, j], -float(CAP * (j + 1)), None, ALU.add))
            ch.wait()
            ch.do(v.tensor_tensor(step_[:, :, 0], start[:, :, 0], base_e[:, :], ALU.subtract))
            for j in range(1, MORE):
                ch.do(v.tensor_tensor(step_[:, :, j], start[:, :, j], start[:, :, j - 1], ALU.subtract))
            ch.link(v.tensor_tensor(r6, rank, row16(base_e), ALU.add))
            for j in range(MORE):
                ch.link(v.tensor_scalar(r7, rank, float(CAP * (j + 1)), None, ALU.is_ge))
                ch.link(v.tensor_tensor(r7, r7, step_[:, :, j].unsqueeze(1).to_broadcast([P, NT, NE]), ALU.mult))
                ch.link(v.tensor_tensor(r6, r6, r7, ALU.add))
            for j, oh in enumerate((oh1, oh2)):
                ch.link(v.tensor_tensor(r7, oh, r6, ALU.mult))
                ch.link(v.tensor_reduce(r[8], r7, AX, ALU.add))
                v.tensor_copy(slot_i[:, j, :], r[8]).then_inc(slot_ok, 1)
                dve.wait_ge(slot_ok, j + 1)

            with dve.Fori(1, 5) as i:
                step(i * 2 + 1, 1, stored=i * 16)
                step(i * 2 + 2, 0, stored=i * 16)
            step(11, 1, stored=16 * 5)
            step(12, 0, masks_too=False, stored=16 * 5)
            step(13, 1, index_too=False, masks_too=False, stored=16 * 6)
            step(14, 0, index_too=False, masks_too=False, stored=16 * 6)
            step(15, 1, index_too=False, masks_too=False, stored=16 * 7, turn_next=False)
            y_half(NE - 1, 1, 16 * (NE // 2 - 1))

            dve.wait_ge(ov_ok, 1)
            n_over = dve.value_load(ovt[0:1, MAX_OVER:MAX_OVER + 1], min_val=0, max_val=MAX_OVER)
            with dve.If(n_over > 0):
                with dve.Fori(0, n_over) as k:
                    e = dve.value_load(ovt[0:1, bass.ds(k, 1)], min_val=0, max_val=NE - 1)
                    v.tensor_scalar(ovkey[:, :], key[:, :, bass.ds(e, 1)].rearrange("p t o -> p (t o)"),
                                    ovt_f[:, 1, bass.ds(k, 1)], None, ALU.subtract).then_inc(ov_key, 1)
                    dve.wait_ge(ov_key, k + 1)
                    for t in range(NT):
                        ins = v.tensor_scalar(mb[:, 0, t, :], slot_row[:, :], ovkey[:, t:t + 1], None, ALU.is_equal)
                    ins.then_inc(mb_ok, 1)
                    dve.wait_ge(ov_pe, k * 5 + 1)
                    v.tensor_copy(idx_f[:, 0, :], ps[:, 7, 0:2]).then_inc(idx_cp, 1)
                    dve.wait_ge(idx_cp, k + NE + 1)
                    v.scalar_tensor_tensor(idx_vf[:, :], idx_f[:, 0, 1:2], float(P), idx_f[:, 0, 0:1],
                                           ALU.mult, ALU.add).then_inc(ov_idx, 1)
                    dve.wait_ge(ov_pe, k * 5 + 2)
                    v.tensor_copy(xgt[:, :, :], ps[:, 2:4, :].rearrange("p b (k c) -> p (b k) c", k=4)).then_inc(ov_dve, 1)
                    dve.wait_ge(ov_pe, k * 5 + 3)
                    dve.wait_ge(ov_act, k + 1)
                    v.tensor_tensor(act_g, act_g, ps[:, 1, :], ALU.mult).then_inc(ov_dve, 1)
                    dve.wait_ge(ov_pe, k * 5 + 4)
                    v.tensor_copy(act_t, ps[:, 4, :].rearrange("p (k c) -> p k c", k=DE // P)).then_inc(ov_dve, 1)
                    dve.wait_ge(ov_pe, k * 5 + 5)
                    v.tensor_copy(yb[:, 0, :].rearrange("p (h n) -> p h n", h=2), ps[:, 5:7, :]).then_inc(ov_dve, 1)
            with dve.Else():
                dve.nop()

            for t in range(NT + 1):
                if t < NT:
                    n = TILES[t]
                    y1, y2_, xr = ya[0:n, t, :], yc[0:n, t, :], x1[0:n, t, :]
                    dve.wait_ge(y_in[t], 32)
                    dve.wait_ge(y_scaled, t + 1)
                    ch.do(v.scalar_tensor_tensor(y1, y2_, w12[0:n, 1, t:t + 1], y1, ALU.mult, ALU.add))
                if t:
                    n_ = TILES[t - 1]
                    r_, q_, w_ = (x[0:n_, t - 1:t] for x in (rstd, nt1, ssq))
                    dve.wait_ge(fin_act, t)
                    v.tensor_scalar(w_, w_, 1.0 / D, RMS_EPS, ALU.mult, ALU.add).then_inc(rms_ask, 1)
                if t < NT:
                    ch.wait()
                    ch.do(v.tensor_tensor(y1, y1, gt2_bc[0:n, t // 4, :], ALU.mult))
                if t:
                    dve.wait_ge(rms_sqrt, NT + t + 1)
                    ch.do(v.reciprocal(r_, q_))
                ch.wait()
                if t < NT:
                    v.tensor_tensor(xr, xr, y1, ALU.add).then_inc(fin_dve, 1)
                if t:
                    ch.link(v.tensor_tensor(q_, r_, r_, ALU.mult))
                    ch.link(v.scalar_tensor_tensor(q_, q_, -0.5, w_, ALU.mult, ALU.mult))
                    ch.link(v.scalar_tensor_tensor(r_, q_, 1.5, r_, ALU.add, ALU.mult))
                    if t >= 3:
                        dve.wait_ge(y_out[(t - 1) % 2], 16 * ((t - 1) // 2))
                    v.scalar_tensor_tensor(yo[0:n_, (t - 1) % 2, :], x1[0:n_, t - 1, :], rstd[0:n_, t - 1:t],
                                           gfin_bc[0:n_, :], ALU.mult, ALU.mult).then_inc(fin_ok, 1)


_INS = ['x_prompt', 'x_sample', 'state_lru_h', 'state_lru_conv', 'state_conf_conv', 'c_prompt', 'c_sample',
        'w_ada', 'b_ada', 'g_mix', 'g_ffn', 'w_in', 'b_in', 'lru_conv_w', 'lru_conv_b', 'lru_wa', 'lru_ba',
        'lru_wx', 'lru_bx', 'lru_lambda', 'w_lru_o', 'conf_conv_w', 'conf_conv_b', 'conf_ln_g', 'conf_ln_b',
        'w_conf_o', 'w_out', 'w_router', 'b_router', 'w_gate', 'w_up', 'w_down', 'g_final']
_OUTS = [('yp', (1, 512, 1024)), ('ys', (8, 4, 1024)), ('hp', (1, 1, 1024)), ('lcp', (1, 1, 3, 1024)),
         ('ccp', (1, 1, 30, 1024)), ('hs', (1, 8, 1024)), ('lcs', (1, 8, 3, 1024)), ('ccs', (1, 8, 30, 1024))]


def kernel(**inputs):
    import numpy as _np
    import concourse.bacc as _bacc
    from concourse.bass_utils import run_bass_kernel_spmd as _run

    nc = _bacc.Bacc("TRN2", target_bir_lowering=False, num_devices=1)
    arrays, aps = {}, {}
    for name in _INS:
        x = _np.ascontiguousarray(inputs[name])
        arrays[f"in_{name}"] = x
        aps[name] = nc.dram_tensor(f"in_{name}", x.shape, mybir.dt.from_np(x.dtype), kind="ExternalInput").ap()
    for name, shape in _OUTS:
        aps[name] = nc.dram_tensor(f"out_{name}", shape, F32, kind="ExternalOutput").ap()
    build(nc, aps)
    r = _run(nc, [arrays], core_ids=[0])
    return tuple(r.results[0][f"out_{name}"] for name, _ in _OUTS)
```
